# Optimizing a Trainium2 kernel written in Bass

```python
import jax, jax.numpy as jnp
from jax import lax
import numpy as np

D_MODEL = 1024
BATCH = 1
SEQ = 256
DEPTH = 2

HEAD_DIM = 64
ROPE_DIM = HEAD_DIM // 4
ROPE_THETA = 500000.0
EPS = 1e-6
NEG = -1e30
BIG = 1e9

GLA_HEADS = 4
GLA_DK = 64
GLA_DV = 128
GLA_GATE_RANK = 16
GLA_GATE_NORM = 16.0
GLA_CHUNK = 64

SWA_Q_HEADS = 8
SWA_KV_HEADS = 2
SWA_WINDOW = 128
BAND_BLOCK = 128

RET_HEADS = 4
RET_DK = 64
RET_DV = 128
RET_CHUNK = 64
RET_THETA = 10000.0

NSA_Q_HEADS = 8
NSA_KV_HEADS = 2
CMP_BLOCK = 32
CMP_STRIDE = 16
CMP_HIDDEN = 256
SEL_BLOCK = 64
SEL_TOP_N = 16
SEL_QUERY_BLOCK = 64
NSA_WINDOW = 512

D_FF = 2816
N_EXPERTS = 8
TOP_K = 2
D_FF_EXPERT = 3584

L0_SPLITS = (GLA_HEADS * GLA_DK, GLA_HEADS * GLA_DK, GLA_HEADS * GLA_DV, GLA_GATE_RANK, GLA_HEADS * GLA_DV,
             SWA_Q_HEADS * HEAD_DIM, SWA_KV_HEADS * HEAD_DIM, SWA_KV_HEADS * HEAD_DIM)
L0_IN = sum(L0_SPLITS)
L0_MIX = GLA_HEADS * GLA_DV + SWA_Q_HEADS * HEAD_DIM
L1_SPLITS = (RET_HEADS * RET_DK, RET_HEADS * RET_DK, RET_HEADS * RET_DV, RET_HEADS * RET_DV,
             NSA_Q_HEADS * HEAD_DIM) + (NSA_KV_HEADS * HEAD_DIM,) * 6 + (NSA_Q_HEADS * 3,)
L1_IN = sum(L1_SPLITS)
L1_MIX = RET_HEADS * RET_DV + NSA_Q_HEADS * HEAD_DIM
N_EVEN = (DEPTH + 1) // 2
N_ODD = DEPTH // 2

kernel_name = 'hybrid_gla_swa_retention_nsa_moe'

def rmsnorm(x, g):
    x32 = x.astype(jnp.float32)
    y = x32 * lax.rsqrt(jnp.mean(x32 * x32, axis=-1, keepdims=True) + EPS)
    return (y * g.astype(jnp.float32)).astype(x.dtype)

def head_layernorm(x, g):
    mu = jnp.mean(x, axis=-1, keepdims=True)
    xc = x - mu
    y = xc * lax.rsqrt(jnp.mean(xc * xc, axis=-1, keepdims=True) + EPS)
    return y * g.astype(jnp.float32).reshape(x.shape[2], x.shape[3])

def rope(x, pos, rot_dim, theta):
    half = rot_dim // 2
    inv = jnp.float32(theta) ** (-jnp.arange(half, dtype=jnp.float32) * 2.0 / rot_dim)
    ang = pos.astype(jnp.float32)[..., None] * inv
    cos = jnp.cos(ang)[:, :, None, :]
    sin = jnp.sin(ang)[:, :, None, :]
    x1 = x[..., :half]
    x2 = x[..., half:rot_dim]
    return jnp.concatenate([x1 * cos - x2 * sin, x2 * cos + x1 * sin, x[..., rot_dim:]], axis=-1)

def _split(h, sizes):
    return jnp.split(h, np.cumsum(sizes)[:-1].tolist(), axis=-1)

def _to_chunks(x, c):
    b, t, h, d = x.shape
    return x.reshape(b, t // c, c, h, d).transpose(1, 0, 3, 2, 4)

def _from_chunks(o):
    n, b, h, c, d = o.shape
    return o.transpose(1, 0, 3, 2, 4).reshape(b, n * c, h, d)

def swiglu(x, w_gate, w_up, w_down):
    return (jax.nn.silu(x @ w_gate) * (x @ w_up)) @ w_down

def gla_chunked(q, k, v, log_alpha):
    B, T, H, dk = q.shape
    dv = v.shape[-1]
    C = GLA_CHUNK
    qc, kc, vc, gc = [_to_chunks(t, C) for t in (q, k, v, log_alpha)]
    b = jnp.cumsum(gc, axis=3)
    b_last = b[:, :, :, -1:, :]
    q_in = qc * jnp.exp(b)
    k_in = kc * jnp.exp(-b)
    k_state = kc * jnp.exp(b_last - b)
    causal = jnp.tril(jnp.ones((C, C), dtype=bool))
    scores = jnp.where(causal, jnp.einsum('nbhtd,nbhsd->nbhts', q_in, k_in), 0.0)
    o_intra = jnp.einsum('nbhts,nbhsv->nbhtv', scores, vc)
    chunk_decay = jnp.exp(b_last[:, :, :, 0, :])

    def step(state, inp):
        qi, ks, vv, dec = inp
        out = jnp.einsum('bhtd,bhdv->bhtv', qi, state)
        state = dec[..., None] * state + jnp.einsum('bhsd,bhsv->bhdv', ks, vv)
        return state, out

    state0 = jnp.zeros((B, H, dk, dv), jnp.float32)
    _, o_inter = lax.scan(step, state0, (q_in, k_state, vc, chunk_decay))
    return _from_chunks(o_intra + o_inter)

def retention_chunked(q, k, v):
    B, T, H, dk = q.shape
    dv = v.shape[-1]
    C = RET_CHUNK
    log_gamma = jnp.log(1.0 - jnp.exp2(-5.0 - jnp.arange(H, dtype=jnp.float32)))
    qc, kc, vc = _to_chunks(q, C), _to_chunks(k, C), _to_chunks(v, C)
    i = jnp.arange(C, dtype=jnp.float32)
    diff = i[:, None] - i[None, :]
    decay_in = jnp.where(diff >= 0, jnp.exp(log_gamma[:, None, None] * jnp.maximum(diff, 0.0)), 0.0)
    scores = jnp.einsum('nbhtd,nbhsd->nbhts', qc, kc) * decay_in
    o_intra = jnp.einsum('nbhts,nbhsv->nbhtv', scores, vc)
    q_dec = qc * jnp.exp(log_gamma[:, None] * (i + 1.0))[:, :, None]
    k_dec = kc * jnp.exp(log_gamma[:, None] * (C - 1.0 - i))[:, :, None]
    chunk_decay = jnp.exp(log_gamma * C)[:, None, None]

    def step(state, inp):
        qd, kd, vv = inp
        out = jnp.einsum('bhtd,bhdv->bhtv', qd, state)
        state = chunk_decay * state + jnp.einsum('bhsd,bhsv->bhdv', kd, vv)
        return state, out

    state0 = jnp.zeros((B, H, dk, dv), jnp.float32)
    _, o_inter = lax.scan(step, state0, (q_dec, k_dec, vc))
    return _from_chunks(o_intra + o_inter)

def banded_window_attention(q, k, v, window, sinks=None):
    B, T, Hq, Dh = q.shape
    Hkv = k.shape[2]
    G = Hq // Hkv
    Bq = BAND_BLOCK
    NB = T // Bq
    P = -(-window // Bq)
    L = (P + 1) * Bq
    pad = ((0, 0), (P * Bq, 0), (0, 0), (0, 0))
    kp = jnp.pad(k, pad)
    vp = jnp.pad(v, pad)
    band = jnp.arange(NB)[:, None] * Bq + jnp.arange(L)[None, :]
    kb = jnp.moveaxis(kp[:, band], 1, 0)
    vb = jnp.moveaxis(vp[:, band], 1, 0)
    qb = jnp.moveaxis(q.reshape(B, NB, Bq, Hkv, G, Dh), 1, 0)
    r = jnp.arange(Bq)[:, None]
    c = jnp.arange(L)[None, :]
    rel = r + P * Bq - c
    scale = Dh ** -0.5

    def block(args):
        qi, ki, vi, bi = args
        s = jnp.einsum('bqhgd,bkhd->bhgqk', qi, ki) * scale
        key_pos = bi * Bq + c - P * Bq
        mask = (rel >= 0) & (rel < window) & (key_pos >= 0)
        s = jnp.where(mask, s, NEG)
        if sinks is None:
            p = jax.nn.softmax(s, axis=-1)
        else:
            sk = sinks.astype(jnp.float32).reshape(Hkv, G)[None, :, :, None, None]
            m = jnp.maximum(jnp.max(s, axis=-1, keepdims=True), sk)
            e = jnp.exp(s - m)
            p = e / (jnp.sum(e, axis=-1, keepdims=True) + jnp.exp(sk - m))
        return jnp.einsum('bhgqk,bkhd->bqhgd', p, vi)

    o = lax.map(block, (qb, kb, vb, jnp.arange(NB)))
    return jnp.moveaxis(o, 0, 1).reshape(B, T, Hq, Dh)

def compress_tokens(t, pos_emb, w1, b1, w2, b2):
    B, T, H, Dh = t.shape
    nc = (T - CMP_BLOCK) // CMP_STRIDE + 1
    idx = jnp.arange(nc)[:, None] * CMP_STRIDE + jnp.arange(CMP_BLOCK)[None, :]
    blk = t[:, idx] + pos_emb[:, None, :]
    blk = jnp.transpose(blk, (0, 1, 3, 2, 4)).reshape(B, nc, H, CMP_BLOCK * Dh)
    hid = jax.nn.gelu(blk @ w1 + b1)
    return hid @ w2 + b2

def nsa_compressed_branch(q, kc, vc):
    T = q.shape[1]
    nc = kc.shape[1]
    s = jnp.einsum('bthgd,bnhd->bhgtn', q, kc) * HEAD_DIM ** -0.5
    blk_end = jnp.arange(nc)[None, :] * CMP_STRIDE + CMP_BLOCK - 1
    mask = blk_end <= jnp.arange(T)[:, None]
    p = jnp.where(mask, jax.nn.softmax(jnp.where(mask, s, NEG), axis=-1), 0.0)
    o = jnp.einsum('bhgtn,bnhd->bthgd', p, vc)
    return o, p

def _selection_weights():
    n_prev = CMP_BLOCK // CMP_STRIDE - 1
    offs = np.arange(-n_prev, SEL_BLOCK // CMP_STRIDE)
    start = offs * CMP_STRIDE
    shared = np.minimum(start + CMP_BLOCK, SEL_BLOCK) - np.maximum(start, 0)
    return offs, (shared / CMP_STRIDE).astype(np.float32)

def nsa_select_blocks(p_cmp):
    p = jnp.sum(p_cmp, axis=2)
    T = p.shape[2]
    nc = p.shape[3]
    ns = T // SEL_BLOCK
    offs, wts = _selection_weights()
    cidx = (SEL_BLOCK // CMP_STRIDE) * np.arange(ns)[:, None] + offs[None, :]
    valid = (cidx >= 0) & (cidx < nc)
    gathered = p[..., np.clip(cidx, 0, nc - 1)]
    importance = jnp.sum(gathered * np.where(valid, wts[None, :], 0.0).astype(np.float32), axis=-1)
    t_blk = jnp.arange(T)[:, None] // SEL_BLOCK
    j = jnp.arange(ns)[None, :]
    forced = (j == 0) | (j == t_blk) | (j == t_blk - 1)
    allowed = j <= t_blk
    score = jnp.where(forced, BIG, jnp.where(allowed, importance, -BIG))
    _, idx = lax.top_k(score, min(SEL_TOP_N, ns))
    return idx

def nsa_selected_branch(q, k, v, idx):
    B, T, Hkv, G, Dh = q.shape
    ns = T // SEL_BLOCK
    n = idx.shape[-1]
    kb = k.reshape(B, ns, SEL_BLOCK, Hkv, Dh).transpose(0, 3, 1, 2, 4)
    vb = v.reshape(B, ns, SEL_BLOCK, Hkv, Dh).transpose(0, 3, 1, 2, 4)
    Qb = SEL_QUERY_BLOCK
    nq = T // Qb
    qs = jnp.moveaxis(q.reshape(B, nq, Qb, Hkv, G, Dh), 1, 0)
    ids = jnp.moveaxis(idx.reshape(B, Hkv, nq, Qb, n), 2, 0)
    b_i = jnp.arange(B)[:, None, None, None]
    h_i = jnp.arange(Hkv)[None, :, None, None]
    within = jnp.arange(SEL_BLOCK)
    scale = Dh ** -0.5

    def block(args):
        qi, ii, qblk = args
        ks = kb[b_i, h_i, ii]
        vs = vb[b_i, h_i, ii]
        s = jnp.einsum('bqhgd,bhqnkd->bhgqnk', qi, ks) * scale
        tq = qblk * Qb + jnp.arange(Qb)
        key_pos = ii[..., None] * SEL_BLOCK + within
        mask = key_pos <= tq[None, None, :, None, None]
        s = jnp.where(mask[:, :, None], s, NEG).reshape(B, Hkv, G, Qb, n * SEL_BLOCK)
        p = jax.nn.softmax(s, axis=-1).reshape(B, Hkv, G, Qb, n, SEL_BLOCK)
        return jnp.einsum('bhgqnk,bhqnkd->bqhgd', p, vs)

    o = lax.map(block, (qs, ids, jnp.arange(nq)))
    return jnp.moveaxis(o, 0, 1).reshape(B, T, Hkv, G, Dh)

def even_mixer(xn, positions, w_in, gla_gate_up, gla_gate_bias, gla_out_norm,
               swa_q_norm, swa_k_norm, swa_sinks, w_out):
    B, T, _ = xn.shape
    proj = (xn @ w_in).astype(jnp.float32)
    gq, gk, gv, g_low, g_out, sq, sk, sv = _split(proj, L0_SPLITS)
    gq = gq.reshape(B, T, GLA_HEADS, GLA_DK) * GLA_DK ** -0.5
    gk = gk.reshape(B, T, GLA_HEADS, GLA_DK)
    gv = gv.reshape(B, T, GLA_HEADS, GLA_DV)
    log_alpha = jax.nn.log_sigmoid(g_low @ gla_gate_up + gla_gate_bias).reshape(B, T, GLA_HEADS, GLA_DK) / GLA_GATE_NORM
    o_gla = gla_chunked(gq, gk, gv, log_alpha)
    o_gla = rmsnorm(o_gla, gla_out_norm).reshape(B, T, GLA_HEADS * GLA_DV) * jax.nn.silu(g_out)
    sq = rope(rmsnorm(sq.reshape(B, T, SWA_Q_HEADS, HEAD_DIM), swa_q_norm), positions, ROPE_DIM, ROPE_THETA)
    sk = rope(rmsnorm(sk.reshape(B, T, SWA_KV_HEADS, HEAD_DIM), swa_k_norm), positions, ROPE_DIM, ROPE_THETA)
    sv = sv.reshape(B, T, SWA_KV_HEADS, HEAD_DIM)
    o_swa = banded_window_attention(sq, sk, sv, SWA_WINDOW, swa_sinks).reshape(B, T, SWA_Q_HEADS * HEAD_DIM)
    mixed = jnp.concatenate([o_gla, o_swa], axis=-1)
    return mixed.astype(xn.dtype) @ w_out

def odd_mixer(xn, positions, w_in, ret_out_norm, nsa_q_norm, nsa_kc_norm, nsa_ks_norm, nsa_kw_norm,
              cmp_k, cmp_v, w_out):
    B, T, _ = xn.shape
    G = NSA_Q_HEADS // NSA_KV_HEADS
    proj = (xn @ w_in).astype(jnp.float32)
    rq, rk, rv, rg, nq, kc, vc, ksl, vsl, kwn, vwn, ng = _split(proj, L1_SPLITS)
    rq = rope(rq.reshape(B, T, RET_HEADS, RET_DK), positions, RET_DK, RET_THETA)
    rk = rope(rk.reshape(B, T, RET_HEADS, RET_DK), positions, RET_DK, RET_THETA) * RET_DK ** -0.5
    o_ret = retention_chunked(rq, rk, rv.reshape(B, T, RET_HEADS, RET_DV))
    o_ret = head_layernorm(o_ret, ret_out_norm).reshape(B, T, RET_HEADS * RET_DV) * jax.nn.silu(rg)
    q = rope(rmsnorm(nq.reshape(B, T, NSA_Q_HEADS, HEAD_DIM), nsa_q_norm), positions, ROPE_DIM, ROPE_THETA)
    qg = q.reshape(B, T, NSA_KV_HEADS, G, HEAD_DIM)
    kc_blk = compress_tokens(kc.reshape(B, T, NSA_KV_HEADS, HEAD_DIM), *cmp_k)
    vc_blk = compress_tokens(vc.reshape(B, T, NSA_KV_HEADS, HEAD_DIM), *cmp_v)
    n_cmp = kc_blk.shape[1]
    end_pos = positions[:, np.arange(n_cmp) * CMP_STRIDE + CMP_BLOCK - 1]
    kc_blk = rope(rmsnorm(kc_blk, nsa_kc_norm), end_pos, ROPE_DIM, ROPE_THETA)
    o_cmp, p_cmp = nsa_compressed_branch(qg, kc_blk, vc_blk)
    sel_idx = nsa_select_blocks(p_cmp)
    ks = rope(rmsnorm(ksl.reshape(B, T, NSA_KV_HEADS, HEAD_DIM), nsa_ks_norm), positions, ROPE_DIM, ROPE_THETA)
    o_slc = nsa_selected_branch(qg, ks, vsl.reshape(B, T, NSA_KV_HEADS, HEAD_DIM), sel_idx)
    kw = rope(rmsnorm(kwn.reshape(B, T, NSA_KV_HEADS, HEAD_DIM), nsa_kw_norm), positions, ROPE_DIM, ROPE_THETA)
    o_win = banded_window_attention(q, kw, vwn.reshape(B, T, NSA_KV_HEADS, HEAD_DIM), NSA_WINDOW)
    o_win = o_win.reshape(B, T, NSA_KV_HEADS, G, HEAD_DIM)
    gate = jax.nn.sigmoid(ng).reshape(B, T, NSA_KV_HEADS, G, 3)
    o_nsa = gate[..., 0:1] * o_cmp + gate[..., 1:2] * o_slc + gate[..., 2:3] * o_win
    mixed = jnp.concatenate([o_ret, o_nsa.reshape(B, T, NSA_Q_HEADS * HEAD_DIM)], axis=-1)
    return mixed.astype(xn.dtype) @ w_out

def moe_swiglu(x, router_w, router_b, w_gate, w_up, w_down):
    logits = (x @ router_w).astype(jnp.float32) + router_b.astype(jnp.float32)
    top_val, top_idx = lax.top_k(logits, TOP_K)
    top_w = jax.nn.softmax(top_val, axis=-1)
    combine = jnp.sum(jax.nn.one_hot(top_idx, N_EXPERTS, dtype=jnp.float32) * top_w[..., None], axis=-2)
    out = jnp.zeros(x.shape, jnp.float32)
    for e in range(N_EXPERTS):
        out = out + combine[..., e:e + 1] * swiglu(x, w_gate[e], w_up[e], w_down[e])
    return out.astype(x.dtype)

def setup_inputs(seed: int = 0) -> dict:
    key = jax.random.key(seed)
    ks = iter(jax.random.split(key, 64))
    f32 = jnp.float32
    NE, NO = N_EVEN, N_ODD

    def dense(shape, fan_in):
        return jax.random.normal(next(ks), shape, f32) * fan_in ** -0.5

    def gain(shape):
        return 1.0 + 0.05 * jax.random.normal(next(ks), shape, f32)

    def small(shape, s):
        return s * jax.random.normal(next(ks), shape, f32)

    x = jax.random.normal(next(ks), (BATCH, SEQ, D_MODEL), f32)
    start = jax.random.randint(next(ks), (BATCH, 1), 0, 1024, dtype=jnp.int32)
    positions = start + jnp.arange(SEQ, dtype=jnp.int32)[None, :]
    return {
        'x': x,
        'positions': positions,
        'ln_mix_e': gain((NE, D_MODEL)),
        'w_in_e': dense((NE, D_MODEL, L0_IN), D_MODEL),
        'gla_gate_up': dense((NE, GLA_GATE_RANK, GLA_HEADS * GLA_DK), GLA_GATE_RANK),
        'gla_gate_bias': small((NE, GLA_HEADS * GLA_DK), 0.1),
        'gla_out_norm': gain((NE, GLA_DV)),
        'swa_q_norm': gain((NE, HEAD_DIM)),
        'swa_k_norm': gain((NE, HEAD_DIM)),
        'swa_sinks': small((NE, SWA_Q_HEADS), 0.5),
        'w_out_e': dense((NE, L0_MIX, D_MODEL), L0_MIX),
        'ln_ffn_e': gain((NE, D_MODEL)),
        'ffn_w_gate': dense((NE, D_MODEL, D_FF), D_MODEL),
        'ffn_w_up': dense((NE, D_MODEL, D_FF), D_MODEL),
        'ffn_w_down': dense((NE, D_FF, D_MODEL), D_FF),
        'ln_mix_o': gain((NO, D_MODEL)),
        'w_in_o': dense((NO, D_MODEL, L1_IN), D_MODEL),
        'ret_out_norm': gain((NO, RET_HEADS * RET_DV)),
        'nsa_q_norm': gain((NO, HEAD_DIM)),
        'nsa_kc_norm': gain((NO, HEAD_DIM)),
        'nsa_ks_norm': gain((NO, HEAD_DIM)),
        'nsa_kw_norm': gain((NO, HEAD_DIM)),
        'cmp_pos_k': small((NO, CMP_BLOCK, HEAD_DIM), 0.1),
        'cmp_w1_k': dense((NO, CMP_BLOCK * HEAD_DIM, CMP_HIDDEN), CMP_BLOCK * HEAD_DIM),
        'cmp_b1_k': small((NO, CMP_HIDDEN), 0.02),
        'cmp_w2_k': dense((NO, CMP_HIDDEN, HEAD_DIM), CMP_HIDDEN),
        'cmp_b2_k': small((NO, HEAD_DIM), 0.02),
        'cmp_pos_v': small((NO, CMP_BLOCK, HEAD_DIM), 0.1),
        'cmp_w1_v': dense((NO, CMP_BLOCK * HEAD_DIM, CMP_HIDDEN), CMP_BLOCK * HEAD_DIM),
        'cmp_b1_v': small((NO, CMP_HIDDEN), 0.02),
        'cmp_w2_v': dense((NO, CMP_HIDDEN, HEAD_DIM), CMP_HIDDEN),
        'cmp_b2_v': small((NO, HEAD_DIM), 0.02),
        'w_out_o': dense((NO, L1_MIX, D_MODEL), L1_MIX),
        'ln_ffn_o': gain((NO, D_MODEL)),
        'router_w': dense((NO, D_MODEL, N_EXPERTS), D_MODEL),
        'router_b': small((NO, N_EXPERTS), 0.01),
        'exp_w_gate': dense((NO, N_EXPERTS, D_MODEL, D_FF_EXPERT), D_MODEL),
        'exp_w_up': dense((NO, N_EXPERTS, D_MODEL, D_FF_EXPERT), D_MODEL),
        'exp_w_down': dense((NO, N_EXPERTS, D_FF_EXPERT, D_MODEL), D_FF_EXPERT),
    }

def reference(x, positions,
              ln_mix_e, w_in_e, gla_gate_up, gla_gate_bias, gla_out_norm, swa_q_norm, swa_k_norm, swa_sinks,
              w_out_e, ln_ffn_e, ffn_w_gate, ffn_w_up, ffn_w_down,
              ln_mix_o, w_in_o, ret_out_norm, nsa_q_norm, nsa_kc_norm, nsa_ks_norm, nsa_kw_norm,
              cmp_pos_k, cmp_w1_k, cmp_b1_k, cmp_w2_k, cmp_b2_k,
              cmp_pos_v, cmp_w1_v, cmp_b1_v, cmp_w2_v, cmp_b2_v,
              w_out_o, ln_ffn_o, router_w, router_b, exp_w_gate, exp_w_up, exp_w_down):
    h = x
    for layer in range(DEPTH):
        i = layer // 2
        if layer % 2 == 0:
            h = h + even_mixer(rmsnorm(h, ln_mix_e[i]), positions, w_in_e[i], gla_gate_up[i], gla_gate_bias[i],
                               gla_out_norm[i], swa_q_norm[i], swa_k_norm[i], swa_sinks[i], w_out_e[i])
            h = h + swiglu(rmsnorm(h, ln_ffn_e[i]), ffn_w_gate[i], ffn_w_up[i], ffn_w_down[i])
        else:
            cmp_k = (cmp_pos_k[i], cmp_w1_k[i], cmp_b1_k[i], cmp_w2_k[i], cmp_b2_k[i])
            cmp_v = (cmp_pos_v[i], cmp_w1_v[i], cmp_b1_v[i], cmp_w2_v[i], cmp_b2_v[i])
            h = h + odd_mixer(rmsnorm(h, ln_mix_o[i]), positions, w_in_o[i], ret_out_norm[i], nsa_q_norm[i],
                              nsa_kc_norm[i], nsa_ks_norm[i], nsa_kw_norm[i], cmp_k, cmp_v, w_out_o[i])
            h = h + moe_swiglu(rmsnorm(h, ln_ffn_o[i]), router_w[i], router_b[i],
                               exp_w_gate[i], exp_w_up[i], exp_w_down[i])
    return h


_drawn_inputs = setup_inputs


def setup_inputs(seed=0):
    import zlib

    import numpy as np

    out = dict(_drawn_inputs(seed))
    spreads = {}
    factors = {'swa_q_norm': 3.914,
     'swa_k_norm': 3.341,
     'nsa_q_norm': 4.097,
     'nsa_kc_norm': 8.0,
     'nsa_ks_norm': 8.0,
     'nsa_kw_norm': 8.0,
     'cmp_pos_k': 3.723,
     'cmp_b1_k': 8.0,
     'cmp_b2_k': 8.0,
     'cmp_b1_v': 8.0,
     'cmp_b2_v': 8.0,
     'router_b': 3.614}
    for name, (base, spread) in spreads.items():
        noise = np.random.default_rng([zlib.crc32(name.encode()), seed]).standard_normal(out[name].shape)
        drawn = base * np.exp(spread * noise) if base else spread * noise
        out[name] = __import__('jax').numpy.asarray(drawn.astype(out[name].dtype))
    for name, factor in factors.items():
        out[name] = (out[name] * factor).astype(out[name].dtype)
    return out
```

```python
from contextlib import ExitStack

import concourse.bass as bass
from concourse import mybir

F32 = mybir.dt.float32
BF16 = mybir.dt.bfloat16
I32 = mybir.dt.int32
U32 = mybir.dt.uint32
ALU = mybir.AluOpType
ACT = mybir.ActivationFunctionType
AX_X = mybir.AxisListType.X

P = 128
T = 256
TT = T // P
D = 1024
KC = D // P
HD = 64
EPS = 1e-6
SCALE = HD ** -0.5
NEG = -1e30

D_FF = 2816
N_EXPERTS = 8
D_FFE = 3584
TOP_K = 2

GQ, GK, GV, GLOW, GOUT, SQ, SK, SV, L0_IN = 0, 256, 512, 1024, 1040, 1552, 2064, 2192, 2320
RQ, RK, RV, RG, NQ, L1_IN = 0, 256, 512, 1024, 1536, 2840
KS_, KW_, KC_, VC_, VS_, VW_, NG_ = 2048, 2176, 2304, 2432, 2560, 2688, 2816

NCMP = 15
CMP_H = 256
SLAB = 512
RING = 7

C_ID, C_TRI, C_SAME, C_CH, C_RD, C_RO, C_SWA, C_FULL = 0, 128, 256, 384, 386, 898, 1410, 1666
C_CADD, C_CONE, C_INV, C_IOTA, NC = 1922, 1952, 1982, 2022, 2030
R_GB, R_GN, R_SQ, R_SK, R_RN, R_NQ, R_KC, R_KS, R_KW, R_B2K, R_B2V, R_SINK, R_RB, NR = (
    0, 256, 384, 448, 512, 1024, 1088, 1152, 1216, 1280, 1344, 1408, 1416, 1424)
V_LN, V_B1K, V_B1V, V_PK, V_PV, NV = 0, 32, 34, 36, 52, 68

TWO_PI = 6.283185307179586
PI2_A = 6.28125
PI2_B = 0.00193500518798828125
PI2_C = TWO_PI - PI2_A - PI2_B
ROUND = 12582912.0

L0_PROJ = 0
L0_OUT = L0_PROJ + 5
L0_FFN = L0_OUT + 2
FFN_SLABS = -(-D_FF // SLAB)
L1_PROJ = L0_FFN + 3 * FFN_SLABS
L1_CMP = L1_PROJ + 6
L1_OUT = L1_CMP + 2
MOE = L1_OUT + 2
MOE_SLABS = D_FFE // SLAB
MOE_SLOTS = 3 * MOE_SLABS
FFN_TILES = D_FF // P
MOE_TILES = D_FFE // P
assert MOE % RING == 0 and MOE_SLOTS % RING == 0


def gate_slot(j):
    return 3 * j - 1 if j else 0


def up_slot(j):
    return gate_slot(j) + 1


def down_slot(j, slabs):
    return 3 * j + 4 if j < slabs - 1 else 3 * slabs - 1


def ffn_order(slabs):
    order = [None] * (3 * slabs)
    for j in range(slabs):
        order[gate_slot(j)] = ("gate", j)
        order[up_slot(j)] = ("up", j)
        order[down_slot(j, slabs)] = ("down", j)
    return order


def tiles_of(j, tiles):
    return range(4 * j, min(4 * j + 4, tiles))


def spread(ap, axis, n):
    v = ap.unsqueeze(axis)
    shape = list(v.shape)
    shape[axis] = n
    return v.to_broadcast(shape)


def build(nc, x, pos, consts, rowv, colv, w):
    with ExitStack() as ctx:
        def sb(name, shape, dt=F32):
            return ctx.enter_context(nc.sbuf_tensor(name, shape, dt))

        def sem(name):
            return ctx.enter_context(nc.semaphore(name))

        out = w["out"]
        ring = sb("ring", [P, RING, 4096])
        h = sb("h", [P, TT, D])
        xn = sb("xn", [P, TT, D])
        xT = sb("xT", [P, KC, T])
        pr = sb("pr", [P, TT, L1_IN])
        con = sb("con", [P, NC])
        row = sb("row", [P, NR])
        col = sb("col", [P, NV])
        ws = sb("ws", [P, 4096])
        qkT = sb("qkT", [P, 2048])
        gT = sb("gT", [16, T])
        gup = sb("gup", [16, 256])
        posi = sb("posi", [P, 3], I32)
        posf = sb("posf", [P, 3])
        trig = sb("trig", [P, 2, 3, 40])
        w2 = sb("w2", [P, 2, 2, HD])
        kcT = sb("kcT", [P, 64])
        cv = sb("cv", [64, 2, HD])
        rw = sb("rw", [P, KC, N_EXPERTS])
        mbf = sb("mbf", [P, 2, T], BF16)
        idb = sb("idb", [P, P], BF16)
        mhalf = sb("mhalf", [P, 24])
        sm = sb("sm", [P, 512])
        ps = [ctx.enter_context(nc.psum_tensor(f"ps{i}", [P, 512], F32)) for i in range(8)]

        ident = con[:, C_ID:C_ID + P]
        tri = con[:, C_TRI:C_TRI + P]
        same = con[:, C_SAME:C_SAME + P]
        mix = xn
        mixT = xT

        ssq = sm[:, 0:8]
        rstd = sm[:, 8:16]
        hss = sm[:, 16:40]
        hrs = sm[:, 40:64]
        dec = sm[:, 64:72]
        amax = sm[:, 72:80]
        nmax = sm[:, 80:88]
        sinkd = sm[:, 88:96]
        esink = sm[:, 96:104]
        den = sm[:, 104:120].rearrange("p (t h) -> p t h", t=2)
        rden = sm[:, 120:128]
        wgt = sm[:, 128:136]
        gates = sm[:, 136:184].rearrange("p (t c) -> p t c", t=2)
        logit = sm[:, 184:200].rearrange("p (t e) -> p t e", t=2)
        top = sm[:, 200:216].rearrange("p (t e) -> p t e", t=2)
        topi = sm[:, 216:232].bitcast(U32).rearrange("p (t e) -> p t e", t=2)
        topf = sm[:, 232:248].rearrange("p (t e) -> p t e", t=2)
        dtop = sm[:, 248:250]
        etop = sm[:, 250:252]
        wtop = sm[:, 252:256].rearrange("p (k t) -> p k t", k=2)
        comb = sm[:, 256:272].rearrange("p (t e) -> p t e", t=2)
        comb2 = sm[:, 272:288].rearrange("p (t e) -> p t e", t=2)
        dsum = sm[:, 288:290]
        hmu = sm[:, 296:304]
        cden = sm[:, 304:320].rearrange("p (t h) -> p t h", t=2)
        cmx = sm[:, 320:336].rearrange("p (t h) -> p t h", t=2)
        ckss = sm[0:64, 336:338]

        x_in = sem("x_in")
        small_in = sem("small_in")
        slot_full = [sem(f"slot_full{i}") for i in range(RING)]
        sumsq_ready = sem("sumsq_ready")
        xn_ready = sem("xn_ready")
        xnT_done = sem("xnT_done")
        xT_ready = sem("xT_ready")
        proj_done = sem("proj_done")
        proj_out = sem("proj_out")
        dve_steps = sem("dve_steps")
        act_steps = sem("act_steps")
        pool_steps = sem("pool_steps")
        mhalf_ready = sem("mhalf_ready")
        mean_ready = sem("mean_ready")
        rsqrt_ready = sem("rsqrt_ready")
        masks_ready = sem("masks_ready")
        gT_done = sem("gT_done")
        gT_ready = sem("gT_ready")
        z_done = sem("z_done")
        z_ready = sem("z_ready")
        softplus_ready = sem("softplus_ready")
        la_ready = sem("la_ready")
        cum_done = sem("cum_done")
        decay_ready = sem("decay_ready")
        dl_ready = sem("dl_ready")
        ebl_ready = sem("ebl_ready")
        gla_ops_ready = sem("gla_ops_ready")
        gla_T_done = sem("gla_T_done")
        gla_T_ready = sem("gla_T_ready")
        kv_done = sem("kv_done")
        state_ready = sem("state_ready")
        lin_scores_done = sem("lin_scores_done")
        lin_scores_ready = sem("lin_scores_ready")
        lin_out_done = sem("lin_out_done")
        lin_sq_ready = sem("lin_sq_ready")
        silu_ready = sem("silu_ready")
        head_sq_ready = sem("head_sq_ready")
        head_rows_ready = sem("head_rows_ready")
        dup_ready = sem("dup_ready")
        trig_ready = sem("trig_ready")
        angle_ready = sem("angle_ready")
        head_T_done = sem("head_T_done")
        head_T_ready = sem("head_T_ready")
        scores_done = sem("scores_done")
        nmax_ready = sem("nmax_ready")
        esink_ready = sem("esink_ready")
        probs_ready = sem("probs_ready")
        probsT_done = sem("probsT_done")
        probsT_act = sem("probsT_act")
        probsT_dve = sem("probsT_dve")
        pv_done = sem("pv_done")
        pv_used = sem("pv_used")
        mix_ready = sem("mix_ready")
        mixT_done = sem("mixT_done")
        mixT_ready = sem("mixT_ready")
        out_done = sem("out_done")
        h_ready = sem("h_ready")
        ret_rows_ready = sem("ret_rows_ready")
        ret_T_done = sem("ret_T_done")
        ret_T_ready = sem("ret_T_ready")
        kcT_done = sem("kcT_done")
        blk_ready = sem("blk_ready")
        hid_done = sem("hid_done")
        hid_x = sem("hid_x")
        hid_e = sem("hid_e")
        hid_ready = sem("hid_ready")
        cmp_done = sem("cmp_done")
        ckv_ready = sem("ckv_ready")
        cksq_ready = sem("cksq_ready")
        ckT_done = sem("ckT_done")
        ckT_ready = sem("ckT_ready")
        cs_done = sem("cs_done")
        cs_ready = sem("cs_ready")
        ce_ready = sem("ce_ready")
        cp_ready = sem("cp_ready")
        cpT_done = sem("cpT_done")
        cpT_ready = sem("cpT_ready")
        cpv_done = sem("cpv_done")
        gates_ready = sem("gates_ready")
        gate_up_done = sem("gate_up_done")
        silu_gate = sem("silu_gate")
        hidden_ready = sem("hidden_ready")
        down_done = sem("down_done")
        y_added = sem("y_added")
        router_done = sem("router_done")
        dtop_ready = sem("dtop_ready")
        etop_ready = sem("etop_ready")
        stored = sem("stored")

        block = ctx.enter_context(nc.Block())

        SMALL = 16 * 8

        def rows(ap):
            return ap.rearrange("(k p) n -> p k n", p=P)

        def slot3(n, k):
            return ring[:, n % RING, :].rearrange("p (k n) -> p k n", k=k)

        @block.sync
        def _(sp):
            def load(n, src):
                k, cols = src.shape[1], src.shape[2]
                dst = ring[:, n % RING, 0:k * cols].rearrange("p (k n) -> p k n", k=k)
                sp.dma_start(dst, src).then_inc(slot_full[n % RING], 16)

            def ffn_src(kind, j, wg, wu, wd, tiles):
                lo, hi = SLAB * j, min(SLAB * (j + 1), tiles * P)
                if kind == "down":
                    return rows(wd[lo:hi, :])
                return rows((wg if kind == "gate" else wu)[:, lo:hi])

            def wait_ffn_slot(order, r, tiles, gu0, dn0):
                kind, j = order[r]
                if kind == "down":
                    sp.wait_ge(down_done, dn0 + j + 1)
                else:
                    sp.wait_ge(gate_up_done, gu0 + min(4 * j + 4, tiles))

            def wait_free(n):
                m = n - RING
                if m < 0:
                    return
                if m < L0_OUT:
                    sp.wait_ge(proj_done, 2 * (m + 1))
                elif m < L0_FFN:
                    sp.wait_ge(out_done, 2 * (m - L0_OUT + 1))
                elif m < L1_PROJ:
                    wait_ffn_slot(ffn_order(FFN_SLABS), m - L0_FFN, FFN_TILES, 0, 0)
                elif m < L1_CMP:
                    sp.wait_ge(proj_done, 10 + 2 * (m - L1_PROJ + 1))
                elif m < L1_OUT:
                    sp.wait_ge(hid_done, m - L1_CMP + 1)
                else:
                    sp.wait_ge(out_done, 4 + 2 * (m - L1_OUT + 1))

            n = 0
            for s in range(5):
                wait_free(n)
                load(n, rows(w["w_in_e"][0, :, SLAB * s:min(SLAB * (s + 1), L0_IN)]))
                n += 1
            for s in range(2):
                wait_free(n)
                load(n, rows(w["w_out_e"][0, :, SLAB * s:SLAB * (s + 1)]))
                n += 1
            for kind, j in ffn_order(FFN_SLABS):
                wait_free(n)
                load(n, ffn_src(kind, j, w["ffn_w_gate"][0], w["ffn_w_up"][0], w["ffn_w_down"][0], FFN_TILES))
                n += 1
            for s in range(6):
                wait_free(n)
                load(n, rows(w["w_in_o"][0, :, SLAB * s:min(SLAB * (s + 1), L1_IN)]))
                n += 1
            for name in ("cmp_w1_k", "cmp_w1_v"):
                wait_free(n)
                load(n, rows(w[name][0]))
                n += 1
            for s in range(2):
                wait_free(n)
                load(n, rows(w["w_out_o"][0, :, SLAB * s:SLAB * (s + 1)]))
                n += 1

            order = ffn_order(MOE_SLABS)

            def load_expert(e, r):
                kind, j = order[r]
                name = {"gate": "exp_w_gate", "up": "exp_w_up", "down": "exp_w_down"}[kind]
                if kind == "down":
                    src = w[name][0, bass.ds(e, 1), SLAB * j:SLAB * (j + 1), :]
                else:
                    src = w[name][0, bass.ds(e, 1), :, SLAB * j:SLAB * (j + 1)]
                src = src.rearrange("a k n -> (a k) n")
                load(MOE + r, rows(src))

            for r in range(RING):
                wait_free(MOE + r)
                load_expert(0, r)

            def rest_of_expert(e):
                for r in range(RING, MOE_SLOTS):
                    wait_ffn_slot(order, r - RING, MOE_TILES, e * MOE_TILES + FFN_TILES, e * MOE_SLABS + FFN_SLABS)
                    load_expert(e, r)

            with sp.Fori(0, N_EXPERTS - 1) as e:
                rest_of_expert(e)
                for r in range(RING):
                    wait_ffn_slot(order, MOE_SLOTS - RING + r, MOE_TILES,
                                  e * MOE_TILES + FFN_TILES, e * MOE_SLABS + FFN_SLABS)
                    load_expert(e + 1, r)
            rest_of_expert(N_EXPERTS - 1)
            sp.wait_ge(y_added, 1 + N_EXPERTS)
            sp.dma_start(out.rearrange("(t p) n -> p t n", p=P), h[:, :, :]).then_inc(stored, 16)
            sp.wait_ge(stored, 16)

        UNITS = [(tt, 1024, SV, 0, None) for tt in range(TT)]
        UNITS += [(tt, 1024, VS_, 1, 1) for tt in range(TT)]
        UNITS += [(tt, 1536, VW_, 1, 2) for tt in range(TT)]
        groups_before = [0]
        for u in UNITS:
            groups_before.append(groups_before[-1] + 2 * (u[0] + 1))
        probs = ws[:, 0:2048].rearrange("p (h k) -> p h k", h=8)
        probsT = ws[:, 2048:4096].rearrange("p (k h t) -> p k h t", k=2, h=8)
        qT = qkT[:, 0:1024].rearrange("p (j t) -> p j t", j=4)

        def head_of(bank, i, per):
            half = 4 // per
            return 2 * ((bank % half) * per + i) + bank // half

        la = ws[:, 0:512].rearrange("p (t c) -> p t c", t=TT)
        eb = ws[:, 512:1024].rearrange("p (t c) -> p t c", t=TT)
        enb = ws[:, 1024:1536].rearrange("p (t c) -> p t c", t=TT)
        ebl = ws[:, 1536:2048].rearrange("p (t c) -> p t c", t=TT)
        qin = ws[:, 2048:2560].rearrange("p (t c) -> p t c", t=TT)
        kin = ws[:, 2560:3072].rearrange("p (t c) -> p t c", t=TT)
        kst = ws[:, 3072:3584].rearrange("p (t c) -> p t c", t=TT)
        tmp = ws[:, 3584:4096].rearrange("p (t c) -> p t c", t=TT)
        state = ws[:, 0:1536].rearrange("p (c h v) -> p c h v", c=3, h=4)
        linqT = qkT[:, 0:512].rearrange("p (j t) -> p j t", j=2)
        linkT = qkT[:, 512:1024].rearrange("p (j t) -> p j t", j=2)
        glasc = qkT[:, 1024:2048].rearrange("p (r t j q) -> p r t j q", r=2, t=TT, j=2)
        retsc = ws[:, 0:1536].rearrange("p (b h q) -> p b h q", b=3, h=4)
        linsq = ws[:, 2048:3072].rearrange("p (t c) -> p t c", t=TT)
        headsq = ws[:, 0:1536]
        dup = ws[:, 1536:2560].rearrange("p (t g d c) -> p t g d c", t=TT, g=4, d=2)
        rtmp = ws[:, 2560:4096]
        blk = ws[:, 0:2048].rearrange("p (v l c) -> p v l c", v=2, l=16)
        hidx = ws[:, 2048:2304].rearrange("p (v c) -> p v c", v=2)
        hide = ws[:, 2304:2560].rearrange("p (v c) -> p v c", v=2)
        hid = ws[:, 2560:2816].rearrange("p (v c) -> p v c", v=2)
        ckdup = ws[0:64, 2816:2944]
        cktmp = ws[0:64, 2944:3072]
        csm = ws[:, 3072:3328].rearrange("p (t x) -> p t x", t=TT)
        cpd = ws[:, 3328:3840].rearrange("p (t x) -> p t x", t=TT)
        cpT = ws[0:64, 0:1024].rearrange("p (t j q) -> p t j q", t=TT, j=4)
        hT = ws[:, 0:2048].rearrange("p (i t) -> p i t", i=8)
        sg = ws[:, 2048:3072].rearrange("p (i t) -> p i t", i=4)

        @block.tensor
        def _(pe):
            mm = nc.tensor.matmul

            def slot_wait(n, e=None):
                k = 16 * (n // RING + 1)
                pe.wait_ge(slot_full[n % RING], k if e is None else e * (16 * MOE_SLOTS // RING) + k)

            def transpose_norm(k):
                for tt in range(TT):
                    pe.wait_ge(xn_ready, TT * k + tt + 1)
                    for b in range(2):
                        for c in range(4):
                            last = nc.tensor.transpose(ps[4 + 2 * tt + b][:, c * P:(c + 1) * P],
                                                       xn[:, tt, (4 * b + c) * P:(4 * b + c + 1) * P], ident)
                        last.then_inc(xnT_done, 1)

            def project(first, widths, unit0, done, used):
                u = unit0
                for s, width in enumerate(widths):
                    slot_wait(first + s)
                    wt = ring[:, (first + s) % RING, 0:KC * width].rearrange("p (k n) -> p k n", k=KC)
                    for tt in range(TT):
                        if u - unit0 >= 4:
                            pe.wait_ge(used, u - 3)
                        for k in range(KC):
                            last = mm(ps[u % 4][:, 0:width], xT[:, k, tt * P:(tt + 1) * P], wt[:, k, :],
                                      start=(k == 0), stop=(k == KC - 1))
                        last.then_inc(done, 1)
                        u += 1

            def out_projection(layer):
                for tt in range(TT):
                    pe.wait_ge(mix_ready, 3 * layer + tt + 1)
                    for b in range(2):
                        for c in range(4):
                            last = nc.tensor.transpose(ps[4 + 2 * tt + b][:, c * P:(c + 1) * P],
                                                       mix[:, tt, (4 * b + c) * P:(4 * b + c + 1) * P], ident)
                        last.then_inc(mixT_done, 1)
                pe.wait_ge(mixT_ready, 4 * (layer + 1))
                project(L0_OUT if layer == 0 else L1_OUT, [SLAB, SLAB], 4 * layer, out_done, h_ready)

            def attend(n):
                tt, k0, v0, mask, _ = UNITS[n]
                kT = qkT[:, k0:k0 + 512].rearrange("p (g t) -> p g t", g=2)
                keys = P * (tt + 1)
                per = 512 // keys
                for b in range(8 // per):
                    bank = ps[b][:, :].rearrange("p (h k) -> p h k", h=per)
                    m = mbf[:, mask, T - keys:T]
                    mm(bank, idb[:, :], spread(m, 1, per), start=True, stop=False)
                    for i in range(per):
                        hh = head_of(b, i, per)
                        r = 64 * (hh % 2)
                        last = mm(bank[:, i, :], qT[r:r + 64, hh // 2, tt * P:(tt + 1) * P],
                                  kT[r:r + 64, hh // 4, 0:keys], start=False, stop=(i == per - 1))
                last.then_inc(scores_done, 1)
                pe.wait_ge(probs_ready, n + 1)
                g = groups_before[n]
                for kt in range(tt + 1):
                    for quad in range(2):
                        if g >= 2:
                            pe.wait_ge(probsT_act if g % 2 == 0 else probsT_dve, g // 2)
                        for i in range(4):
                            last = nc.tensor.transpose(ps[4 + g % 2][:, i * P:(i + 1) * P],
                                                       probs[:, 4 * quad + i, kt * P:(kt + 1) * P], ident)
                        last.then_inc(probsT_done, 1)
                        g += 1
                pe.wait_ge(probsT_act, g // 2)
                pe.wait_ge(probsT_dve, g // 2)
                if n:
                    pe.wait_ge(pv_used, n)
                for hh in range(8):
                    for kt in range(tt + 1):
                        c = v0 + HD * (hh // 4)
                        last = mm(ps[6][:, hh * HD:(hh + 1) * HD], probsT[:, kt, hh, :],
                                  pr[:, kt, c:c + HD], start=(kt == 0), stop=(kt == tt))
                last.then_inc(pv_done, 1)

            def feed_forward(first, slabs, tiles, e, gu0, dn0, y0):
                def down(j):
                    pe.wait_ge(hidden_ready, gu0 + min(4 * j + 4, tiles))
                    slot_wait(first + down_slot(j, slabs), e)
                    wd = slot3(first + down_slot(j, slabs), 4)
                    if j == 0:
                        pe.wait_ge(y_added, y0)
                    for i in tiles_of(j, tiles):
                        for tt in range(TT):
                            for half in range(2):
                                last = mm(ps[4 + 2 * tt + half][:, :], hT[:, i % 8, tt * P:(tt + 1) * P],
                                          wd[:, i % 4, half * 512:(half + 1) * 512],
                                          start=(i == 0), stop=(i == tiles - 1))
                    last.then_inc(down_done, 1)

                for j in range(slabs):
                    slot_wait(first + gate_slot(j), e)
                    slot_wait(first + up_slot(j), e)
                    width = P * len(tiles_of(j, tiles))
                    wg, wu = (ring[:, (first + f(j)) % RING, 0:KC * width].rearrange("p (k n) -> p k n", k=KC)
                              for f in (gate_slot, up_slot))
                    for i in tiles_of(j, tiles):
                        if i >= 4 or first > L0_FFN:
                            pe.wait_ge(hidden_ready, gu0 + (i - 3))
                        c = (i % 4) * P
                        for k in range(KC):
                            mm(ps[i % 4][:, 0:T], wg[:, k, c:c + P], xT[:, k, :], start=(k == 0), stop=(k == KC - 1))
                        for k in range(KC):
                            last = mm(ps[i % 4][:, T:2 * T], wu[:, k, c:c + P], xT[:, k, :],
                                      start=(k == 0), stop=(k == KC - 1))
                        last.then_inc(gate_up_done, 1)
                    if j:
                        down(j - 1)
                down(slabs - 1)

            def linear_scores(banks, at, q_tt, k_tt):
                for hh in range(4):
                    r = 64 * (hh % 2)
                    c = (2 * at + hh // 2) * P
                    last = mm(banks[hh % 2][:, c:c + P], linkT[r:r + 64, hh // 2, k_tt * P:(k_tt + 1) * P],
                              linqT[r:r + 64, hh // 2, q_tt * P:(q_tt + 1) * P], start=True, stop=True)
                last.then_inc(lin_scores_done, 1)

            pe.wait_ge(small_in, SMALL)
            transpose_norm(0)
            pe.wait_ge(xT_ready, 4)
            project(L0_PROJ, [SLAB] * 4 + [L0_IN - 4 * SLAB], 0, proj_done, proj_out)
            pe.wait_ge(proj_out, 6)
            for tt in range(TT):
                last = nc.tensor.transpose(ps[4][0:16, tt * P:(tt + 1) * P], pr[:, tt, GLOW:GLOW + 16], ident)
            last.then_inc(gT_done, 1)
            pe.wait_ge(gT_ready, 1)
            for tt in range(TT):
                last = mm(ps[5][:, tt * 256:(tt + 1) * 256], gT[:, tt * P:(tt + 1) * P], gup[:, :],
                          start=True, stop=True)
            last.then_inc(z_done, 1)
            pe.wait_ge(la_ready, 1)
            for tt in range(TT):
                mm(ps[6][:, tt * 256:(tt + 1) * 256], tri, la[:, tt, :], start=True, stop=True)
                mm(ps[7][:, tt * 256:(tt + 1) * 256], same, la[:, tt, :], start=True, stop=True)
                for hp in range(2):
                    c = 4 * hp + 2 * tt
                    last = mm(ps[4][:, c:c + 2], la[:, tt, hp * P:(hp + 1) * P], con[:, C_CH:C_CH + 2],
                              start=True, stop=True)
            last.then_inc(cum_done, 1)
            pe.wait_ge(gla_ops_ready, 1)
            pe.wait_ge(proj_out, 10)
            for src, bank in ((qin, ps[0]), (kin, ps[1])):
                for hp in range(2):
                    for tt in range(TT):
                        c = (2 * hp + tt) * P
                        last = nc.tensor.transpose(bank[:, c:c + P], src[:, tt, hp * P:(hp + 1) * P], ident)
                last.then_inc(gla_T_done, 1)
            for c in range(3):
                r = 64 * (c % 2)
                for hp in range(2):
                    last = mm(ps[5 + c][:, hp * 256:(hp + 1) * 256], kst[r:r + 64, c // 2, hp * P:(hp + 1) * P],
                              pr[r:r + 64, c // 2, GV + hp * 256:GV + (hp + 1) * 256], start=True, stop=True)
            last.then_inc(kv_done, 1)
            pe.wait_ge(gla_T_ready, 2)
            for tt in range(TT):
                linear_scores(ps[2:4], tt, tt, tt)
            pe.wait_ge(state_ready, 1)
            pe.wait_ge(lin_scores_ready, 2)
            for tt in range(TT):
                for hh in range(4):
                    for c in range(2 * tt, 2 * tt + 2):
                        t0 = 64 * (c % 2)
                        o = ps[tt][t0:t0 + 64, hh * P:(hh + 1) * P]
                        last = mm(o, glasc[:, hh % 2, tt, hh // 2, t0:t0 + 64],
                                  pr[:, tt, GV + hh * P:GV + (hh + 1) * P], start=True, stop=(c == 0))
                        if c:
                            last = mm(o, linqT[:, hh // 2, c * 64:(c + 1) * 64], state[:, c - 1, hh, :],
                                      start=False, stop=True)
                last.then_inc(lin_out_done, 1)

            def head_transposes(n_q, n_k, done0):
                for j in range(n_q):
                    for tt in range(TT):
                        c = (2 * (j % 2) + tt) * P
                        last = nc.tensor.transpose(ps[2 + j // 2][:, c:c + P],
                                                   pr[:, tt, done0 + j * P:done0 + (j + 1) * P], ident)
                    if j % 2:
                        last.then_inc(head_T_done, 1)

            def dup_transposes(n_k):
                for g in range(n_k):
                    for tt in range(TT):
                        c = (2 * (g % 2) + tt) * P
                        src = dup[:, tt, g, :, :].rearrange("p d c -> p (d c)")
                        last = nc.tensor.transpose(ps[4 + g // 2][:, c:c + P], src, ident)
                    if g % 2:
                        last.then_inc(head_T_done, 1)

            pe.wait_ge(head_rows_ready, 1)
            pe.wait_ge(dup_ready, 1)
            head_transposes(4, 2, SQ)
            dup_transposes(2)
            pe.wait_ge(head_T_ready, 3)
            pe.wait_ge(masks_ready, 3)
            for n in range(2):
                attend(n)
            out_projection(0)
            transpose_norm(1)
            pe.wait_ge(xT_ready, 8)
            feed_forward(L0_FFN, FFN_SLABS, FFN_TILES, None, 0, 0, 0)

            transpose_norm(2)
            pe.wait_ge(xT_ready, 12)
            project(L1_PROJ, [SLAB] * 5 + [L1_IN - 5 * SLAB], 10, proj_done, proj_out)
            pe.wait_ge(ret_rows_ready, 1)
            for i, bank in ((0, ps[4]), (1, ps[5])):
                for hp in range(2):
                    for tt in range(TT):
                        c = (2 * hp + tt) * P
                        src = pr[:, tt, RQ + 256 * i + hp * P:RQ + 256 * i + (hp + 1) * P]
                        last = nc.tensor.transpose(bank[:, c:c + P], src, ident)
                last.then_inc(ret_T_done, 1)
            pe.wait_ge(ret_T_ready, 2)
            pe.wait_ge(proj_out, 22)
            linear_scores(ps[0:2], 0, 0, 0)
            linear_scores(ps[0:2], 1, 1, 1)
            linear_scores(ps[2:4], 0, 1, 0)
            pe.wait_ge(lin_scores_ready, 2 + 6)
            for tt in range(TT):
                for hh in range(4):
                    blocks = [(0, 0)] if tt == 0 else [(1, 1), (2, 0)]
                    for n, (b, kt) in enumerate(blocks):
                        last = mm(ps[6 + tt][:, hh * P:(hh + 1) * P], retsc[:, b, hh, :],
                                  pr[:, kt, RV + hh * P:RV + (hh + 1) * P], start=(n == 0), stop=(n == tt))
                last.then_inc(lin_out_done, 1)
            pe.wait_ge(head_rows_ready, 2)
            pe.wait_ge(dup_ready, 2)
            head_transposes(4, 4, NQ)
            dup_transposes(4)
            pe.wait_ge(head_T_ready, 7)
            for i in range(2):
                for tt in range(TT):
                    last = nc.tensor.transpose(ps[i][:, tt * P:(tt + 1) * P],
                                               pr[:, tt, KC_ + i * P:KC_ + (i + 1) * P], ident)
                last.then_inc(kcT_done, 1)
            for i in range(2):
                pe.wait_ge(blk_ready, i + 1)
                slot_wait(L1_CMP + i)
                w1 = slot3(L1_CMP + i, 16)
                for ht in range(2):
                    for l in range(16):
                        last = mm(ps[2 + i][:, ht * 64:(ht + 1) * 64], w1[:, l, ht * P:(ht + 1) * P],
                                  blk[:, i, l, :], start=(l == 0), stop=(l == 15))
                last.then_inc(hid_done, 1)
            pe.wait_ge(hid_ready, 1)
            for i in range(2):
                for ht in range(2):
                    last = mm(ps[4][0:64, i * HD:(i + 1) * HD], hid[:, i, ht * 64:(ht + 1) * 64], w2[:, i, ht, :],
                              start=(ht == 0), stop=(ht == 1))
            last.then_inc(cmp_done, 1)
            pe.wait_ge(ckv_ready, 1)
            nc.tensor.transpose(ps[5][:, 0:64], ckdup, ident[0:64, 0:64]).then_inc(ckT_done, 1)
            pe.wait_ge(ckT_ready, 1)
            for tt in range(TT):
                for hh in range(8):
                    r, g = 64 * (hh % 2), hh // 4
                    c = 64 * tt + (hh % 4 // 2 * 2 + g) * 16
                    last = mm(ps[hh % 2][:, c:c + NCMP], qT[r:r + 64, hh // 2, tt * P:(tt + 1) * P],
                              kcT[r:r + 64, 32 * g:32 * g + NCMP], start=True, stop=True)
            last.then_inc(cs_done, 1)
            pe.wait_ge(cp_ready, 1)
            for tt in range(TT):
                for j in range(4):
                    last = nc.tensor.transpose(ps[2 + tt][0:64, j * P:(j + 1) * P], cpd[:, tt, j * 64:(j + 1) * 64],
                                               ident)
                last.then_inc(cpT_done, 1)
            pe.wait_ge(cpT_ready, 2)
            for tt in range(TT):
                for hh in range(8):
                    g, j = hh // 4, 2 * (hh % 2) + hh % 4 // 2
                    c = 256 * tt + (hh % 4) * HD
                    last = mm(ps[4 + g][:, c:c + HD], cpT[32 * g:32 * g + 32, tt, j, :],
                              cv[32 * g:32 * g + 32, 1, :], start=True, stop=True)
                last.then_inc(cpv_done, 1)
            pe.wait_ge(mix_ready, 3)
            for n in range(2, 6):
                attend(n)
            out_projection(1)
            transpose_norm(3)
            pe.wait_ge(xT_ready, 16)
            for tt in range(TT):
                for k in range(KC):
                    last = mm(ps[0][:, tt * 8:(tt + 1) * 8], xT[:, k, tt * P:(tt + 1) * P], rw[:, k, :],
                              start=(k == 0), stop=(k == KC - 1))
            last.then_inc(router_done, 1)
            pe.wait_ge(dtop_ready, 1)
            with pe.Fori(0, N_EXPERTS) as e:
                feed_forward(MOE, MOE_SLABS, MOE_TILES, e, e * MOE_TILES + FFN_TILES,
                             e * MOE_SLABS + FFN_SLABS, e + 1)

        @block.scalar
        def _(act):
            A = nc.scalar.activation
            steps = [0]

            def step(ins):
                steps[0] += 1
                ins.then_inc(act_steps, 1)

            def settle():
                act.wait_ge(act_steps, steps[0])

            act.dma_start(h[:, :, :], x.rearrange("(t p) n -> p t n", p=P)).then_inc(x_in, 16)
            act.dma_start(con[:, :], consts).then_inc(small_in, 16)
            act.dma_start(col[:, :], colv).then_inc(small_in, 16)
            act.dma_start(row[:, :], rowv.partition_broadcast(P)).then_inc(small_in, 16)
            act.dma_start(posi[:, :], pos).then_inc(small_in, 16)
            act.dma_start(gup[:, :], w["gla_gate_up"][0]).then_inc(small_in, 16)
            act.dma_start(w2[:, 0, :, :], rows(w["cmp_w2_k"][0])).then_inc(small_in, 16)
            act.dma_start(w2[:, 1, :, :], rows(w["cmp_w2_v"][0])).then_inc(small_in, 16)
            act.dma_start(rw[:, :, :], rows(w["router_w"][0])).then_inc(small_in, 16)

            def sums_of_squares(k):
                for tt in range(TT):
                    c = TT * k + tt
                    A(xn[:, tt, :], h[:, tt, :], ACT.Square, accum_out=ssq[:, c:c + 1]).then_inc(sumsq_ready, 1)

            def copy_projection(units, pieces):
                for u, (tt, parts) in zip(units, pieces):
                    act.wait_ge(proj_done, u + 1)
                    for n, (src, dst, width) in enumerate(parts):
                        ins = A(pr[:, tt, dst:dst + width], ps[u % 4][:, src:src + width], ACT.Copy)
                        if n == len(parts) - 1:
                            ins.then_inc(proj_out, 1)

            def attend(n):
                tt = UNITS[n][0]
                keys = P * (tt + 1)
                per = 512 // keys
                act.wait_ge(nmax_ready, n + 1)
                if n:
                    act.wait_ge(probsT_done, groups_before[n])
                for b in range(8 // per):
                    for i in range(per):
                        hh = head_of(b, i, per)
                        ins = A(probs[:, hh, 0:keys], ps[b][:, i * keys:(i + 1) * keys], ACT.Exp,
                                bias=nmax[:, hh:hh + 1], scale=SCALE, accum_out=den[:, tt, hh:hh + 1])
                ins.then_inc(probs_ready, 1)
                if UNITS[n][4] is None:
                    A(esink, sinkd, ACT.Exp).then_inc(esink_ready, 1)
                for g in range(groups_before[n], groups_before[n + 1], 2):
                    kt = (g - groups_before[n]) // 2
                    act.wait_ge(probsT_done, g + 1)
                    if n:
                        act.wait_ge(pv_done, n)
                    A(probsT[:, kt, 0:4, :], ps[4][:, :].rearrange("p (h t) -> p h t", h=4),
                      ACT.Copy).then_inc(probsT_act, 1)

            def feed_forward(tiles, gu0):
                for i in range(tiles):
                    act.wait_ge(gate_up_done, gu0 + (i + 1))
                    if i >= 4 or gu0 is not FIRST:
                        act.wait_ge(hidden_ready, gu0 + (i - 3))
                    A(sg[:, i % 4, :], ps[i % 4][:, 0:T], ACT.Silu).then_inc(silu_gate, 1)

            FIRST = 0
            act.wait_ge(x_in, 16)
            sums_of_squares(0)
            act.wait_ge(small_in, SMALL)
            for m, c0 in enumerate((C_SWA, C_FULL)):
                A(mbf[:, m, :], con[:, c0:c0 + T], ACT.Copy).then_inc(masks_ready, 1)
            A(idb[:, :], ident, ACT.Copy).then_inc(masks_ready, 1)
            act.wait_ge(angle_ready, 1)
            A(trig[:, :, :, :], trig[:, :, :, :], ACT.Sin).then_inc(trig_ready, 1)
            copy_projection(range(10), [(u % 2, [(0, SLAB * (u // 2), min(SLAB, L0_IN - SLAB * (u // 2)))])
                                        for u in range(10)])
            act.wait_ge(z_ready, 1)
            step(A(tmp[:, :, :], eb[:, :, :], ACT.Exp, scale=-1.0))
            settle()
            A(tmp[:, :, :], tmp[:, :, :], ACT.Ln, bias=1.0).then_inc(softplus_ready, 1)
            act.wait_ge(cum_done, 1)
            act.wait_ge(dl_ready, 1)
            cum = ps[6][:, :].rearrange("p (t c) -> p t c", t=TT)
            A(eb[:, :, :], cum, ACT.Exp, scale=1.0 / 16)
            A(enb[:, :, :], cum, ACT.Exp, scale=-1.0 / 16)
            A(dec, ps[4][:, 0:8], ACT.Exp, scale=1.0 / 16).then_inc(decay_ready, 1)
            A(ebl[:, :, :], tmp[:, :, :], ACT.Exp, scale=1.0 / 16).then_inc(ebl_ready, 1)
            for i, dst in enumerate((linqT, linkT)):
                act.wait_ge(gla_T_done, i + 1)
                A(dst[:, :, :], ps[i][:, :].rearrange("p (j t) -> p j t", j=2), ACT.Copy).then_inc(gla_T_ready, 1)
            for tt in range(TT):
                act.wait_ge(lin_out_done, tt + 1)
                A(linsq[:, tt, :], ps[tt][:, :], ACT.Square).then_inc(lin_sq_ready, 1)
            for tt in range(TT):
                A(pr[:, tt, GOUT:GOUT + 512], pr[:, tt, GOUT:GOUT + 512], ACT.Silu).then_inc(silu_ready, 1)

            def head_squares(c0, heads, n):
                v = headsq[:, 0:TT * heads * HD].rearrange("p (t c) -> p t c", t=TT)
                A(v, pr[:, :, c0:c0 + heads * HD], ACT.Square).then_inc(head_sq_ready, 1)

            def head_copies(first, banks):
                for i, (b, c) in enumerate(banks):
                    act.wait_ge(head_T_done, first + i + 1)
                    A(qkT[:, c:c + 512], ps[b][:, :], ACT.Copy).then_inc(head_T_ready, 1)

            head_squares(SQ, 10, 0)
            act.wait_ge(head_rows_ready, 1)
            for d in range(2):
                ins = A(dup[:, :, 0:2, d, :], pr[:, :, SK:SK + 128].rearrange("p t (g c) -> p t g c", g=2), ACT.Copy)
            ins.then_inc(dup_ready, 1)
            head_copies(0, [(2, 0), (3, 512), (4, 1024)])
            for n in range(2):
                attend(n)
            act.wait_ge(h_ready, 4)
            sums_of_squares(1)
            feed_forward(FFN_TILES, FIRST)

            act.wait_ge(y_added, 1)
            sums_of_squares(2)
            pieces = [(u % 2, [(0, SLAB * (u // 2), SLAB)]) for u in range(8)]
            pieces += [(tt, [(0, KC_, 256), (256, KS_, 128), (384, VS_, 128)]) for tt in range(TT)]
            pieces += [(tt, [(0, KW_, 128), (128, VW_, 152)]) for tt in range(TT)]
            copy_projection(range(10, 22), pieces)
            for i, dst in enumerate((linqT, linkT)):
                act.wait_ge(ret_T_done, i + 1)
                A(dst[:, :, :], ps[4 + i][:, :].rearrange("p (j t) -> p j t", j=2), ACT.Copy).then_inc(ret_T_ready, 1)
            for tt in range(TT):
                A(pr[:, tt, RG:RG + 512], pr[:, tt, RG:RG + 512], ACT.Silu).then_inc(silu_ready, 1)
            act.wait_ge(proj_out, 22)
            A(gates[:, :, :], pr[:, :, NG_:NG_ + 24], ACT.Exp, scale=-1.0).then_inc(gates_ready, 1)
            act.wait_ge(lin_out_done, 4)
            head_squares(NQ, 12, 1)
            act.wait_ge(head_rows_ready, 2)
            for d in range(2):
                ins = A(dup[:, :, :, d, :], pr[:, :, KS_:KS_ + 256].rearrange("p t (g c) -> p t g c", g=4), ACT.Copy)
            ins.then_inc(dup_ready, 1)
            head_copies(3, [(2, 0), (3, 512), (4, 1024), (5, 1536)])
            act.wait_ge(hid_x, 1)
            A(hide[:, :, :], hide[:, :, :], ACT.Exp, scale=-2 * 0.7978845608028654).then_inc(hid_e, 1)
            act.wait_ge(ckT_done, 1)
            A(kcT[:, :], ps[5][:, 0:64], ACT.Copy).then_inc(ckT_ready, 1)
            act.wait_ge(cs_ready, 1)
            A(csm[:, :, 0:120], csm[:, :, 0:120], ACT.Exp, scale=SCALE).then_inc(ce_ready, 1)
            for tt in range(TT):
                act.wait_ge(cpT_done, tt + 1)
                A(cpT[:, tt, :, :], ps[2 + tt][0:64, :].rearrange("p (j q) -> p j q", j=4),
                  ACT.Copy).then_inc(cpT_ready, 1)
            for n in range(2, 6):
                attend(n)
            act.wait_ge(h_ready, 8)
            sums_of_squares(3)
            act.wait_ge(dtop_ready, 1)
            A(etop, dtop, ACT.Exp).then_inc(etop_ready, 1)
            with act.Fori(0, N_EXPERTS) as e:
                feed_forward(MOE_TILES, e * MOE_TILES + FFN_TILES)

        @block.vector
        def _(dve):
            V = nc.vector
            steps = [0]
            powers = [0]

            def step(ins):
                steps[0] += 1
                ins.then_inc(dve_steps, 1)

            def settle():
                dve.wait_ge(dve_steps, steps[0])

            def link(ins):
                step(ins)
                settle()

            def normalise(k):
                dve.wait_ge(sumsq_ready, TT * (k + 1))
                rsqrt_mean(rstd[:, TT * k:TT * (k + 1)], ssq[:, TT * k:TT * (k + 1)], D)
                for tt in range(TT):
                    c = TT * k + tt
                    V.tensor_scalar(xn[:, tt, :], h[:, tt, :], rstd[:, c:c + 1], None, ALU.mult).then_inc(xn_ready, 1)
                for tt in range(TT):
                    for b in range(2):
                        dve.wait_ge(xnT_done, 4 * k + 2 * tt + b + 1)
                        g = col[:, V_LN + KC * k + 4 * b:V_LN + KC * k + 4 * b + 4]
                        V.tensor_tensor(xT[:, 4 * b:4 * b + 4, tt * P:(tt + 1) * P],
                                        ps[4 + 2 * tt + b][:, :].rearrange("p (c t) -> p c t", c=4),
                                        spread(g, 2, P), ALU.mult).then_inc(xT_ready, 1)

            def rsqrt_mean(dst, src, n):
                powers[0] += 1
                V.tensor_scalar(dst, src, 1.0 / n, EPS, ALU.mult, ALU.add).then_inc(mean_ready, 1)
                dve.wait_ge(rsqrt_ready, powers[0])

            def rotate(x1, x2, cos, sin, t):
                step(V.tensor_tensor(t[0], x1, cos, ALU.mult))
                step(V.tensor_tensor(t[1], x2, sin, ALU.mult))
                step(V.tensor_tensor(t[2], x2, cos, ALU.mult))
                step(V.tensor_tensor(t[3], x1, sin, ALU.mult))
                settle()
                step(V.tensor_tensor(x1, t[0], t[1], ALU.subtract))
                return V.tensor_tensor(x2, t[2], t[3], ALU.add)

            def heads_norm(c0, heads, gains, n):
                dve.wait_ge(head_sq_ready, n + 1)
                v = headsq[:, 0:TT * heads * HD].rearrange("p (t h c) -> p (t h) c", t=TT, c=HD)
                ss = hss[:, 0:TT * heads]
                rs = hrs[:, 0:TT * heads]
                link(V.tensor_reduce(ss, v, AX_X, ALU.add))
                rsqrt_mean(rs, ss, HD)
                xh = pr[:, :, c0:c0 + heads * HD].rearrange("p t (h c) -> p t h c", h=heads)
                link(V.tensor_tensor(xh, xh, spread(rs.rearrange("p (t h) -> p t h", t=TT), 3, HD), ALU.mult))
                at = 0
                for g0, count in gains:
                    for tt in range(TT):
                        g = spread(row[:, g0:g0 + HD], 1, count)
                        step(V.tensor_tensor(xh[:, tt, at:at + count, :], xh[:, tt, at:at + count, :], g, ALU.mult))
                    at += count
                settle()
                sin = spread(trig[:, 0, 0:TT, 0:8], 2, heads)
                cos = spread(trig[:, 1, 0:TT, 0:8], 2, heads)
                w_ = TT * heads * 8
                t = [rtmp[:, i * w_:(i + 1) * w_].rearrange("p (t h c) -> p t h c", t=TT, h=heads) for i in range(4)]
                rotate(xh[:, :, :, 0:8], xh[:, :, :, 8:16], cos, sin, t).then_inc(head_rows_ready, 1)
                dve.wait_ge(head_rows_ready, n + 1)

            def attend(n):
                tt, _, _, _, branch = UNITS[n]
                keys = P * (tt + 1)
                per = 512 // keys
                dve.wait_ge(scores_done, n + 1)
                for b in range(8 // per):
                    first = head_of(b, 0, per)
                    heads = amax.rearrange("p (i r) -> p r i", r=2)[:, first % 2, first // 2:first // 2 + per]
                    step(V.tensor_reduce(heads,
                                         ps[b][:, :].rearrange("p (h k) -> p h k", h=per), AX_X, ALU.max))
                settle()
                if branch is None:
                    sink = row[:, R_SINK:R_SINK + 8]
                    link(V.scalar_tensor_tensor(amax, amax, SCALE, sink, ALU.mult, ALU.max))
                    if n:
                        dve.wait_ge(esink_ready, n)
                    step(V.tensor_tensor(sinkd, sink, amax, ALU.subtract))
                    V.tensor_scalar(nmax, amax, -1.0, None, ALU.mult).then_inc(nmax_ready, 1)
                else:
                    V.tensor_scalar(nmax, amax, -SCALE, None, ALU.mult).then_inc(nmax_ready, 1)
                for g in range(groups_before[n] + 1, groups_before[n + 1], 2):
                    kt = (g - groups_before[n]) // 2
                    dve.wait_ge(probsT_done, g + 1)
                    V.tensor_copy(probsT[:, kt, 4:8, :],
                                  ps[5][:, :].rearrange("p (h t) -> p h t", h=4)).then_inc(probsT_dve, 1)
                dd = den[:, tt, :]
                if branch is None:
                    dve.wait_ge(esink_ready, n + 1)
                    link(V.tensor_tensor(dd, dd, esink, ALU.add))
                link(V.reciprocal(rden, dd))
                o = ps[6][:, :].rearrange("p (h c) -> p h c", h=8)
                dst = mix[:, tt, 512:1024].rearrange("p (h c) -> p h c", h=8)
                if branch is None:
                    dve.wait_ge(pv_done, n + 1)
                    V.tensor_tensor(dst, o, spread(rden, 2, HD), ALU.mult).then_inc(pv_used, 1)
                else:
                    gt = gates[:, tt, :].rearrange("p (h b) -> p h b", b=3)[:, :, branch]
                    link(V.tensor_tensor(wgt, rden, gt, ALU.mult))
                    dve.wait_ge(pv_done, n + 1)
                    t = qkT_tmp
                    V.tensor_tensor(t, o, spread(wgt, 2, HD), ALU.mult).then_inc(pv_used, 1)
                    dve.wait_ge(pv_used, n + 1)
                    ins = V.tensor_tensor(dst, dst, t, ALU.add)
                    if branch == 2:
                        ins.then_inc(mix_ready, 1)
                    else:
                        step(ins)
                        settle()

            qkT_tmp = pr[:, 0, RG:RG + 512].rearrange("p (h c) -> p h c", h=8)

            def copy_mixT(layer):
                for tt in range(TT):
                    for b in range(2):
                        dve.wait_ge(mixT_done, 4 * layer + 2 * tt + b + 1)
                        V.tensor_copy(mixT[:, 4 * b:4 * b + 4, tt * P:(tt + 1) * P],
                                      ps[4 + 2 * tt + b][:, :].rearrange("p (c t) -> p c t", c=4))\
                         .then_inc(mixT_ready, 1)
                for u in range(4):
                    s, tt = u // 2, u % 2
                    dve.wait_ge(out_done, 4 * layer + u + 1)
                    hs = h[:, tt, s * 512:(s + 1) * 512]
                    V.tensor_tensor(hs, hs, ps[u][:, :], ALU.add).then_inc(h_ready, 1)

            def feed_forward(tiles, slabs, gu0, dn0, y0, weight):
                for i in range(tiles):
                    dve.wait_ge(silu_gate, gu0 + (i + 1))
                    if i >= 8:
                        dve.wait_ge(down_done, dn0 + (i // 4 - 1))
                    elif dn0 is not FIRST and i % 4 == 0:
                        dve.wait_ge(down_done, dn0)
                    V.tensor_tensor(hT[:, i % 8, :], sg[:, i % 4, :], ps[i % 4][:, T:2 * T],
                                    ALU.mult).then_inc(hidden_ready, 1)
                dve.wait_ge(down_done, dn0 + slabs)
                for tt in range(TT):
                    for half in range(2):
                        hs = h[:, tt, half * 512:(half + 1) * 512]
                        bank = ps[4 + 2 * tt + half][:, :]
                        if weight is None:
                            ins = V.tensor_tensor(hs, bank, hs, ALU.add)
                        else:
                            ins = V.scalar_tensor_tensor(hs, bank, weight(tt), hs, ALU.mult, ALU.add)
                ins.then_inc(y_added, 1)

            FIRST = 0
            dve.wait_ge(x_in, 16)
            normalise_first = True
            dve.wait_ge(small_in, SMALL)
            link(V.tensor_copy(posf[:, :], posi[:, :]))
            ang = ws[:, 0:120].rearrange("p (j f) -> p j f", j=3)
            turns = ws[:, 120:360].rearrange("p (s f) -> p s f", s=2)
            fold = trig[:, :, :, :].rearrange("p s j f -> p s (j f)")
            for j in range(3):
                step(V.tensor_scalar(ang[:, j, :], con[:, C_INV:C_INV + 40], posf[:, j:j + 1], None, ALU.mult))
            settle()
            angf = ws[:, 0:120]
            for s in range(2):
                step(V.tensor_scalar(turns[:, s, :], angf, 1 / TWO_PI, 0.25 * s, ALU.mult, ALU.add))
            settle()
            link(V.tensor_scalar(turns, turns, ROUND, None, ALU.add))
            link(V.tensor_scalar(turns, turns, -ROUND, None, ALU.add))
            for s in range(2):
                step(V.scalar_tensor_tensor(fold[:, s, :], turns[:, s, :], -PI2_A, angf, ALU.mult, ALU.add))
            settle()
            link(V.scalar_tensor_tensor(fold, turns, -PI2_B, fold, ALU.mult, ALU.add))
            link(V.scalar_tensor_tensor(fold, turns, -PI2_C, fold, ALU.mult, ALU.add))
            link(V.tensor_scalar(fold[:, 1, :], fold[:, 1, :], TWO_PI / 4, None, ALU.add))
            V.tensor_scalar(fold, fold, 3.1415925, -3.1415925, ALU.min, ALU.max).then_inc(angle_ready, 1)
            normalise(0)

            dve.wait_ge(gT_done, 1)
            V.tensor_copy(gT[:, :], ps[4][0:16, 0:T]).then_inc(gT_ready, 1)
            dve.wait_ge(z_done, 1)
            z = ps[5][:, :].rearrange("p (t c) -> p t c", t=TT)
            link(V.tensor_tensor(la, z, spread(row[:, R_GB:R_GB + 256], 1, TT), ALU.add))
            V.scalar_tensor_tensor(eb, la, -1.0, la, ALU.mult, ALU.max).then_inc(z_ready, 1)
            dve.wait_ge(softplus_ready, 1)
            V.scalar_tensor_tensor(la, la, 0.0, tmp, ALU.min, ALU.subtract).then_inc(la_ready, 1)
            dve.wait_ge(cum_done, 1)
            link(V.tensor_copy(ebl, ps[6][:, :].rearrange("p (t c) -> p t c", t=TT)))
            V.tensor_tensor(tmp, ps[7][:, :].rearrange("p (t c) -> p t c", t=TT), ebl,
                            ALU.subtract).then_inc(dl_ready, 1)
            dve.wait_ge(decay_ready, 1)
            step(V.scalar_tensor_tensor(qin, pr[:, :, GQ:GQ + 256], HD ** -0.5, eb, ALU.mult, ALU.mult))
            step(V.tensor_tensor(kin, pr[:, :, GK:GK + 256], enb, ALU.mult))
            dve.wait_ge(ebl_ready, 1)
            V.tensor_tensor(kst, pr[:, :, GK:GK + 256], ebl, ALU.mult).then_inc(gla_ops_ready, 1)
            dve.wait_ge(kv_done, 1)
            dve.wait_ge(pool_steps, 2)
            for c in range(3):
                for hp in range(2):
                    for r in range(2):
                        q = slice(64 * r, 64 * r + 64)
                        kv = ps[5 + c][q, hp * 256 + r * P:hp * 256 + (r + 1) * P]
                        s = state[q, c, 2 * hp + r, :]
                        if c == 0:
                            ins = V.tensor_copy(s, kv)
                        else:
                            d = dec[q, 4 * hp + c:4 * hp + c + 1]
                            ins = V.scalar_tensor_tensor(s, state[q, c - 1, 2 * hp + r, :], d, kv,
                                                         ALU.mult, ALU.add)
                        if c < 2 or (hp, r) != (1, 1):
                            step(ins)
                        else:
                            ins.then_inc(state_ready, 1)
                settle()
            dve.wait_ge(lin_scores_done, 2)
            for r in range(2):
                V.copy_predicated(glasc[:, r, :, :, :].rearrange("p a b t -> p (a b) t"),
                                  spread(tri.bitcast(I32), 1, 4),
                                  ps[2 + r][:, :].rearrange("p (h t) -> p h t", h=4)).then_inc(lin_scores_ready, 1)

            def gated(layer, gain, c0):
                for tt in range(TT):
                    m = mix[:, tt, 0:512]
                    link(V.tensor_tensor(m, m, gain, ALU.mult)) if len(gain.shape) == 2 else \
                        link(V.tensor_tensor(m.rearrange("p (h c) -> p h c", h=4), m.rearrange("p (h c) -> p h c", h=4),
                                             gain, ALU.mult))
                    dve.wait_ge(silu_ready, TT * layer + tt + 1)
                    link(V.tensor_tensor(m, m, pr[:, tt, c0:c0 + 512], ALU.mult))

            dve.wait_ge(lin_sq_ready, 2)
            link(V.tensor_reduce(hss[:, 0:8], ws[:, 2048:3072].rearrange("p (h c) -> p h c", c=P), AX_X, ALU.add))
            rsqrt_mean(hrs[:, 0:8], hss[:, 0:8], P)
            for tt in range(TT):
                step(V.tensor_tensor(mix[:, tt, 0:512].rearrange("p (h c) -> p h c", h=4),
                                     ps[tt][:, :].rearrange("p (h c) -> p h c", h=4),
                                     spread(hrs[:, 4 * tt:4 * tt + 4], 2, P), ALU.mult))
            settle()
            gated(0, spread(row[:, R_GN:R_GN + P], 1, 4), GOUT)

            dve.wait_ge(trig_ready, 1)
            heads_norm(SQ, 10, [(R_SQ, 8), (R_SK, 2)], 0)
            attend(0)
            dve.wait_ge(pv_used, 1)
            link(V.tensor_copy(rden, rden))
            V.tensor_copy(sm[:, 400:401], mix[:, 0, 1023:1024]).then_inc(mix_ready, 1)
            attend(1)
            dve.wait_ge(pv_used, 2)
            V.tensor_copy(sm[:, 400:401], mix[:, 1, 1023:1024]).then_inc(mix_ready, 1)
            copy_mixT(0)
            dve.wait_ge(h_ready, 4)
            normalise(1)
            feed_forward(FFN_TILES, FFN_SLABS, FIRST, FIRST, 0, None)

            dve.wait_ge(y_added, 1)
            normalise(2)
            dve.wait_ge(proj_out, 12)
            qk = pr[:, :, RQ:RQ + 512].rearrange("p t (h c) -> p t h c", h=8)
            t = [ws[:, i * 512:(i + 1) * 512].rearrange("p (t h c) -> p t h c", t=TT, h=8) for i in range(4)]
            rotate(qk[:, :, :, 0:32], qk[:, :, :, 32:64], spread(trig[:, 1, 0:TT, 8:40], 2, 8),
                   spread(trig[:, 0, 0:TT, 8:40], 2, 8), t).then_inc(ret_rows_ready, 1)
            dve.wait_ge(lin_scores_done, 2 + 3)
            for i, d0 in enumerate((C_RD, C_RD, C_RO)):
                for r in range(2):
                    bank = ps[2 * (i // 2) + r][:, (i % 2) * 256:(i % 2 + 1) * 256]
                    V.tensor_tensor(retsc[:, i, :, :].rearrange("p (j r) q -> p r j q", r=2)[:, r, :, :],
                                    bank.rearrange("p (j q) -> p j q", j=2),
                                    con[:, d0:d0 + 512].rearrange("p (j r q) -> p r j q", j=2, r=2)[:, r, :, :],
                                    ALU.mult).then_inc(lin_scores_ready, 1)
            for tt in range(TT):
                dve.wait_ge(lin_out_done, 2 + tt + 1)
                step(V.tensor_reduce(hss[:, 4 * tt:4 * tt + 4], ps[6 + tt][:, :].rearrange("p (h c) -> p h c", h=4),
                                     AX_X, ALU.add))
            settle()
            link(V.tensor_scalar(hmu, hss[:, 0:8], 1.0 / P, None, ALU.mult))
            for tt in range(TT):
                m = mix[:, tt, 0:512].rearrange("p (h c) -> p h c", h=4)
                link(V.tensor_tensor(m, ps[6 + tt][:, :].rearrange("p (h c) -> p h c", h=4),
                                     spread(hmu[:, 4 * tt:4 * tt + 4], 2, P), ALU.subtract))
                link(V.tensor_tensor(linsq[:, tt, :], mix[:, tt, 0:512], mix[:, tt, 0:512], ALU.mult))
            link(V.tensor_reduce(hss[:, 0:8], ws[:, 2048:3072].rearrange("p (h c) -> p h c", c=P), AX_X, ALU.add))
            rsqrt_mean(hrs[:, 0:8], hss[:, 0:8], P)
            for tt in range(TT):
                m = mix[:, tt, 0:512].rearrange("p (h c) -> p h c", h=4)
                step(V.tensor_tensor(m, m, spread(hrs[:, 4 * tt:4 * tt + 4], 2, P), ALU.mult))
            settle()
            gated(1, row[:, R_RN:R_RN + 512], RG)

            heads_norm(NQ, 12, [(R_NQ, 8), (R_KS, 2), (R_KW, 2)], 1)
            dve.wait_ge(gates_ready, 1)
            link(V.tensor_scalar(gates, gates, 1.0, None, ALU.add))
            link(V.reciprocal(gates, gates))
            dve.wait_ge(head_T_ready, 7)
            link(V.memset(blk, 0.0))
            for i, v0 in enumerate((V_PK, V_PV)):
                dve.wait_ge(kcT_done, i + 1)
                for r in range(2):
                    for g in range(2):
                        for half in range(2):
                            src = ps[i][64 * g:64 * g + 64, 16 * half:16 * half + 240]\
                                .rearrange("p (n l r) -> p l n r", l=8, r=2)[:, :, :, r]
                            q = slice(64 * r, 64 * r + 64)
                            dst = blk[q, i, 8 * half:8 * half + 8, 32 * g:32 * g + NCMP]
                            pe_ = col[q, v0 + 8 * half:v0 + 8 * half + 8]
                            ins = V.tensor_tensor(dst, src, spread(pe_, 2, NCMP), ALU.add)
                            if (r, g, half) == (1, 1, 1):
                                ins.then_inc(blk_ready, 1)
                            else:
                                step(ins)
            for i, b0 in enumerate((V_B1K, V_B1V)):
                dve.wait_ge(hid_done, i + 1)
                step(V.tensor_tensor(hidx[:, i, :].rearrange("p (a c) -> p a c", a=2),
                                     ps[2 + i][:, 0:128].rearrange("p (a c) -> p a c", a=2),
                                     spread(col[:, b0:b0 + 2], 2, 64), ALU.add))
            settle()
            link(V.tensor_tensor(hid, hidx, hidx, ALU.mult))
            link(V.tensor_scalar(hid, hid, 0.044715, 1.0, ALU.mult, ALU.add))
            V.tensor_tensor(hide, hid, hidx, ALU.mult).then_inc(hid_x, 1)
            dve.wait_ge(hid_e, 1)
            link(V.tensor_scalar(hid, hide, 1.0, None, ALU.add))
            link(V.reciprocal(hid, hid))
            V.tensor_tensor(hid, hid, hidx, ALU.mult).then_inc(hid_ready, 1)
            dve.wait_ge(cmp_done, 1)
            link(V.tensor_tensor(cv[:, :, :], ps[4][0:64, 0:128].rearrange("p (i c) -> p i c", i=2),
                                 row[0:64, R_B2K:R_B2K + 128].rearrange("p (i c) -> p i c", i=2), ALU.add))
            ck = cv[:, 0, :]
            link(V.tensor_tensor(cktmp[:, 0:64], ck, ck, ALU.mult))
            link(V.tensor_reduce(ckss[:, 0:1], cktmp[:, 0:64], AX_X, ALU.add))
            rsqrt_mean(ckss[:, 1:2], ckss[:, 0:1], HD)
            link(V.scalar_tensor_tensor(ck, ck, ckss[:, 1:2], row[0:64, R_KC:R_KC + HD], ALU.mult, ALU.mult))
            t = [cktmp[:, i * 8:(i + 1) * 8] for i in range(4)]
            step(rotate(ck[:, 0:8], ck[:, 8:16], trig[0:64, 1, 2, 0:8], trig[0:64, 0, 2, 0:8], t))
            settle()
            V.tensor_copy(ckdup.rearrange("p (d c) -> p d c", d=2), spread(ck, 1, 2)).then_inc(ckv_ready, 1)
            dve.wait_ge(cs_done, 1)
            for tt in range(TT):
                s4 = csm[:, tt, 0:120].rearrange("p (x n) -> p x n", n=NCMP)
                for r in range(2):
                    src = ps[r][:, tt * 64:(tt + 1) * 64].rearrange("p (x n) -> p x n", n=16)[:, :, 0:NCMP]
                    step(V.tensor_tensor(s4[:, 4 * r:4 * r + 4, :], src,
                                         spread(con[:, C_CADD + NCMP * tt:C_CADD + NCMP * (tt + 1)], 1, 4), ALU.add))
                settle()
                link(V.tensor_reduce(cmx[:, tt, :], s4, AX_X, ALU.max))
                ins = V.tensor_tensor(s4, s4, spread(cmx[:, tt, :], 2, NCMP), ALU.subtract)
                if tt == 0:
                    step(ins)
                else:
                    ins.then_inc(cs_ready, 1)
            link(V.memset(cpd, 0.0))
            dve.wait_ge(ce_ready, 1)
            for tt in range(TT):
                s4 = csm[:, tt, 0:120].rearrange("p (x n) -> p x n", n=NCMP)
                step(V.tensor_reduce(cden[:, tt, :], s4, AX_X, ALU.add))
                dst = cpd[:, tt, :].rearrange("p (x n) -> p x n", n=32)[:, :, 0:NCMP]
                ins = V.tensor_tensor(dst, s4, spread(con[:, C_CONE + NCMP * tt:C_CONE + NCMP * (tt + 1)], 1, 8), ALU.mult)
                if tt == 0:
                    step(ins)
                else:
                    ins.then_inc(cp_ready, 1)
            settle()
            link(V.reciprocal(cden, cden))
            for tt in range(TT):
                gt = gates[:, tt, :].rearrange("p (g j r b) -> p g j r b", g=2, j=2, r=2)[:, :, :, :, 0]
                cd = cden[:, tt, :].rearrange("p (r j g) -> p g j r", r=2, j=2)
                link(V.tensor_tensor(wgt.rearrange("p (g j r) -> p g j r", g=2, j=2), cd, gt, ALU.mult))
                dve.wait_ge(cpv_done, 2)
                for g in range(2):
                    ins = V.tensor_tensor(mix[:, tt, 512 + 256 * g:768 + 256 * g].rearrange("p (h c) -> p h c", h=4),
                                          ps[4 + g][:, 256 * tt:256 * (tt + 1)].rearrange("p (h c) -> p h c", h=4),
                                          spread(wgt[:, 4 * g:4 * g + 4], 2, HD), ALU.mult)
                if tt == 0:
                    link(ins)
                else:
                    ins.then_inc(mix_ready, 1)
                    dve.wait_ge(mix_ready, 3)
            for n in range(2, 6):
                attend(n)
            copy_mixT(1)
            dve.wait_ge(h_ready, 8)
            normalise(3)
            dve.wait_ge(router_done, 1)
            link(V.tensor_tensor(logit, ps[0][:, 0:16].rearrange("p (t e) -> p t e", t=TT),
                                 spread(row[:, R_RB:R_RB + 8], 1, TT), ALU.add))
            for tt in range(TT):
                step(V.max(top[:, tt, :], logit[:, tt, :]))
            settle()
            for tt in range(TT):
                step(V.max_index(topi[:, tt, :], top[:, tt, :], logit[:, tt, :]))
            settle()
            step(V.tensor_copy(topf, topi))
            V.tensor_tensor(dtop, top[:, :, 1], top[:, :, 0], ALU.subtract).then_inc(dtop_ready, 1)
            dve.wait_ge(etop_ready, 1)
            settle()
            link(V.tensor_scalar(dsum, etop, 1.0, None, ALU.add))
            link(V.reciprocal(wtop[:, 0, :], dsum))
            link(V.tensor_tensor(wtop[:, 1, :], etop, wtop[:, 0, :], ALU.mult))
            for tt in range(TT):
                for k, dst in ((0, comb), (1, comb2)):
                    step(V.tensor_scalar(dst[:, tt, :], con[:, C_IOTA:C_IOTA + 8], topf[:, tt, k:k + 1],
                                         wtop[:, k, tt:tt + 1], ALU.is_equal, ALU.mult))
            settle()
            link(V.tensor_tensor(comb, comb, comb2, ALU.add))
            with dve.Fori(0, N_EXPERTS) as e:
                feed_forward(MOE_TILES, MOE_SLABS, e * MOE_TILES + FFN_TILES, e * MOE_SLABS + FFN_SLABS, e + 1,
                             lambda tt: comb[:, tt, bass.ds(e, 1)])

        @block.gpsimd
        def _(pool):
            nc.gpsimd.memset(glasc, 0.0).then_inc(pool_steps, 1)
            nc.gpsimd.memset(mhalf[:, :], -0.5).then_inc(mhalf_ready, 1)
            pool.wait_ge(mhalf_ready, 1)
            for n, v in enumerate((rstd[:, 0:2], hrs[:, 0:8], hrs[:, 0:20], rstd[:, 2:4],
                                   rstd[:, 4:6], hrs[:, 0:8], hrs[:, 0:24], ckss[:, 1:2], rstd[:, 6:8])):
                pool.wait_ge(mean_ready, n + 1)
                p, c = v.shape
                nc.gpsimd.tensor_tensor(v, v, mhalf[0:p, 0:c], ALU.pow).then_inc(rsqrt_ready, 1)
                if n == 0:
                    pool.wait_ge(gla_ops_ready, 1)
                    nc.gpsimd.memset(state, 0.0).then_inc(pool_steps, 1)


_WEIGHTS = ["w_in_e", "gla_gate_up", "w_out_e", "ffn_w_gate", "ffn_w_up", "ffn_w_down", "w_in_o",
            "cmp_w1_k", "cmp_w2_k", "cmp_w1_v", "cmp_w2_v", "w_out_o", "router_w",
            "exp_w_gate", "exp_w_up", "exp_w_down"]


def shape_constants():
    import numpy as np

    c = np.zeros((P, NC), np.float32)
    i = np.arange(P)
    c[:, C_ID:C_ID + P] = np.eye(P)
    chunk = i // 64
    same = chunk[:, None] == chunk[None, :]
    c[:, C_TRI:C_TRI + P] = same & (i[:, None] <= i[None, :])
    c[:, C_SAME:C_SAME + P] = same
    c[:, C_CH:C_CH + 2] = chunk[:, None] == np.arange(2)[None, :]
    for hh in range(4):
        lg = float(np.log(np.float32(1.0) - np.float32(2.0 ** (-5 - hh))))
        diff = i[None, :] - i[:, None]
        c[:, C_RD + hh * P:C_RD + (hh + 1) * P] = np.where(diff >= 0, np.exp(lg * np.maximum(diff, 0)), 0) * HD ** -0.5
        c[:, C_RO + hh * P:C_RO + (hh + 1) * P] = np.exp(lg * (diff + P)) * HD ** -0.5
    diag = np.where(i[None, :] <= i[:, None], 0.0, NEG)
    c[:, C_SWA:C_SWA + P] = np.where(i[None, :] > i[:, None], 0.0, NEG)
    c[:, C_SWA + P:C_SWA + T] = diag
    c[:, C_FULL + P:C_FULL + T] = diag
    end = np.arange(NCMP) * 16 + 31
    for tt in range(TT):
        ok = end[None, :] <= (tt * P + i)[:, None]
        c[:, C_CADD + NCMP * tt:C_CADD + NCMP * (tt + 1)] = np.where(ok, 0.0, NEG)
        c[:, C_CONE + NCMP * tt:C_CONE + NCMP * (tt + 1)] = ok
    f = np.arange(8, dtype=np.float32)
    c[:, C_INV:C_INV + 8] = np.float32(500000.0) ** (-f * np.float32(2.0) / np.float32(16))
    f = np.arange(32, dtype=np.float32)
    c[:, C_INV + 8:C_INV + 40] = np.float32(10000.0) ** (-f * np.float32(2.0) / np.float32(64))
    c[:, C_IOTA:C_IOTA + 8] = np.arange(8)
    return c


def kernel(**inputs):
    import numpy as np
    import concourse.bacc as bacc
    from concourse.bass_utils import run_bass_kernel_spmd

    a = {k: np.ascontiguousarray(v) for k, v in inputs.items()}
    rowv = np.concatenate([a[k].reshape(-1) for k in (
        "gla_gate_bias", "gla_out_norm", "swa_q_norm", "swa_k_norm", "ret_out_norm", "nsa_q_norm", "nsa_kc_norm",
        "nsa_ks_norm", "nsa_kw_norm", "cmp_b2_k", "cmp_b2_v", "swa_sinks", "router_b")])[None, :]
    colv = np.concatenate([a[k].reshape(-1, P).T for k in (
        "ln_mix_e", "ln_ffn_e", "ln_mix_o", "ln_ffn_o", "cmp_b1_k", "cmp_b1_v", "cmp_pos_k", "cmp_pos_v")], axis=1)
    assert rowv.shape[1] == NR and colv.shape[1] == NV
    token = a["positions"].reshape(-1)
    pos = np.zeros((P, 3), token.dtype)
    pos[:, 0], pos[:, 1] = token[:P], token[P:]
    for g in range(2):
        pos[32 * g:32 * g + NCMP, 2] = token[np.arange(NCMP) * 16 + 31]

    nc = bacc.Bacc("TRN2", target_bir_lowering=False, num_devices=1)
    arrays = {}

    def feed(name, arr):
        arr = np.ascontiguousarray(arr)
        arrays[name] = arr
        return nc.dram_tensor(name, arr.shape, mybir.dt.from_np(arr.dtype), kind="ExternalInput").ap()

    x = feed("x_dram", a["x"].reshape(T, D))
    p = feed("pos_dram", pos)
    c = feed("consts_dram", shape_constants())
    r = feed("rows_dram", rowv)
    v = feed("cols_dram", colv)
    w = {k: feed(k + "_dram", a[k]) for k in _WEIGHTS}
    w["out"] = nc.dram_tensor("out_dram", (T, D), F32, kind="ExternalOutput").ap()
    build(nc, x, p, c, r, v, w)
    res = run_bass_kernel_spmd(nc, [arrays], core_ids=[0])
    return res.results[0]["out_dram"].reshape(1, T, D)
```

```python
from contextlib import ExitStack

import concourse.bass as bass
from concourse import mybir

F32 = mybir.dt.float32
F32R = mybir.dt.float32r
BF16 = mybir.dt.bfloat16
I32 = mybir.dt.int32
U32 = mybir.dt.uint32
ALU = mybir.AluOpType
ACT = mybir.ActivationFunctionType
AX_X = mybir.AxisListType.X

P = 128
T = 256
TT = T // P
D = 1024
KC = D // P
HD = 64
EPS = 1e-6
SCALE = HD ** -0.5
NEG = -1e30

D_FF = 2816
N_EXPERTS = 8
D_FFE = 3584
TOP_K = 2

GQ, GK, GV, GLOW, GOUT, SQ, SK, SV, L0_IN = 0, 256, 512, 1024, 1040, 1552, 2064, 2192, 2320
RQ, RK, RV, RG, NQ, L1_IN = 0, 256, 512, 1024, 1536, 2840
KS_, KW_, KC_, VC_, VS_, VW_, NG_ = 2048, 2176, 2304, 2432, 2560, 2688, 2816

NCMP = 15
CMP_H = 256
SLAB = 512
RING = 7

C_ID, C_TRI, C_SAME, C_CH, C_RD, C_RO, C_SWA, C_FULL = 0, 128, 256, 384, 386, 898, 1410, 1666
C_CADD, C_CONE, C_INV, C_IOTA, NC = 1922, 1952, 1982, 2022, 2030
R_GB, R_GN, R_SQ, R_SK, R_RN, R_NQ, R_KC, R_KS, R_KW, R_B2K, R_B2V, R_SINK, R_RB, NR = (
    0, 256, 384, 448, 512, 1024, 1088, 1152, 1216, 1280, 1344, 1408, 1416, 1424)
V_LN, V_B1K, V_B1V, V_PK, V_PV, NV = 0, 32, 34, 36, 52, 68

TWO_PI = 6.283185307179586
PI2_A = 6.28125
PI2_B = 0.00193500518798828125
PI2_C = TWO_PI - PI2_A - PI2_B
ROUND = 12582912.0

L0_PROJ = 0
L0_OUT = L0_PROJ + 5
L0_FFN = L0_OUT + 2
FFN_SLABS = -(-D_FF // SLAB)
L1_PROJ = L0_FFN + 3 * FFN_SLABS
L1_CMP = L1_PROJ + 6
L1_OUT = L1_CMP + 2
MOE = L1_OUT + 2
MOE_SLABS = D_FFE // SLAB
MOE_SLOTS = 3 * MOE_SLABS
FFN_TILES = D_FF // P
MOE_TILES = D_FFE // P

CAP = 96
PARTS = -(-T // CAP)
MAX_MORE = TOP_K * T // CAP
NQ_MORE = (PARTS - 1) * N_EXPERTS
D_SU, D_ONE, D_IOTA = 0, P, 2 * P
D_THR = D_IOTA + CAP * PARTS
D_QE, D_QS, D_LOW = D_THR + 1, D_THR + 2, D_THR + 3
D_IK = D_LOW + NQ_MORE
ND = D_IK + MAX_MORE
assert ND <= 1024 and NQ_MORE <= 64
assert MOE % RING == 0 and MOE_SLOTS % RING == 0


def gate_slot(j):
    return 3 * j - 1 if j else 0


def up_slot(j):
    return gate_slot(j) + 1


def down_slot(j, slabs):
    return 3 * j + 4 if j < slabs - 1 else 3 * slabs - 1


def ffn_order(slabs):
    order = [None] * (3 * slabs)
    for j in range(slabs):
        order[gate_slot(j)] = ("gate", j)
        order[up_slot(j)] = ("up", j)
        order[down_slot(j, slabs)] = ("down", j)
    return order


def tiles_of(j, tiles):
    return range(4 * j, min(4 * j + 4, tiles))


def spread(ap, axis, n):
    v = ap.unsqueeze(axis)
    shape = list(v.shape)
    shape[axis] = n
    return v.to_broadcast(shape)


def build(nc, x, pos, consts, expert_consts, rowv, colv, w):
    with ExitStack() as ctx:
        def sb(name, shape, dt=F32):
            return ctx.enter_context(nc.sbuf_tensor(name, shape, dt))

        def sem(name):
            return ctx.enter_context(nc.semaphore(name))

        out = w["out"]
        ring = sb("ring", [P, RING, 4096])
        h = sb("h", [P, TT, D])
        xn = sb("xn", [P, TT, D])
        con = sb("con", [P, NC])
        row = sb("row", [P, NR])
        col = sb("col", [P, NV])
        arena = nc.sbuf_base
        pr = sb("pr", [P, TT, L1_IN])
        xT = sb("xT", [P, KC, T])
        qkT = sb("qkT", [P, 2048])
        ws = sb("ws", [P, 4096])
        arena_end = nc.sbuf_base
        gT = sb("gT", [16, T])
        gup = sb("gup", [16, 256])
        posi = sb("posi", [P, 3], I32)
        posf = sb("posf", [P, 3])
        trig = sb("trig", [P, 2, 3, 40])
        w2 = sb("w2", [P, 2, 2, HD])
        kcT = sb("kcT", [P, 64])
        cv = sb("cv", [64, 2, HD])
        rw = sb("rw", [P, KC, N_EXPERTS])
        mbf = sb("mbf", [P, 2, T], BF16)
        idb = sb("idb", [P, P], BF16)
        items = sb("items", [1, 3 * MAX_MORE], I32)
        mhalf = sb("mhalf", [P, 24])
        sm = sb("sm", [P, 512])
        ps = [ctx.enter_context(nc.psum_tensor(f"ps{i}", [P, 512], F32)) for i in range(8)]

        ident = con[:, C_ID:C_ID + P]
        tri = con[:, C_TRI:C_TRI + P]
        same = con[:, C_SAME:C_SAME + P]
        mix = xn
        mixT = xT

        room = [arena]

        def take(name, shape, dt=F32):
            at = -(-room[0] // 32) * 32
            n = 1
            for d in shape[1:]:
                n *= d
            room[0] = at + 4 * n
            assert room[0] <= arena_end
            return nc.alloc_sbuf_tensor_at(name, shape, dt, offset=at)

        whi = take("whi", [P, 4, 1024], F32R)
        wlo = take("wlo", [P, 4, 1024], F32R)
        xehi = take("xehi", [P, KC, CAP], F32R)
        xelo = take("xelo", [P, KC, CAP], F32R)
        ehhi = take("ehhi", [P, 4, CAP], F32R)
        ehlo = take("ehlo", [P, 4, CAP], F32R)
        both = -(-room[0] // 32) * 32
        egate = take("egate", [CAP, SLAB])
        ehrow = take("ehrow", [CAP, SLAB])
        osb = take("osb", [CAP, D])
        pick = take("pick", [P, TT, CAP])
        spreadw = take("spreadw", [P, TT, CAP])
        spreadwT = take("spreadwT", [CAP, T])
        pairs = take("pairs", [P, TT, NQ_MORE])
        chosen = take("chosen", [P, TT, 8])
        rank = take("rank", [P, TT, 8])
        active = take("active", [NQ_MORE, 1])
        slots = take("slots", [NQ_MORE, MAX_MORE])
        xe32 = nc.alloc_sbuf_tensor_at("xe32", [P, KC, CAP], F32, offset=both)
        assert KC * CAP <= 2 * SLAB

        ssq = sm[:, 0:8]
        rstd = sm[:, 8:16]
        hss = sm[:, 16:40]
        hrs = sm[:, 40:64]
        dec = sm[:, 64:72]
        amax = sm[:, 72:80]
        nmax = sm[:, 80:88]
        sinkd = sm[:, 88:96]
        esink = sm[:, 96:104]
        den = sm[:, 104:120].rearrange("p (t h) -> p t h", t=2)
        rden = sm[:, 120:128]
        wgt = sm[:, 128:136]
        gates = sm[:, 136:184].rearrange("p (t c) -> p t c", t=2)
        logit = sm[:, 184:200].rearrange("p (t e) -> p t e", t=2)
        top = sm[:, 200:216].rearrange("p (t e) -> p t e", t=2)
        topi = sm[:, 216:232].bitcast(U32).rearrange("p (t e) -> p t e", t=2)
        topf = sm[:, 232:248].rearrange("p (t e) -> p t e", t=2)
        dtop = sm[:, 248:250]
        etop = sm[:, 250:252]
        wtop = sm[:, 252:256].rearrange("p (k t) -> p k t", k=2)
        comb = sm[:, 256:272].rearrange("p (t e) -> p t e", t=2)
        comb2 = sm[:, 272:288].rearrange("p (t e) -> p t e", t=2)
        dsum = sm[:, 288:290]
        hmu = sm[:, 296:304]
        cden = sm[:, 304:320].rearrange("p (t h) -> p t h", t=2)
        cmx = sm[:, 320:336].rearrange("p (t h) -> p t h", t=2)
        ckss = sm[0:64, 336:338]

        x_in = sem("x_in")
        small_in = sem("small_in")
        late_in = sem("late_in")
        slot_full = [sem(f"slot_full{i}") for i in range(RING)]
        sumsq_ready = sem("sumsq_ready")
        xn_ready = sem("xn_ready")
        xnT_done = sem("xnT_done")
        xT_ready = sem("xT_ready")
        proj_done = sem("proj_done")
        proj_out = sem("proj_out")
        dve_steps = sem("dve_steps")
        act_steps = sem("act_steps")
        pool_steps = sem("pool_steps")
        mhalf_ready = sem("mhalf_ready")
        mean_ready = sem("mean_ready")
        rsqrt_ready = sem("rsqrt_ready")
        masks_ready = sem("masks_ready")
        gT_done = sem("gT_done")
        gT_ready = sem("gT_ready")
        z_done = sem("z_done")
        z_ready = sem("z_ready")
        softplus_ready = sem("softplus_ready")
        la_ready = sem("la_ready")
        cum_done = sem("cum_done")
        decay_ready = sem("decay_ready")
        dl_ready = sem("dl_ready")
        ebl_ready = sem("ebl_ready")
        gla_ops_ready = sem("gla_ops_ready")
        gla_T_done = sem("gla_T_done")
        gla_T_ready = sem("gla_T_ready")
        kv_done = sem("kv_done")
        state_ready = sem("state_ready")
        lin_scores_done = sem("lin_scores_done")
        lin_scores_ready = sem("lin_scores_ready")
        lin_out_done = sem("lin_out_done")
        lin_sq_ready = sem("lin_sq_ready")
        silu_ready = sem("silu_ready")
        head_sq_ready = sem("head_sq_ready")
        head_rows_ready = sem("head_rows_ready")
        dup_ready = sem("dup_ready")
        trig_ready = sem("trig_ready")
        angle_ready = sem("angle_ready")
        head_T_done = sem("head_T_done")
        head_T_ready = sem("head_T_ready")
        scores_done = sem("scores_done")
        nmax_ready = sem("nmax_ready")
        esink_ready = sem("esink_ready")
        probs_ready = sem("probs_ready")
        probsT_done = sem("probsT_done")
        probsT_act = sem("probsT_act")
        probsT_dve = sem("probsT_dve")
        pv_done = sem("pv_done")
        pv_used = sem("pv_used")
        mix_ready = sem("mix_ready")
        mixT_done = sem("mixT_done")
        mixT_ready = sem("mixT_ready")
        out_done = sem("out_done")
        h_ready = sem("h_ready")
        ret_rows_ready = sem("ret_rows_ready")
        ret_T_done = sem("ret_T_done")
        ret_T_ready = sem("ret_T_ready")
        kcT_done = sem("kcT_done")
        blk_ready = sem("blk_ready")
        hid_done = sem("hid_done")
        hid_x = sem("hid_x")
        hid_e = sem("hid_e")
        hid_ready = sem("hid_ready")
        cmp_done = sem("cmp_done")
        ckv_ready = sem("ckv_ready")
        cksq_ready = sem("cksq_ready")
        ckT_done = sem("ckT_done")
        ckT_ready = sem("ckT_ready")
        cs_done = sem("cs_done")
        cs_ready = sem("cs_ready")
        ce_ready = sem("ce_ready")
        cp_ready = sem("cp_ready")
        cpT_done = sem("cpT_done")
        cpT_ready = sem("cpT_ready")
        cpv_done = sem("cpv_done")
        gates_ready = sem("gates_ready")
        gate_up_done = sem("gate_up_done")
        silu_gate = sem("silu_gate")
        hidden_ready = sem("hidden_ready")
        down_done = sem("down_done")
        y_added = sem("y_added")
        router_done = sem("router_done")
        dtop_ready = sem("dtop_ready")
        etop_ready = sem("etop_ready")
        expert_consts_in = sem("expert_consts_in")
        chosen_ready = sem("chosen_ready")
        rank_done = sem("rank_done")
        pick_ready = sem("pick_ready")
        gather_done = sem("gather_done")
        whi_ready = sem("whi_ready")
        wlo_ready = sem("wlo_ready")
        quarter_used = sem("quarter_used")
        egate_ready = sem("egate_ready")
        ehrow_ready = sem("ehrow_ready")
        ehT_done = sem("ehT_done")
        ehhi_ready = sem("ehhi_ready")
        ehlo_ready = sem("ehlo_ready")
        xe32_ready = sem("xe32_ready")
        xehi_ready = sem("xehi_ready")
        xelo_ready = sem("xelo_ready")
        spreadw_ready = sem("spreadw_ready")
        spreadwT_done = sem("spreadwT_done")
        spreadwT_ready = sem("spreadwT_ready")
        o_ready = sem("o_ready")
        scatter_done = sem("scatter_done")
        y_used = sem("y_used")
        count_done = sem("count_done")
        active_ready = sem("active_ready")
        place_done = sem("place_done")
        slots_ready = sem("slots_ready")
        list_done = sem("list_done")
        list_ready = sem("list_ready")
        list_pairs_ready = sem("list_pairs_ready")
        moe_done = sem("moe_done")
        stored = sem("stored")

        block = ctx.enter_context(nc.Block())

        SMALL = 16 * 4

        def rows(ap):
            return ap.rearrange("(k p) n -> p k n", p=P)

        def slot3(n, k):
            return ring[:, n % RING, :].rearrange("p (k n) -> p k n", k=k)

        def item_of(eng, k):
            def read(n, top_):
                return eng.value_load(items[0:1, bass.ds(k + n * MAX_MORE, 1)], min_val=0, max_val=top_)
            return read(2, 1), read(0, N_EXPERTS - 1), read(1, CAP * (PARTS - 1))

        @block.sync
        def _(sp):
            def load(n, src):
                k, cols = src.shape[1], src.shape[2]
                dst = ring[:, n % RING, 0:k * cols].rearrange("p (k n) -> p k n", k=k)
                sp.dma_start(dst, src).then_inc(slot_full[n % RING], 16)

            def ffn_src(kind, j, wg, wu, wd, tiles):
                lo, hi = SLAB * j, min(SLAB * (j + 1), tiles * P)
                if kind == "down":
                    return rows(wd[lo:hi, :])
                return rows((wg if kind == "gate" else wu)[:, lo:hi])

            def wait_ffn_slot(order, r, tiles, gu0, dn0):
                kind, j = order[r]
                if kind == "down":
                    sp.wait_ge(down_done, dn0 + j + 1)
                else:
                    sp.wait_ge(gate_up_done, gu0 + min(4 * j + 4, tiles))

            def wait_free(n):
                m = n - RING
                if m < 0:
                    return
                if m < L0_OUT:
                    sp.wait_ge(proj_done, 2 * (m + 1))
                elif m < L0_FFN:
                    sp.wait_ge(out_done, 2 * (m - L0_OUT + 1))
                elif m < L1_PROJ:
                    wait_ffn_slot(ffn_order(FFN_SLABS), m - L0_FFN, FFN_TILES, 0, 0)
                elif m < L1_CMP:
                    sp.wait_ge(proj_done, 10 + 2 * (m - L1_PROJ + 1))
                elif m < L1_OUT:
                    sp.wait_ge(hid_done, m - L1_CMP + 1)
                else:
                    sp.wait_ge(out_done, 4 + 2 * (m - L1_OUT + 1))

            sp.dma_start(h[:, :, :], x.rearrange("(t p) n -> p t n", p=P)).then_inc(x_in, 16)
            sp.dma_start(con[:, :], consts).then_inc(small_in, 16)
            sp.dma_start(col[:, :], colv).then_inc(small_in, 16)
            sp.dma_start(row[:, :], rowv.partition_broadcast(P)).then_inc(small_in, 16)
            sp.dma_start(posi[:, :], pos).then_inc(small_in, 16)
            n = 0
            for s in range(5):
                wait_free(n)
                load(n, rows(w["w_in_e"][0, :, SLAB * s:min(SLAB * (s + 1), L0_IN)]))
                n += 1
            for s in range(2):
                wait_free(n)
                load(n, rows(w["w_out_e"][0, :, SLAB * s:SLAB * (s + 1)]))
                n += 1
            for kind, j in ffn_order(FFN_SLABS):
                wait_free(n)
                load(n, ffn_src(kind, j, w["ffn_w_gate"][0], w["ffn_w_up"][0], w["ffn_w_down"][0], FFN_TILES))
                n += 1
            for s in range(6):
                wait_free(n)
                load(n, rows(w["w_in_o"][0, :, SLAB * s:min(SLAB * (s + 1), L1_IN)]))
                n += 1
            for name in ("cmp_w1_k", "cmp_w1_v"):
                wait_free(n)
                load(n, rows(w[name][0]))
                n += 1
            for s in range(2):
                wait_free(n)
                load(n, rows(w["w_out_o"][0, :, SLAB * s:SLAB * (s + 1)]))
                n += 1

            order = ffn_order(MOE_SLABS)

            def load_expert(e, r):
                kind, j = order[r]
                name = {"gate": "exp_w_gate", "up": "exp_w_up", "down": "exp_w_down"}[kind]
                if kind == "down":
                    src = w[name][0, bass.ds(e, 1), SLAB * j:SLAB * (j + 1), :]
                else:
                    src = w[name][0, bass.ds(e, 1), :, SLAB * j:SLAB * (j + 1)]
                src = src.rearrange("a k n -> (a k) n")
                load(MOE + r, rows(src))

            for r in range(RING):
                wait_free(MOE + r)
                load_expert(0, r)

            def wait_split(i, r):
                sp.wait_ge(wlo_ready, i * 4 * MOE_SLOTS + 4 * (r + 1))

            def rest_of_expert(e):
                for r in range(RING, MOE_SLOTS):
                    wait_split(e, r - RING)
                    load_expert(e, r)

            with sp.Fori(0, N_EXPERTS - 1) as e:
                rest_of_expert(e)
                for r in range(RING):
                    wait_split(e, MOE_SLOTS - RING + r)
                    load_expert(e + 1, r)
            rest_of_expert(N_EXPERTS - 1)
            sp.wait_ge(y_used, TT * N_EXPERTS)
            sp.wait_ge(list_ready, 1)
            with sp.Fori(0, MAX_MORE) as k:
                used, e, _ = item_of(sp, k)
                i = k + N_EXPERTS
                with sp.If(used > 0):
                    for r in range(MOE_SLOTS):
                        wait_split(i - 1 if r < RING else i, (r - RING) % MOE_SLOTS)
                        load_expert(e, r)
            sp.wait_ge(moe_done, 1)
            sp.dma_start(out.rearrange("(t p) n -> p t n", p=P), h[:, :, :]).then_inc(stored, 16)
            sp.wait_ge(stored, 16)

        UNITS = [(tt, 1024, SV, 0, None) for tt in range(TT)]
        UNITS += [(tt, 1024, VS_, 1, 1) for tt in range(TT)]
        UNITS += [(tt, 1536, VW_, 1, 2) for tt in range(TT)]
        groups_before = [0]
        for u in UNITS:
            groups_before.append(groups_before[-1] + 2 * (u[0] + 1))
        probs = ws[:, 0:2048].rearrange("p (h k) -> p h k", h=8)
        probsT = ws[:, 2048:4096].rearrange("p (k h t) -> p k h t", k=2, h=8)
        qT = qkT[:, 0:1024].rearrange("p (j t) -> p j t", j=4)

        def head_of(bank, i, per):
            half = 4 // per
            return 2 * ((bank % half) * per + i) + bank // half

        la = ws[:, 0:512].rearrange("p (t c) -> p t c", t=TT)
        eb = ws[:, 512:1024].rearrange("p (t c) -> p t c", t=TT)
        enb = ws[:, 1024:1536].rearrange("p (t c) -> p t c", t=TT)
        ebl = ws[:, 1536:2048].rearrange("p (t c) -> p t c", t=TT)
        qin = ws[:, 2048:2560].rearrange("p (t c) -> p t c", t=TT)
        kin = ws[:, 2560:3072].rearrange("p (t c) -> p t c", t=TT)
        kst = ws[:, 3072:3584].rearrange("p (t c) -> p t c", t=TT)
        tmp = ws[:, 3584:4096].rearrange("p (t c) -> p t c", t=TT)
        state = ws[:, 0:1536].rearrange("p (c h v) -> p c h v", c=3, h=4)
        linqT = qkT[:, 0:512].rearrange("p (j t) -> p j t", j=2)
        linkT = qkT[:, 512:1024].rearrange("p (j t) -> p j t", j=2)
        glasc = qkT[:, 1024:2048].rearrange("p (r t j q) -> p r t j q", r=2, t=TT, j=2)
        retsc = ws[:, 0:1536].rearrange("p (b h q) -> p b h q", b=3, h=4)
        linsq = ws[:, 2048:3072].rearrange("p (t c) -> p t c", t=TT)
        headsq = ws[:, 0:1536]
        dup = ws[:, 1536:2560].rearrange("p (t g d c) -> p t g d c", t=TT, g=4, d=2)
        rtmp = ws[:, 2560:4096]
        blk = ws[:, 0:2048].rearrange("p (v l c) -> p v l c", v=2, l=16)
        hidx = ws[:, 2048:2304].rearrange("p (v c) -> p v c", v=2)
        hide = ws[:, 2304:2560].rearrange("p (v c) -> p v c", v=2)
        hid = ws[:, 2560:2816].rearrange("p (v c) -> p v c", v=2)
        ckdup = ws[0:64, 2816:2944]
        cktmp = ws[0:64, 2944:3072]
        csm = ws[:, 3072:3328].rearrange("p (t x) -> p t x", t=TT)
        cpd = ws[:, 3328:3840].rearrange("p (t x) -> p t x", t=TT)
        cpT = ws[0:64, 0:1024].rearrange("p (t j q) -> p t j q", t=TT, j=4)
        hT = ws[:, 0:2048].rearrange("p (i t) -> p i t", i=8)
        sg = ws[:, 2048:3072].rearrange("p (i t) -> p i t", i=4)
        econ = con[:, C_RD:C_RD + ND]

        @block.tensor
        def _(pe):
            mm = nc.tensor.matmul

            def slot_wait(n, e=None):
                k = 16 * (n // RING + 1)
                pe.wait_ge(slot_full[n % RING], k if e is None else e * (16 * MOE_SLOTS // RING) + k)

            def transpose_norm(k):
                for tt in range(TT):
                    pe.wait_ge(xn_ready, TT * k + tt + 1)
                    for b in range(2):
                        for c in range(4):
                            last = nc.tensor.transpose(ps[4 + 2 * tt + b][:, c * P:(c + 1) * P],
                                                       xn[:, tt, (4 * b + c) * P:(4 * b + c + 1) * P], ident)
                        last.then_inc(xnT_done, 1)

            def project(first, widths, unit0, done, used):
                u = unit0
                for s, width in enumerate(widths):
                    slot_wait(first + s)
                    wt = ring[:, (first + s) % RING, 0:KC * width].rearrange("p (k n) -> p k n", k=KC)
                    for tt in range(TT):
                        if u - unit0 >= 4:
                            pe.wait_ge(used, u - 3)
                        for k in range(KC):
                            last = mm(ps[u % 4][:, 0:width], xT[:, k, tt * P:(tt + 1) * P], wt[:, k, :],
                                      start=(k == 0), stop=(k == KC - 1))
                        last.then_inc(done, 1)
                        u += 1

            def out_projection(layer):
                for tt in range(TT):
                    pe.wait_ge(mix_ready, 3 * layer + tt + 1)
                    for b in range(2):
                        for c in range(4):
                            last = nc.tensor.transpose(ps[4 + 2 * tt + b][:, c * P:(c + 1) * P],
                                                       mix[:, tt, (4 * b + c) * P:(4 * b + c + 1) * P], ident)
                        last.then_inc(mixT_done, 1)
                pe.wait_ge(mixT_ready, 4 * (layer + 1))
                project(L0_OUT if layer == 0 else L1_OUT, [SLAB, SLAB], 4 * layer, out_done, h_ready)

            def attend(n):
                tt, k0, v0, mask, _ = UNITS[n]
                kT = qkT[:, k0:k0 + 512].rearrange("p (g t) -> p g t", g=2)
                keys = P * (tt + 1)
                per = 512 // keys
                for b in range(8 // per):
                    bank = ps[b][:, :].rearrange("p (h k) -> p h k", h=per)
                    m = mbf[:, mask, T - keys:T]
                    mm(bank, idb[:, :], spread(m, 1, per), start=True, stop=False)
                    for i in range(per):
                        hh = head_of(b, i, per)
                        r = 64 * (hh % 2)
                        last = mm(bank[:, i, :], qT[r:r + 64, hh // 2, tt * P:(tt + 1) * P],
                                  kT[r:r + 64, hh // 4, 0:keys], start=False, stop=(i == per - 1))
                last.then_inc(scores_done, 1)
                pe.wait_ge(probs_ready, n + 1)
                g = groups_before[n]
                for kt in range(tt + 1):
                    for quad in range(2):
                        if g >= 2:
                            pe.wait_ge(probsT_act if g % 2 == 0 else probsT_dve, g // 2)
                        for i in range(4):
                            last = nc.tensor.transpose(ps[4 + g % 2][:, i * P:(i + 1) * P],
                                                       probs[:, 4 * quad + i, kt * P:(kt + 1) * P], ident)
                        last.then_inc(probsT_done, 1)
                        g += 1
                pe.wait_ge(probsT_act, g // 2)
                pe.wait_ge(probsT_dve, g // 2)
                if n:
                    pe.wait_ge(pv_used, n)
                for hh in range(8):
                    for kt in range(tt + 1):
                        c = v0 + HD * (hh // 4)
                        last = mm(ps[6][:, hh * HD:(hh + 1) * HD], probsT[:, kt, hh, :],
                                  pr[:, kt, c:c + HD], start=(kt == 0), stop=(kt == tt))
                last.then_inc(pv_done, 1)

            def feed_forward(first=L0_FFN, slabs=FFN_SLABS, tiles=FFN_TILES):
                def down(j):
                    pe.wait_ge(hidden_ready, min(4 * j + 4, tiles))
                    slot_wait(first + down_slot(j, slabs))
                    wd = slot3(first + down_slot(j, slabs), 4)
                    for i in tiles_of(j, tiles):
                        for tt in range(TT):
                            for half in range(2):
                                last = mm(ps[4 + 2 * tt + half][:, :], hT[:, i % 8, tt * P:(tt + 1) * P],
                                          wd[:, i % 4, half * 512:(half + 1) * 512],
                                          start=(i == 0), stop=(i == tiles - 1))
                    last.then_inc(down_done, 1)

                for j in range(slabs):
                    slot_wait(first + gate_slot(j))
                    slot_wait(first + up_slot(j))
                    width = P * len(tiles_of(j, tiles))
                    wg, wu = (ring[:, (first + f(j)) % RING, 0:KC * width].rearrange("p (k n) -> p k n", k=KC)
                              for f in (gate_slot, up_slot))
                    for i in tiles_of(j, tiles):
                        if i >= 4:
                            pe.wait_ge(hidden_ready, i - 3)
                        c = (i % 4) * P
                        for k in range(KC):
                            mm(ps[i % 4][:, 0:T], wg[:, k, c:c + P], xT[:, k, :], start=(k == 0), stop=(k == KC - 1))
                        for k in range(KC):
                            last = mm(ps[i % 4][:, T:2 * T], wu[:, k, c:c + P], xT[:, k, :],
                                      start=(k == 0), stop=(k == KC - 1))
                        last.then_inc(gate_up_done, 1)
                    if j:
                        down(j - 1)
                down(slabs - 1)

            def linear_scores(banks, at, q_tt, k_tt):
                for hh in range(4):
                    r = 64 * (hh % 2)
                    c = (2 * at + hh // 2) * P
                    last = mm(banks[hh % 2][:, c:c + P], linkT[r:r + 64, hh // 2, k_tt * P:(k_tt + 1) * P],
                              linqT[r:r + 64, hh // 2, q_tt * P:(q_tt + 1) * P], start=True, stop=True)
                last.then_inc(lin_scores_done, 1)

            pe.wait_ge(small_in, SMALL)
            transpose_norm(0)
            pe.wait_ge(xT_ready, 4)
            project(L0_PROJ, [SLAB] * 4 + [L0_IN - 4 * SLAB], 0, proj_done, proj_out)
            pe.wait_ge(proj_out, 6)
            for tt in range(TT):
                last = nc.tensor.transpose(ps[4][0:16, tt * P:(tt + 1) * P], pr[:, tt, GLOW:GLOW + 16], ident)
            last.then_inc(gT_done, 1)
            pe.wait_ge(gT_ready, 1)
            pe.wait_ge(late_in, 64)
            for tt in range(TT):
                last = mm(ps[5][:, tt * 256:(tt + 1) * 256], gT[:, tt * P:(tt + 1) * P], gup[:, :],
                          start=True, stop=True)
            last.then_inc(z_done, 1)
            pe.wait_ge(la_ready, 1)
            for tt in range(TT):
                mm(ps[6][:, tt * 256:(tt + 1) * 256], tri, la[:, tt, :], start=True, stop=True)
                mm(ps[7][:, tt * 256:(tt + 1) * 256], same, la[:, tt, :], start=True, stop=True)
                for hp in range(2):
                    c = 4 * hp + 2 * tt
                    last = mm(ps[4][:, c:c + 2], la[:, tt, hp * P:(hp + 1) * P], con[:, C_CH:C_CH + 2],
                              start=True, stop=True)
            last.then_inc(cum_done, 1)
            pe.wait_ge(gla_ops_ready, 1)
            pe.wait_ge(proj_out, 10)
            for src, bank in ((qin, ps[0]), (kin, ps[1])):
                for hp in range(2):
                    for tt in range(TT):
                        c = (2 * hp + tt) * P
                        last = nc.tensor.transpose(bank[:, c:c + P], src[:, tt, hp * P:(hp + 1) * P], ident)
                last.then_inc(gla_T_done, 1)
            for c in range(3):
                r = 64 * (c % 2)
                for hp in range(2):
                    last = mm(ps[5 + c][:, hp * 256:(hp + 1) * 256], kst[r:r + 64, c // 2, hp * P:(hp + 1) * P],
                              pr[r:r + 64, c // 2, GV + hp * 256:GV + (hp + 1) * 256], start=True, stop=True)
            last.then_inc(kv_done, 1)
            pe.wait_ge(gla_T_ready, 2)
            for tt in range(TT):
                linear_scores(ps[2:4], tt, tt, tt)
            pe.wait_ge(state_ready, 1)
            pe.wait_ge(lin_scores_ready, 2)
            for tt in range(TT):
                for hh in range(4):
                    for c in range(2 * tt, 2 * tt + 2):
                        t0 = 64 * (c % 2)
                        o = ps[tt][t0:t0 + 64, hh * P:(hh + 1) * P]
                        last = mm(o, glasc[:, hh % 2, tt, hh // 2, t0:t0 + 64],
                                  pr[:, tt, GV + hh * P:GV + (hh + 1) * P], start=True, stop=(c == 0))
                        if c:
                            last = mm(o, linqT[:, hh // 2, c * 64:(c + 1) * 64], state[:, c - 1, hh, :],
                                      start=False, stop=True)
                last.then_inc(lin_out_done, 1)

            def head_transposes(n_q, n_k, done0):
                for j in range(n_q):
                    for tt in range(TT):
                        c = (2 * (j % 2) + tt) * P
                        last = nc.tensor.transpose(ps[2 + j // 2][:, c:c + P],
                                                   pr[:, tt, done0 + j * P:done0 + (j + 1) * P], ident)
                    if j % 2:
                        last.then_inc(head_T_done, 1)

            def dup_transposes(n_k):
                for g in range(n_k):
                    for tt in range(TT):
                        c = (2 * (g % 2) + tt) * P
                        src = dup[:, tt, g, :, :].rearrange("p d c -> p (d c)")
                        last = nc.tensor.transpose(ps[4 + g // 2][:, c:c + P], src, ident)
                    if g % 2:
                        last.then_inc(head_T_done, 1)

            pe.wait_ge(head_rows_ready, 1)
            pe.wait_ge(dup_ready, 1)
            head_transposes(4, 2, SQ)
            dup_transposes(2)
            pe.wait_ge(head_T_ready, 3)
            pe.wait_ge(masks_ready, 3)
            for n in range(2):
                attend(n)
            out_projection(0)
            transpose_norm(1)
            pe.wait_ge(xT_ready, 8)
            feed_forward()

            transpose_norm(2)
            pe.wait_ge(xT_ready, 12)
            project(L1_PROJ, [SLAB] * 5 + [L1_IN - 5 * SLAB], 10, proj_done, proj_out)
            pe.wait_ge(ret_rows_ready, 1)
            for i, bank in ((0, ps[4]), (1, ps[5])):
                for hp in range(2):
                    for tt in range(TT):
                        c = (2 * hp + tt) * P
                        src = pr[:, tt, RQ + 256 * i + hp * P:RQ + 256 * i + (hp + 1) * P]
                        last = nc.tensor.transpose(bank[:, c:c + P], src, ident)
                last.then_inc(ret_T_done, 1)
            pe.wait_ge(ret_T_ready, 2)
            pe.wait_ge(proj_out, 22)
            linear_scores(ps[0:2], 0, 0, 0)
            linear_scores(ps[0:2], 1, 1, 1)
            linear_scores(ps[2:4], 0, 1, 0)
            pe.wait_ge(lin_scores_ready, 2 + 6)
            for tt in range(TT):
                for hh in range(4):
                    blocks = [(0, 0)] if tt == 0 else [(1, 1), (2, 0)]
                    for n, (b, kt) in enumerate(blocks):
                        last = mm(ps[6 + tt][:, hh * P:(hh + 1) * P], retsc[:, b, hh, :],
                                  pr[:, kt, RV + hh * P:RV + (hh + 1) * P], start=(n == 0), stop=(n == tt))
                last.then_inc(lin_out_done, 1)
            pe.wait_ge(head_rows_ready, 2)
            pe.wait_ge(dup_ready, 2)
            head_transposes(4, 4, NQ)
            dup_transposes(4)
            pe.wait_ge(head_T_ready, 7)
            for i in range(2):
                for tt in range(TT):
                    last = nc.tensor.transpose(ps[i][:, tt * P:(tt + 1) * P],
                                               pr[:, tt, KC_ + i * P:KC_ + (i + 1) * P], ident)
                last.then_inc(kcT_done, 1)
            for i in range(2):
                pe.wait_ge(blk_ready, i + 1)
                slot_wait(L1_CMP + i)
                w1 = slot3(L1_CMP + i, 16)
                for ht in range(2):
                    for l in range(16):
                        last = mm(ps[2 + i][:, ht * 64:(ht + 1) * 64], w1[:, l, ht * P:(ht + 1) * P],
                                  blk[:, i, l, :], start=(l == 0), stop=(l == 15))
                last.then_inc(hid_done, 1)
            pe.wait_ge(hid_ready, 1)
            for i in range(2):
                for ht in range(2):
                    last = mm(ps[4][0:64, i * HD:(i + 1) * HD], hid[:, i, ht * 64:(ht + 1) * 64], w2[:, i, ht, :],
                              start=(ht == 0), stop=(ht == 1))
            last.then_inc(cmp_done, 1)
            pe.wait_ge(ckv_ready, 1)
            nc.tensor.transpose(ps[5][:, 0:64], ckdup, ident[0:64, 0:64]).then_inc(ckT_done, 1)
            pe.wait_ge(ckT_ready, 1)
            for tt in range(TT):
                for hh in range(8):
                    r, g = 64 * (hh % 2), hh // 4
                    c = 64 * tt + (hh % 4 // 2 * 2 + g) * 16
                    last = mm(ps[hh % 2][:, c:c + NCMP], qT[r:r + 64, hh // 2, tt * P:(tt + 1) * P],
                              kcT[r:r + 64, 32 * g:32 * g + NCMP], start=True, stop=True)
            last.then_inc(cs_done, 1)
            pe.wait_ge(cp_ready, 1)
            for tt in range(TT):
                for j in range(4):
                    last = nc.tensor.transpose(ps[2 + tt][0:64, j * P:(j + 1) * P], cpd[:, tt, j * 64:(j + 1) * 64],
                                               ident)
                last.then_inc(cpT_done, 1)
            pe.wait_ge(cpT_ready, 2)
            for tt in range(TT):
                for hh in range(8):
                    g, j = hh // 4, 2 * (hh % 2) + hh % 4 // 2
                    c = 256 * tt + (hh % 4) * HD
                    last = mm(ps[4 + g][:, c:c + HD], cpT[32 * g:32 * g + 32, tt, j, :],
                              cv[32 * g:32 * g + 32, 1, :], start=True, stop=True)
                last.then_inc(cpv_done, 1)
            pe.wait_ge(mix_ready, 3)
            for n in range(2, 6):
                attend(n)
            out_projection(1)
            transpose_norm(3)
            pe.wait_ge(xT_ready, 16)
            for tt in range(TT):
                for k in range(KC):
                    last = mm(ps[0][:, tt * 8:(tt + 1) * 8], xT[:, k, tt * P:(tt + 1) * P], rw[:, k, :],
                              start=(k == 0), stop=(k == KC - 1))
            last.then_inc(router_done, 1)
            pe.wait_ge(expert_consts_in, 16)
            pe.wait_ge(chosen_ready, 1)
            mm(ps[1][:, 0:8], econ[:, D_SU:D_SU + P], chosen[:, 0, :], start=True, stop=True)
            mm(ps[1][:, 8:16], econ[:, D_SU:D_SU + P], chosen[:, 1, :], start=True, stop=False)
            mm(ps[1][:, 8:16], econ[:, D_ONE:D_ONE + P], chosen[:, 0, :], start=False, stop=True).then_inc(rank_done, 1)

            def gather(i, added):
                pe.wait_ge(pick_ready, i + 1)
                if added is not None:
                    pe.wait_ge(y_used, added)
                for c in range(KC):
                    for tt in range(TT):
                        last = mm(ps[4 + c // 4][:, c % 4 * CAP:(c % 4 + 1) * CAP], xn[:, tt, c * P:(c + 1) * P],
                                  pick[:, tt, :], start=(tt == 0), stop=(tt == 1))
                last.then_inc(gather_done, 1)

            def scatter(i):
                pe.wait_ge(o_ready, 2 * i + 2)
                pe.wait_ge(spreadwT_ready, i + 1)
                for tt in range(TT):
                    for half in range(2):
                        last = mm(ps[6 - 2 * tt + half][:, :], spreadwT[:, tt * P:(tt + 1) * P],
                                  osb[:, half * 512:(half + 1) * 512], start=True, stop=True)
                    last.then_inc(scatter_done, 1)

            def expert(i, scatter_before, gather_next, more):
                q0 = i * 4 * MOE_SLOTS

                def product(bank, hi, lo, q, n, start, stop):
                    cols = slice(n * 512, (n + 1) * 512)
                    mm(bank, hi, whi[:, q, cols], start=start, stop=False)
                    mm(bank, lo, whi[:, q, cols], start=False, stop=False)
                    return mm(bank, hi, wlo[:, q, cols], start=False, stop=stop)

                def gate_or_up(r, bank):
                    for q in range(4):
                        pe.wait_ge(wlo_ready, q0 + (4 * r + q + 1))
                        for n in range(2):
                            k = 2 * q + n
                            last = product(bank[0:CAP, :], xehi[:, k, :], xelo[:, k, :], q, n, k == 0, k == KC - 1)
                        last.then_inc(quarter_used, 1)

                def turn_hidden(j):
                    pe.wait_ge(ehrow_ready, i * MOE_SLABS + j + 1)
                    for f in range(4):
                        last = nc.tensor.transpose(ps[7][:, f * CAP:(f + 1) * CAP], ehrow[:, f * P:(f + 1) * P],
                                                   ident[0:CAP, 0:CAP])
                    last.then_inc(ehT_done, 1)

                def down(j):
                    r = down_slot(j, MOE_SLABS)
                    pe.wait_ge(ehlo_ready, i * MOE_SLABS + j + 1)
                    for f in range(4):
                        pe.wait_ge(wlo_ready, q0 + (4 * r + f + 1))
                        for half in range(2):
                            last = product(ps[2 + half][0:CAP, :], ehhi[:, f, :], ehlo[:, f, :], f, half,
                                           (j, f) == (0, 0), (j, f) == (MOE_SLABS - 1, 3))
                        last.then_inc(quarter_used, 1)

                pe.wait_ge(xelo_ready, i + 1)
                for j in range(MOE_SLABS):
                    if j:
                        pe.wait_ge(egate_ready, i * MOE_SLABS + j)
                    gate_or_up(gate_slot(j), ps[0])
                    if j:
                        turn_hidden(j - 1)
                    gate_or_up(up_slot(j), ps[1])
                    if j == 0 and scatter_before:
                        scatter(i - 1)
                        pe.wait_ge(y_used, i * 2)
                    if j == 0 and more:
                        pe.wait_ge(y_used, i * 2)
                    if j == 3:
                        pe.wait_ge(spreadw_ready, i + 1)
                        for tt in range(TT):
                            last = nc.tensor.transpose(ps[6][0:CAP, tt * P:(tt + 1) * P], spreadw[:, tt, :], ident)
                        last.then_inc(spreadwT_done, 1)
                    if j == 1 and (scatter_before or more):
                        pe.wait_ge(o_ready, i * 2)
                    if j:
                        down(j - 1)
                turn_hidden(MOE_SLABS - 1)
                if gather_next:
                    gather(i + 1, None)
                down(MOE_SLABS - 1)

            gather(0, None)
            expert(0, False, True, False)
            pe.wait_ge(list_pairs_ready, 1)
            for tt in range(TT):
                last = mm(ps[7][0:NQ_MORE, 0:1], pairs[:, tt, :], econ[:, D_ONE:D_ONE + 1], start=(tt == 0), stop=(tt == 1))
            last.then_inc(count_done, 1)
            pe.wait_ge(active_ready, 1)
            mm(ps[7][0:NQ_MORE, 1:2], econ[0:NQ_MORE, D_LOW:D_LOW + NQ_MORE], active[:, :], start=True,
               stop=True).then_inc(place_done, 1)
            pe.wait_ge(slots_ready, 1)
            for n, c in enumerate((D_QE, D_QS, D_ONE)):
                last = mm(ps[7][0:1, 16 + n * MAX_MORE:16 + (n + 1) * MAX_MORE], econ[0:NQ_MORE, c:c + 1], slots[:, :],
                          start=True, stop=True)
            last.then_inc(list_done, 1)
            pe.wait_ge(list_ready, 1)
            with pe.Fori(1, N_EXPERTS - 1) as i:
                expert(i, True, True, False)
            expert(N_EXPERTS - 1, True, False, False)
            scatter(N_EXPERTS - 1)
            with pe.Fori(0, MAX_MORE) as k:
                used, _, _ = item_of(pe, k)
                with pe.If(used > 0):
                    i = k + N_EXPERTS
                    gather(i, i * 2)
                    expert(i, False, False, True)
                    scatter(i)

        @block.scalar
        def _(act):
            A = nc.scalar.activation
            steps = [0]

            def step(ins):
                steps[0] += 1
                ins.then_inc(act_steps, 1)

            def settle():
                act.wait_ge(act_steps, steps[0])

            act.wait_ge(x_in, 16)
            act.dma_start(gup[:, :], w["gla_gate_up"][0]).then_inc(late_in, 16)
            act.dma_start(w2[:, 0, :, :], rows(w["cmp_w2_k"][0])).then_inc(late_in, 16)
            act.dma_start(w2[:, 1, :, :], rows(w["cmp_w2_v"][0])).then_inc(late_in, 16)
            act.dma_start(rw[:, :, :], rows(w["router_w"][0])).then_inc(late_in, 16)

            def sums_of_squares(k):
                for tt in range(TT):
                    c = TT * k + tt
                    A(xn[:, tt, :], h[:, tt, :], ACT.Square, accum_out=ssq[:, c:c + 1]).then_inc(sumsq_ready, 1)

            def copy_projection(units, pieces):
                for u, (tt, parts) in zip(units, pieces):
                    act.wait_ge(proj_done, u + 1)
                    for n, (src, dst, width) in enumerate(parts):
                        ins = A(pr[:, tt, dst:dst + width], ps[u % 4][:, src:src + width], ACT.Copy)
                        if n == len(parts) - 1:
                            ins.then_inc(proj_out, 1)

            def attend(n):
                tt = UNITS[n][0]
                keys = P * (tt + 1)
                per = 512 // keys
                act.wait_ge(nmax_ready, n + 1)
                if n:
                    act.wait_ge(probsT_done, groups_before[n])
                for b in range(8 // per):
                    for i in range(per):
                        hh = head_of(b, i, per)
                        ins = A(probs[:, hh, 0:keys], ps[b][:, i * keys:(i + 1) * keys], ACT.Exp,
                                bias=nmax[:, hh:hh + 1], scale=SCALE, accum_out=den[:, tt, hh:hh + 1])
                ins.then_inc(probs_ready, 1)
                if UNITS[n][4] is None:
                    A(esink, sinkd, ACT.Exp).then_inc(esink_ready, 1)
                for g in range(groups_before[n], groups_before[n + 1], 2):
                    kt = (g - groups_before[n]) // 2
                    act.wait_ge(probsT_done, g + 1)
                    if n:
                        act.wait_ge(pv_done, n)
                    A(probsT[:, kt, 0:4, :], ps[4][:, :].rearrange("p (h t) -> p h t", h=4),
                      ACT.Copy).then_inc(probsT_act, 1)

            def feed_forward():
                for i in range(FFN_TILES):
                    act.wait_ge(gate_up_done, i + 1)
                    if i >= 4:
                        act.wait_ge(hidden_ready, i - 3)
                    A(sg[:, i % 4, :], ps[i % 4][:, 0:T], ACT.Silu).then_inc(silu_gate, 1)

            act.wait_ge(x_in, 16)
            sums_of_squares(0)
            act.wait_ge(small_in, SMALL)
            for m, c0 in enumerate((C_SWA, C_FULL)):
                A(mbf[:, m, :], con[:, c0:c0 + T], ACT.Copy).then_inc(masks_ready, 1)
            A(idb[:, :], ident, ACT.Copy).then_inc(masks_ready, 1)
            act.wait_ge(angle_ready, 1)
            A(trig[:, :, :, :], trig[:, :, :, :], ACT.Sin).then_inc(trig_ready, 1)
            copy_projection(range(10), [(u % 2, [(0, SLAB * (u // 2), min(SLAB, L0_IN - SLAB * (u // 2)))])
                                        for u in range(10)])
            act.wait_ge(z_ready, 1)
            step(A(tmp[:, :, :], eb[:, :, :], ACT.Exp, scale=-1.0))
            settle()
            A(tmp[:, :, :], tmp[:, :, :], ACT.Ln, bias=1.0).then_inc(softplus_ready, 1)
            act.wait_ge(cum_done, 1)
            act.wait_ge(dl_ready, 1)
            cum = ps[6][:, :].rearrange("p (t c) -> p t c", t=TT)
            A(eb[:, :, :], cum, ACT.Exp, scale=1.0 / 16)
            A(enb[:, :, :], cum, ACT.Exp, scale=-1.0 / 16)
            A(dec, ps[4][:, 0:8], ACT.Exp, scale=1.0 / 16).then_inc(decay_ready, 1)
            A(ebl[:, :, :], tmp[:, :, :], ACT.Exp, scale=1.0 / 16).then_inc(ebl_ready, 1)
            for i, dst in enumerate((linqT, linkT)):
                act.wait_ge(gla_T_done, i + 1)
                A(dst[:, :, :], ps[i][:, :].rearrange("p (j t) -> p j t", j=2), ACT.Copy).then_inc(gla_T_ready, 1)
            for tt in range(TT):
                act.wait_ge(lin_out_done, tt + 1)
                A(linsq[:, tt, :], ps[tt][:, :], ACT.Square).then_inc(lin_sq_ready, 1)
            for tt in range(TT):
                A(pr[:, tt, GOUT:GOUT + 512], pr[:, tt, GOUT:GOUT + 512], ACT.Silu).then_inc(silu_ready, 1)

            def head_squares(c0, heads, n):
                v = headsq[:, 0:TT * heads * HD].rearrange("p (t c) -> p t c", t=TT)
                A(v, pr[:, :, c0:c0 + heads * HD], ACT.Square).then_inc(head_sq_ready, 1)

            def head_copies(first, banks):
                for i, (b, c) in enumerate(banks):
                    act.wait_ge(head_T_done, first + i + 1)
                    A(qkT[:, c:c + 512], ps[b][:, :], ACT.Copy).then_inc(head_T_ready, 1)

            head_squares(SQ, 10, 0)
            act.wait_ge(head_rows_ready, 1)
            for d in range(2):
                ins = A(dup[:, :, 0:2, d, :], pr[:, :, SK:SK + 128].rearrange("p t (g c) -> p t g c", g=2), ACT.Copy)
            ins.then_inc(dup_ready, 1)
            head_copies(0, [(2, 0), (3, 512), (4, 1024)])
            for n in range(2):
                attend(n)
            act.wait_ge(h_ready, 4)
            sums_of_squares(1)
            feed_forward()

            act.wait_ge(y_added, 1)
            sums_of_squares(2)
            pieces = [(u % 2, [(0, SLAB * (u // 2), SLAB)]) for u in range(8)]
            pieces += [(tt, [(0, KC_, 256), (256, KS_, 128), (384, VS_, 128)]) for tt in range(TT)]
            pieces += [(tt, [(0, KW_, 128), (128, VW_, 152)]) for tt in range(TT)]
            copy_projection(range(10, 22), pieces)
            for i, dst in enumerate((linqT, linkT)):
                act.wait_ge(ret_T_done, i + 1)
                A(dst[:, :, :], ps[4 + i][:, :].rearrange("p (j t) -> p j t", j=2), ACT.Copy).then_inc(ret_T_ready, 1)
            for tt in range(TT):
                A(pr[:, tt, RG:RG + 512], pr[:, tt, RG:RG + 512], ACT.Silu).then_inc(silu_ready, 1)
            act.wait_ge(proj_out, 22)
            A(gates[:, :, :], pr[:, :, NG_:NG_ + 24], ACT.Exp, scale=-1.0).then_inc(gates_ready, 1)
            act.wait_ge(lin_out_done, 4)
            act.wait_ge(lin_scores_ready, 8)
            act.dma_start(econ, expert_consts).then_inc(expert_consts_in, 16)
            head_squares(NQ, 12, 1)
            act.wait_ge(head_rows_ready, 2)
            for d in range(2):
                ins = A(dup[:, :, :, d, :], pr[:, :, KS_:KS_ + 256].rearrange("p t (g c) -> p t g c", g=4), ACT.Copy)
            ins.then_inc(dup_ready, 1)
            head_copies(3, [(2, 0), (3, 512), (4, 1024), (5, 1536)])
            act.wait_ge(hid_x, 1)
            A(hide[:, :, :], hide[:, :, :], ACT.Exp, scale=-2 * 0.7978845608028654).then_inc(hid_e, 1)
            act.wait_ge(ckT_done, 1)
            A(kcT[:, :], ps[5][:, 0:64], ACT.Copy).then_inc(ckT_ready, 1)
            act.wait_ge(cs_ready, 1)
            A(csm[:, :, 0:120], csm[:, :, 0:120], ACT.Exp, scale=SCALE).then_inc(ce_ready, 1)
            for tt in range(TT):
                act.wait_ge(cpT_done, tt + 1)
                A(cpT[:, tt, :, :], ps[2 + tt][0:64, :].rearrange("p (j q) -> p j q", j=4),
                  ACT.Copy).then_inc(cpT_ready, 1)
            for n in range(2, 6):
                attend(n)
            act.wait_ge(h_ready, 8)
            sums_of_squares(3)
            act.wait_ge(dtop_ready, 1)
            A(etop, dtop, ACT.Exp).then_inc(etop_ready, 1)

            def split_slot(i, r, first):
                n = MOE + r
                act.wait_ge(slot_full[n % RING], i * (16 * MOE_SLOTS // RING) + 16 * (n // RING + 1))
                for q in range(4):
                    if not (first and r == 0):
                        act.wait_ge(quarter_used, i * 4 * MOE_SLOTS + (4 * r + q - 3))
                    A(whi[:, q, :], ring[:, n % RING, q * 1024:(q + 1) * 1024], ACT.Copy).then_inc(whi_ready, 1)

            def expert(i, output_before, gather_next, first):
                j0 = i * MOE_SLABS

                def hidden(j):
                    act.wait_ge(ehT_done, j0 + (j + 1))
                    A(ehhi[:, :, :], ps[7][:, 0:4 * CAP].rearrange("p (f t) -> p f t", f=4),
                      ACT.Copy).then_inc(ehhi_ready, 1)

                for r, (kind, j) in enumerate(ffn_order(MOE_SLABS)):
                    split_slot(i, r, first)
                    if r == 0 and output_before:
                        output(i - 1)
                    if kind == "up":
                        if j:
                            hidden(j - 1)
                            act.wait_ge(ehrow_ready, j0 + j)
                        act.wait_ge(quarter_used, i * 4 * MOE_SLOTS + 4 * (gate_slot(j) + 1))
                        A(egate[:, :], ps[0][0:CAP, :], ACT.Silu).then_inc(egate_ready, 1)
                hidden(MOE_SLABS - 1)
                if gather_next:
                    next_tokens(i + 1)

            def next_tokens(i):
                act.wait_ge(xe32_ready, i + 1)
                A(xehi[:, :, :], xe32[:, :, :], ACT.Copy).then_inc(xehi_ready, 1)

            def output(i):
                act.wait_ge(quarter_used, (i + 1) * 4 * MOE_SLOTS)
                for half in range(2):
                    A(osb[:, half * 512:(half + 1) * 512], ps[2 + half][0:CAP, :], ACT.Copy).then_inc(o_ready, 1)

            act.wait_ge(router_done, 1)
            next_tokens(0)
            expert(0, False, True, True)
            with act.Fori(1, N_EXPERTS - 1) as i:
                expert(i, True, True, False)
            expert(N_EXPERTS - 1, True, False, False)
            output(N_EXPERTS - 1)
            act.wait_ge(list_ready, 1)
            with act.Fori(0, MAX_MORE) as k:
                used, _, _ = item_of(act, k)
                with act.If(used > 0):
                    i = k + N_EXPERTS
                    next_tokens(i)
                    expert(i, False, False, False)
                    output(i)

        @block.vector
        def _(dve):
            V = nc.vector
            steps = [0]
            powers = [0]

            def step(ins):
                steps[0] += 1
                ins.then_inc(dve_steps, 1)

            def settle():
                dve.wait_ge(dve_steps, steps[0])

            def link(ins):
                step(ins)
                settle()

            def normalise(k):
                dve.wait_ge(sumsq_ready, TT * (k + 1))
                rsqrt_mean(rstd[:, TT * k:TT * (k + 1)], ssq[:, TT * k:TT * (k + 1)], D)
                for tt in range(TT):
                    c = TT * k + tt
                    V.tensor_scalar(xn[:, tt, :], h[:, tt, :], rstd[:, c:c + 1], None, ALU.mult).then_inc(xn_ready, 1)
                for tt in range(TT):
                    for b in range(2):
                        dve.wait_ge(xnT_done, 4 * k + 2 * tt + b + 1)
                        g = col[:, V_LN + KC * k + 4 * b:V_LN + KC * k + 4 * b + 4]
                        V.tensor_tensor(xT[:, 4 * b:4 * b + 4, tt * P:(tt + 1) * P],
                                        ps[4 + 2 * tt + b][:, :].rearrange("p (c t) -> p c t", c=4),
                                        spread(g, 2, P), ALU.mult).then_inc(xT_ready, 1)

            def rsqrt_mean(dst, src, n):
                powers[0] += 1
                V.tensor_scalar(dst, src, 1.0 / n, EPS, ALU.mult, ALU.add).then_inc(mean_ready, 1)
                dve.wait_ge(rsqrt_ready, powers[0])

            def rotate(x1, x2, cos, sin, t):
                step(V.tensor_tensor(t[0], x1, cos, ALU.mult))
                step(V.tensor_tensor(t[1], x2, sin, ALU.mult))
                step(V.tensor_tensor(t[2], x2, cos, ALU.mult))
                step(V.tensor_tensor(t[3], x1, sin, ALU.mult))
                settle()
                step(V.tensor_tensor(x1, t[0], t[1], ALU.subtract))
                return V.tensor_tensor(x2, t[2], t[3], ALU.add)

            def heads_norm(c0, heads, gains, n):
                dve.wait_ge(head_sq_ready, n + 1)
                v = headsq[:, 0:TT * heads * HD].rearrange("p (t h c) -> p (t h) c", t=TT, c=HD)
                ss = hss[:, 0:TT * heads]
                rs = hrs[:, 0:TT * heads]
                link(V.tensor_reduce(ss, v, AX_X, ALU.add))
                rsqrt_mean(rs, ss, HD)
                xh = pr[:, :, c0:c0 + heads * HD].rearrange("p t (h c) -> p t h c", h=heads)
                link(V.tensor_tensor(xh, xh, spread(rs.rearrange("p (t h) -> p t h", t=TT), 3, HD), ALU.mult))
                at = 0
                for g0, count in gains:
                    for tt in range(TT):
                        g = spread(row[:, g0:g0 + HD], 1, count)
                        step(V.tensor_tensor(xh[:, tt, at:at + count, :], xh[:, tt, at:at + count, :], g, ALU.mult))
                    at += count
                settle()
                sin = spread(trig[:, 0, 0:TT, 0:8], 2, heads)
                cos = spread(trig[:, 1, 0:TT, 0:8], 2, heads)
                w_ = TT * heads * 8
                t = [rtmp[:, i * w_:(i + 1) * w_].rearrange("p (t h c) -> p t h c", t=TT, h=heads) for i in range(4)]
                rotate(xh[:, :, :, 0:8], xh[:, :, :, 8:16], cos, sin, t).then_inc(head_rows_ready, 1)
                dve.wait_ge(head_rows_ready, n + 1)

            def attend(n):
                tt, _, _, _, branch = UNITS[n]
                keys = P * (tt + 1)
                per = 512 // keys
                dve.wait_ge(scores_done, n + 1)
                for b in range(8 // per):
                    first = head_of(b, 0, per)
                    heads = amax.rearrange("p (i r) -> p r i", r=2)[:, first % 2, first // 2:first // 2 + per]
                    step(V.tensor_reduce(heads,
                                         ps[b][:, :].rearrange("p (h k) -> p h k", h=per), AX_X, ALU.max))
                settle()
                if branch is None:
                    sink = row[:, R_SINK:R_SINK + 8]
                    link(V.scalar_tensor_tensor(amax, amax, SCALE, sink, ALU.mult, ALU.max))
                    if n:
                        dve.wait_ge(esink_ready, n)
                    step(V.tensor_tensor(sinkd, sink, amax, ALU.subtract))
                    V.tensor_scalar(nmax, amax, -1.0, None, ALU.mult).then_inc(nmax_ready, 1)
                else:
                    V.tensor_scalar(nmax, amax, -SCALE, None, ALU.mult).then_inc(nmax_ready, 1)
                for g in range(groups_before[n] + 1, groups_before[n + 1], 2):
                    kt = (g - groups_before[n]) // 2
                    dve.wait_ge(probsT_done, g + 1)
                    V.tensor_copy(probsT[:, kt, 4:8, :],
                                  ps[5][:, :].rearrange("p (h t) -> p h t", h=4)).then_inc(probsT_dve, 1)
                dd = den[:, tt, :]
                if branch is None:
                    dve.wait_ge(esink_ready, n + 1)
                    link(V.tensor_tensor(dd, dd, esink, ALU.add))
                link(V.reciprocal(rden, dd))
                o = ps[6][:, :].rearrange("p (h c) -> p h c", h=8)
                dst = mix[:, tt, 512:1024].rearrange("p (h c) -> p h c", h=8)
                if branch is None:
                    dve.wait_ge(pv_done, n + 1)
                    V.tensor_tensor(dst, o, spread(rden, 2, HD), ALU.mult).then_inc(pv_used, 1)
                else:
                    gt = gates[:, tt, :].rearrange("p (h b) -> p h b", b=3)[:, :, branch]
                    link(V.tensor_tensor(wgt, rden, gt, ALU.mult))
                    dve.wait_ge(pv_done, n + 1)
                    t = qkT_tmp
                    V.tensor_tensor(t, o, spread(wgt, 2, HD), ALU.mult).then_inc(pv_used, 1)
                    dve.wait_ge(pv_used, n + 1)
                    ins = V.tensor_tensor(dst, dst, t, ALU.add)
                    if branch == 2:
                        ins.then_inc(mix_ready, 1)
                    else:
                        step(ins)
                        settle()

            qkT_tmp = pr[:, 0, RG:RG + 512].rearrange("p (h c) -> p h c", h=8)

            def copy_mixT(layer):
                for tt in range(TT):
                    for b in range(2):
                        dve.wait_ge(mixT_done, 4 * layer + 2 * tt + b + 1)
                        V.tensor_copy(mixT[:, 4 * b:4 * b + 4, tt * P:(tt + 1) * P],
                                      ps[4 + 2 * tt + b][:, :].rearrange("p (c t) -> p c t", c=4))\
                         .then_inc(mixT_ready, 1)
                for u in range(4):
                    s, tt = u // 2, u % 2
                    dve.wait_ge(out_done, 4 * layer + u + 1)
                    hs = h[:, tt, s * 512:(s + 1) * 512]
                    V.tensor_tensor(hs, hs, ps[u][:, :], ALU.add).then_inc(h_ready, 1)

            def feed_forward():
                for i in range(FFN_TILES):
                    dve.wait_ge(silu_gate, i + 1)
                    if i >= 8:
                        dve.wait_ge(down_done, i // 4 - 1)
                    V.tensor_tensor(hT[:, i % 8, :], sg[:, i % 4, :], ps[i % 4][:, T:2 * T],
                                    ALU.mult).then_inc(hidden_ready, 1)
                dve.wait_ge(down_done, FFN_SLABS)
                for tt in range(TT):
                    for half in range(2):
                        hs = h[:, tt, half * 512:(half + 1) * 512]
                        ins = V.tensor_tensor(hs, ps[4 + 2 * tt + half][:, :], hs, ALU.add)
                ins.then_inc(y_added, 1)

            dve.wait_ge(x_in, 16)
            dve.wait_ge(small_in, SMALL)
            normalise(0)
            link(V.tensor_copy(posf[:, :], posi[:, :]))
            ang = ws[:, 0:120].rearrange("p (j f) -> p j f", j=3)
            turns = ws[:, 120:360].rearrange("p (s f) -> p s f", s=2)
            fold = trig[:, :, :, :].rearrange("p s j f -> p s (j f)")
            for j in range(3):
                step(V.tensor_scalar(ang[:, j, :], con[:, C_INV:C_INV + 40], posf[:, j:j + 1], None, ALU.mult))
            settle()
            angf = ws[:, 0:120]
            for s in range(2):
                step(V.tensor_scalar(turns[:, s, :], angf, 1 / TWO_PI, 0.25 * s, ALU.mult, ALU.add))
            settle()
            link(V.tensor_scalar(turns, turns, ROUND, None, ALU.add))
            link(V.tensor_scalar(turns, turns, -ROUND, None, ALU.add))
            for s in range(2):
                step(V.scalar_tensor_tensor(fold[:, s, :], turns[:, s, :], -PI2_A, angf, ALU.mult, ALU.add))
            settle()
            link(V.scalar_tensor_tensor(fold, turns, -PI2_B, fold, ALU.mult, ALU.add))
            link(V.scalar_tensor_tensor(fold, turns, -PI2_C, fold, ALU.mult, ALU.add))
            link(V.tensor_scalar(fold[:, 1, :], fold[:, 1, :], TWO_PI / 4, None, ALU.add))
            V.tensor_scalar(fold, fold, 3.1415925, -3.1415925, ALU.min, ALU.max).then_inc(angle_ready, 1)

            dve.wait_ge(gT_done, 1)
            V.tensor_copy(gT[:, :], ps[4][0:16, 0:T]).then_inc(gT_ready, 1)
            dve.wait_ge(z_done, 1)
            z = ps[5][:, :].rearrange("p (t c) -> p t c", t=TT)
            link(V.tensor_tensor(la, z, spread(row[:, R_GB:R_GB + 256], 1, TT), ALU.add))
            V.scalar_tensor_tensor(eb, la, -1.0, la, ALU.mult, ALU.max).then_inc(z_ready, 1)
            dve.wait_ge(softplus_ready, 1)
            V.scalar_tensor_tensor(la, la, 0.0, tmp, ALU.min, ALU.subtract).then_inc(la_ready, 1)
            dve.wait_ge(cum_done, 1)
            link(V.tensor_copy(ebl, ps[6][:, :].rearrange("p (t c) -> p t c", t=TT)))
            V.tensor_tensor(tmp, ps[7][:, :].rearrange("p (t c) -> p t c", t=TT), ebl,
                            ALU.subtract).then_inc(dl_ready, 1)
            dve.wait_ge(decay_ready, 1)
            step(V.scalar_tensor_tensor(qin, pr[:, :, GQ:GQ + 256], HD ** -0.5, eb, ALU.mult, ALU.mult))
            step(V.tensor_tensor(kin, pr[:, :, GK:GK + 256], enb, ALU.mult))
            dve.wait_ge(ebl_ready, 1)
            V.tensor_tensor(kst, pr[:, :, GK:GK + 256], ebl, ALU.mult).then_inc(gla_ops_ready, 1)
            dve.wait_ge(kv_done, 1)
            dve.wait_ge(pool_steps, 2)
            for c in range(3):
                for hp in range(2):
                    for r in range(2):
                        q = slice(64 * r, 64 * r + 64)
                        kv = ps[5 + c][q, hp * 256 + r * P:hp * 256 + (r + 1) * P]
                        s = state[q, c, 2 * hp + r, :]
                        if c == 0:
                            ins = V.tensor_copy(s, kv)
                        else:
                            d = dec[q, 4 * hp + c:4 * hp + c + 1]
                            ins = V.scalar_tensor_tensor(s, state[q, c - 1, 2 * hp + r, :], d, kv,
                                                         ALU.mult, ALU.add)
                        if c < 2 or (hp, r) != (1, 1):
                            step(ins)
                        else:
                            ins.then_inc(state_ready, 1)
                settle()
            dve.wait_ge(lin_scores_done, 2)
            for r in range(2):
                V.copy_predicated(glasc[:, r, :, :, :].rearrange("p a b t -> p (a b) t"),
                                  spread(tri.bitcast(I32), 1, 4),
                                  ps[2 + r][:, :].rearrange("p (h t) -> p h t", h=4)).then_inc(lin_scores_ready, 1)

            def gated(layer, gain, c0):
                for tt in range(TT):
                    m = mix[:, tt, 0:512]
                    link(V.tensor_tensor(m, m, gain, ALU.mult)) if len(gain.shape) == 2 else \
                        link(V.tensor_tensor(m.rearrange("p (h c) -> p h c", h=4), m.rearrange("p (h c) -> p h c", h=4),
                                             gain, ALU.mult))
                    dve.wait_ge(silu_ready, TT * layer + tt + 1)
                    link(V.tensor_tensor(m, m, pr[:, tt, c0:c0 + 512], ALU.mult))

            dve.wait_ge(lin_sq_ready, 2)
            link(V.tensor_reduce(hss[:, 0:8], ws[:, 2048:3072].rearrange("p (h c) -> p h c", c=P), AX_X, ALU.add))
            rsqrt_mean(hrs[:, 0:8], hss[:, 0:8], P)
            for tt in range(TT):
                step(V.tensor_tensor(mix[:, tt, 0:512].rearrange("p (h c) -> p h c", h=4),
                                     ps[tt][:, :].rearrange("p (h c) -> p h c", h=4),
                                     spread(hrs[:, 4 * tt:4 * tt + 4], 2, P), ALU.mult))
            settle()
            gated(0, spread(row[:, R_GN:R_GN + P], 1, 4), GOUT)

            dve.wait_ge(trig_ready, 1)
            heads_norm(SQ, 10, [(R_SQ, 8), (R_SK, 2)], 0)
            attend(0)
            dve.wait_ge(pv_used, 1)
            link(V.tensor_copy(rden, rden))
            V.tensor_copy(sm[:, 400:401], mix[:, 0, 1023:1024]).then_inc(mix_ready, 1)
            attend(1)
            dve.wait_ge(pv_used, 2)
            V.tensor_copy(sm[:, 400:401], mix[:, 1, 1023:1024]).then_inc(mix_ready, 1)
            copy_mixT(0)
            dve.wait_ge(h_ready, 4)
            normalise(1)
            feed_forward()

            dve.wait_ge(y_added, 1)
            normalise(2)
            dve.wait_ge(proj_out, 12)
            qk = pr[:, :, RQ:RQ + 512].rearrange("p t (h c) -> p t h c", h=8)
            t = [ws[:, i * 512:(i + 1) * 512].rearrange("p (t h c) -> p t h c", t=TT, h=8) for i in range(4)]
            rotate(qk[:, :, :, 0:32], qk[:, :, :, 32:64], spread(trig[:, 1, 0:TT, 8:40], 2, 8),
                   spread(trig[:, 0, 0:TT, 8:40], 2, 8), t).then_inc(ret_rows_ready, 1)
            dve.wait_ge(lin_scores_done, 2 + 3)
            for i, d0 in enumerate((C_RD, C_RD, C_RO)):
                for r in range(2):
                    bank = ps[2 * (i // 2) + r][:, (i % 2) * 256:(i % 2 + 1) * 256]
                    V.tensor_tensor(retsc[:, i, :, :].rearrange("p (j r) q -> p r j q", r=2)[:, r, :, :],
                                    bank.rearrange("p (j q) -> p j q", j=2),
                                    con[:, d0:d0 + 512].rearrange("p (j r q) -> p r j q", j=2, r=2)[:, r, :, :],
                                    ALU.mult).then_inc(lin_scores_ready, 1)
            for tt in range(TT):
                dve.wait_ge(lin_out_done, 2 + tt + 1)
                step(V.tensor_reduce(hss[:, 4 * tt:4 * tt + 4], ps[6 + tt][:, :].rearrange("p (h c) -> p h c", h=4),
                                     AX_X, ALU.add))
            settle()
            link(V.tensor_scalar(hmu, hss[:, 0:8], 1.0 / P, None, ALU.mult))
            for tt in range(TT):
                m = mix[:, tt, 0:512].rearrange("p (h c) -> p h c", h=4)
                link(V.tensor_tensor(m, ps[6 + tt][:, :].rearrange("p (h c) -> p h c", h=4),
                                     spread(hmu[:, 4 * tt:4 * tt + 4], 2, P), ALU.subtract))
                link(V.tensor_tensor(linsq[:, tt, :], mix[:, tt, 0:512], mix[:, tt, 0:512], ALU.mult))
            link(V.tensor_reduce(hss[:, 0:8], ws[:, 2048:3072].rearrange("p (h c) -> p h c", c=P), AX_X, ALU.add))
            rsqrt_mean(hrs[:, 0:8], hss[:, 0:8], P)
            for tt in range(TT):
                m = mix[:, tt, 0:512].rearrange("p (h c) -> p h c", h=4)
                step(V.tensor_tensor(m, m, spread(hrs[:, 4 * tt:4 * tt + 4], 2, P), ALU.mult))
            settle()
            gated(1, row[:, R_RN:R_RN + 512], RG)

            heads_norm(NQ, 12, [(R_NQ, 8), (R_KS, 2), (R_KW, 2)], 1)
            dve.wait_ge(gates_ready, 1)
            link(V.tensor_scalar(gates, gates, 1.0, None, ALU.add))
            link(V.reciprocal(gates, gates))
            dve.wait_ge(head_T_ready, 7)
            link(V.memset(blk, 0.0))
            for i, v0 in enumerate((V_PK, V_PV)):
                dve.wait_ge(kcT_done, i + 1)
                for r in range(2):
                    for g in range(2):
                        for half in range(2):
                            src = ps[i][64 * g:64 * g + 64, 16 * half:16 * half + 240]\
                                .rearrange("p (n l r) -> p l n r", l=8, r=2)[:, :, :, r]
                            q = slice(64 * r, 64 * r + 64)
                            dst = blk[q, i, 8 * half:8 * half + 8, 32 * g:32 * g + NCMP]
                            pe_ = col[q, v0 + 8 * half:v0 + 8 * half + 8]
                            ins = V.tensor_tensor(dst, src, spread(pe_, 2, NCMP), ALU.add)
                            if (r, g, half) == (1, 1, 1):
                                ins.then_inc(blk_ready, 1)
                            else:
                                step(ins)
            for i, b0 in enumerate((V_B1K, V_B1V)):
                dve.wait_ge(hid_done, i + 1)
                step(V.tensor_tensor(hidx[:, i, :].rearrange("p (a c) -> p a c", a=2),
                                     ps[2 + i][:, 0:128].rearrange("p (a c) -> p a c", a=2),
                                     spread(col[:, b0:b0 + 2], 2, 64), ALU.add))
            settle()
            link(V.tensor_tensor(hid, hidx, hidx, ALU.mult))
            link(V.tensor_scalar(hid, hid, 0.044715, 1.0, ALU.mult, ALU.add))
            V.tensor_tensor(hide, hid, hidx, ALU.mult).then_inc(hid_x, 1)
            dve.wait_ge(hid_e, 1)
            link(V.tensor_scalar(hid, hide, 1.0, None, ALU.add))
            link(V.reciprocal(hid, hid))
            V.tensor_tensor(hid, hid, hidx, ALU.mult).then_inc(hid_ready, 1)
            dve.wait_ge(cmp_done, 1)
            link(V.tensor_tensor(cv[:, :, :], ps[4][0:64, 0:128].rearrange("p (i c) -> p i c", i=2),
                                 row[0:64, R_B2K:R_B2K + 128].rearrange("p (i c) -> p i c", i=2), ALU.add))
            ck = cv[:, 0, :]
            link(V.tensor_tensor(cktmp[:, 0:64], ck, ck, ALU.mult))
            link(V.tensor_reduce(ckss[:, 0:1], cktmp[:, 0:64], AX_X, ALU.add))
            rsqrt_mean(ckss[:, 1:2], ckss[:, 0:1], HD)
            link(V.scalar_tensor_tensor(ck, ck, ckss[:, 1:2], row[0:64, R_KC:R_KC + HD], ALU.mult, ALU.mult))
            t = [cktmp[:, i * 8:(i + 1) * 8] for i in range(4)]
            step(rotate(ck[:, 0:8], ck[:, 8:16], trig[0:64, 1, 2, 0:8], trig[0:64, 0, 2, 0:8], t))
            settle()
            V.tensor_copy(ckdup.rearrange("p (d c) -> p d c", d=2), spread(ck, 1, 2)).then_inc(ckv_ready, 1)
            dve.wait_ge(cs_done, 1)
            for tt in range(TT):
                s4 = csm[:, tt, 0:120].rearrange("p (x n) -> p x n", n=NCMP)
                for r in range(2):
                    src = ps[r][:, tt * 64:(tt + 1) * 64].rearrange("p (x n) -> p x n", n=16)[:, :, 0:NCMP]
                    step(V.tensor_tensor(s4[:, 4 * r:4 * r + 4, :], src,
                                         spread(con[:, C_CADD + NCMP * tt:C_CADD + NCMP * (tt + 1)], 1, 4), ALU.add))
                settle()
                link(V.tensor_reduce(cmx[:, tt, :], s4, AX_X, ALU.max))
                ins = V.tensor_tensor(s4, s4, spread(cmx[:, tt, :], 2, NCMP), ALU.subtract)
                if tt == 0:
                    step(ins)
                else:
                    ins.then_inc(cs_ready, 1)
            link(V.memset(cpd, 0.0))
            dve.wait_ge(ce_ready, 1)
            for tt in range(TT):
                s4 = csm[:, tt, 0:120].rearrange("p (x n) -> p x n", n=NCMP)
                step(V.tensor_reduce(cden[:, tt, :], s4, AX_X, ALU.add))
                dst = cpd[:, tt, :].rearrange("p (x n) -> p x n", n=32)[:, :, 0:NCMP]
                ins = V.tensor_tensor(dst, s4, spread(con[:, C_CONE + NCMP * tt:C_CONE + NCMP * (tt + 1)], 1, 8), ALU.mult)
                if tt == 0:
                    step(ins)
                else:
                    ins.then_inc(cp_ready, 1)
            settle()
            link(V.reciprocal(cden, cden))
            for tt in range(TT):
                gt = gates[:, tt, :].rearrange("p (g j r b) -> p g j r b", g=2, j=2, r=2)[:, :, :, :, 0]
                cd = cden[:, tt, :].rearrange("p (r j g) -> p g j r", r=2, j=2)
                link(V.tensor_tensor(wgt.rearrange("p (g j r) -> p g j r", g=2, j=2), cd, gt, ALU.mult))
                dve.wait_ge(cpv_done, 2)
                for g in range(2):
                    ins = V.tensor_tensor(mix[:, tt, 512 + 256 * g:768 + 256 * g].rearrange("p (h c) -> p h c", h=4),
                                          ps[4 + g][:, 256 * tt:256 * (tt + 1)].rearrange("p (h c) -> p h c", h=4),
                                          spread(wgt[:, 4 * g:4 * g + 4], 2, HD), ALU.mult)
                if tt == 0:
                    link(ins)
                else:
                    ins.then_inc(mix_ready, 1)
                    dve.wait_ge(mix_ready, 3)
            for n in range(2, 6):
                attend(n)
            copy_mixT(1)
            dve.wait_ge(h_ready, 8)
            normalise(3)
            dve.wait_ge(router_done, 1)
            link(V.tensor_tensor(logit, ps[0][:, 0:16].rearrange("p (t e) -> p t e", t=TT),
                                 spread(row[:, R_RB:R_RB + 8], 1, TT), ALU.add))
            for tt in range(TT):
                step(V.max(top[:, tt, :], logit[:, tt, :]))
            settle()
            for tt in range(TT):
                step(V.max_index(topi[:, tt, :], top[:, tt, :], logit[:, tt, :]))
            settle()
            step(V.tensor_copy(topf, topi))
            V.tensor_tensor(dtop, top[:, :, 1], top[:, :, 0], ALU.subtract).then_inc(dtop_ready, 1)
            dve.wait_ge(etop_ready, 1)
            settle()
            link(V.tensor_scalar(dsum, etop, 1.0, None, ALU.add))
            link(V.reciprocal(wtop[:, 0, :], dsum))
            link(V.tensor_tensor(wtop[:, 1, :], etop, wtop[:, 0, :], ALU.mult))
            for tt in range(TT):
                for k, dst in ((0, chosen), (1, rank)):
                    step(V.tensor_scalar(dst[:, tt, :], con[:, C_IOTA:C_IOTA + 8], topf[:, tt, k:k + 1], None,
                                         ALU.is_equal))
            settle()
            for tt in range(TT):
                for k, (src, dst) in enumerate(((chosen, comb), (rank, comb2))):
                    step(V.tensor_scalar(dst[:, tt, :], src[:, tt, :], wtop[:, k, tt:tt + 1], None, ALU.mult))
            settle()
            V.tensor_tensor(chosen[:, :, :], chosen[:, :, :], rank[:, :, :], ALU.add).then_inc(chosen_ready, 1)
            step(V.tensor_tensor(comb, comb, comb2, ALU.add))
            dve.wait_ge(rank_done, 1)
            dve.wait_ge(chosen_ready, 1)
            settle()
            link(V.scalar_tensor_tensor(rank[:, :, :], ps[1][:, 0:16].rearrange("p (t e) -> p t e", t=TT), 1.0, chosen[:, :, :],
                                        ALU.add, ALU.mult))
            link(V.tensor_scalar(rank[:, :, :], rank[:, :, :], -1.0, None, ALU.add))

            def iota(first):
                return econ[:, D_IOTA:D_IOTA + CAP] if first is None else econ[:, bass.ds(first + D_IOTA, CAP)]

            def make_pick(i, e, first, waits=True):
                if waits:
                    dve.wait_ge(gather_done, i)
                for tt in range(TT):
                    ins = V.tensor_scalar(pick[:, tt, :], iota(first), rank[:, tt, bass.ds(e, 1)], None, ALU.is_equal)
                ins.then_inc(pick_ready, 1)

            def next_tokens(i):
                dve.wait_ge(gather_done, i + 1)
                for b in range(2):
                    g = col[:, V_LN + 3 * KC + 4 * b:V_LN + 3 * KC + 4 * b + 4]
                    ins = V.tensor_tensor(xe32[:, 4 * b:4 * b + 4, :],
                                          ps[4 + b][:, 0:4 * CAP].rearrange("p (c t) -> p c t", c=4),
                                          spread(g, 2, CAP), ALU.mult)
                ins.then_inc(xe32_ready, 1)
                dve.wait_ge(xehi_ready, i + 1)
                V.tensor_tensor(xelo[:, :, :], xe32[:, :, :], xehi[:, :, :].bitcast(F32),
                                ALU.subtract).then_inc(xelo_ready, 1)

            def add_output(i):
                for tt in range(TT):
                    dve.wait_ge(scatter_done, i * 2 + (tt + 1))
                    for half in range(2):
                        hs = h[:, tt, half * 512:(half + 1) * 512]
                        ins = V.tensor_tensor(hs, ps[6 - 2 * tt + half][:, :], hs, ALU.add)
                    ins.then_inc(y_used, 1)

            def expert(i, e, first, scatter_before, gather_next):
                j0, q0 = i * MOE_SLABS, i * 4 * MOE_SLOTS

                def hidden(j):
                    dve.wait_ge(ehhi_ready, j0 + (j + 1))
                    V.tensor_tensor(ehlo[:, :, :], ps[7][:, 0:4 * CAP].rearrange("p (f t) -> p f t", f=4),
                                    ehhi[:, :, :].bitcast(F32), ALU.subtract).then_inc(ehlo_ready, 1)

                for r, (kind, j) in enumerate(ffn_order(MOE_SLABS)):
                    for q in range(4):
                        dve.wait_ge(whi_ready, q0 + (4 * r + q + 1))
                        V.tensor_tensor(wlo[:, q, :], ring[:, (MOE + r) % RING, q * 1024:(q + 1) * 1024],
                                        whi[:, q, :].bitcast(F32), ALU.subtract).then_inc(wlo_ready, 1)
                    if kind == "up" and j:
                        hidden(j - 1)
                    if r and ffn_order(MOE_SLABS)[r - 1][0] == "up":
                        j = ffn_order(MOE_SLABS)[r - 1][1]
                        dve.wait_ge(egate_ready, j0 + (j + 1))
                        dve.wait_ge(quarter_used, q0 + 4 * (up_slot(j) + 1))
                        if j:
                            dve.wait_ge(ehT_done, j0 + j)
                        V.tensor_tensor(ehrow[:, :], egate[:, :], ps[1][0:CAP, :], ALU.mult).then_inc(ehrow_ready, 1)
                        if j == 0 and scatter_before:
                            add_output(i - 1)
                        if j == 1:
                            dve.wait_ge(spreadwT_done, i)
                            for tt in range(TT):
                                ins = V.tensor_scalar(spreadw[:, tt, :], iota(first), rank[:, tt, bass.ds(e, 1)],
                                                      comb[:, tt, bass.ds(e, 1)], ALU.is_equal, ALU.mult)
                            ins.then_inc(spreadw_ready, 1)
                        if j == 2 and gather_next:
                            make_pick(i + 1, e + 1, first)
                        if j == 3:
                            dve.wait_ge(spreadwT_done, i + 1)
                            dve.wait_ge(scatter_done, i * 2)
                            V.tensor_copy(spreadwT[:, :], ps[6][0:CAP, 0:T]).then_inc(spreadwT_ready, 1)
                hidden(MOE_SLABS - 1)
                if gather_next:
                    next_tokens(i + 1)

            make_pick(0, 0, None, False)
            next_tokens(0)
            expert(0, 0, None, False, True)
            for tt in range(TT):
                ins = V.tensor_copy(pairs[:, tt, :].rearrange("p (c e) -> p c e", e=8),
                                    spread(chosen[:, tt, :], 1, PARTS - 1))
            ins.then_inc(list_pairs_ready, 1)
            dve.wait_ge(count_done, 1)
            V.tensor_scalar(active[:, :], ps[7][0:NQ_MORE, 0:1], econ[0:NQ_MORE, D_THR:D_THR + 1], None,
                            ALU.is_gt).then_inc(active_ready, 1)
            dve.wait_ge(place_done, 1)
            dve.wait_ge(active_ready, 1)
            link(V.tensor_copy(cmx[0:NQ_MORE, 0, 0:1], ps[7][0:NQ_MORE, 1:2]))
            V.tensor_scalar(slots[:, :], econ[0:NQ_MORE, D_IK:D_IK + MAX_MORE], cmx[0:NQ_MORE, 0, 0:1], active[:, :],
                            ALU.is_equal, ALU.mult).then_inc(slots_ready, 1)
            dve.wait_ge(list_done, 1)
            V.tensor_copy(items[:, :], ps[7][0:1, 16:16 + 3 * MAX_MORE]).then_inc(list_ready, 1)
            with dve.Fori(1, N_EXPERTS - 1) as i:
                expert(i, i, None, True, True)
            expert(N_EXPERTS - 1, N_EXPERTS - 1, None, True, False)
            add_output(N_EXPERTS - 1)
            dve.wait_ge(list_ready, 1)
            with dve.Fori(0, MAX_MORE) as k:
                used, e, first = item_of(dve, k)
                with dve.If(used > 0):
                    i = k + N_EXPERTS
                    make_pick(i, e, first)
                    next_tokens(i)
                    expert(i, e, first, False, False)
                    add_output(i)
            V.memset(slots[:, :], 0.0).then_inc(moe_done, 1)

        @block.gpsimd
        def _(pool):
            nc.gpsimd.memset(glasc, 0.0).then_inc(pool_steps, 1)
            nc.gpsimd.memset(mhalf[:, :], -0.5).then_inc(mhalf_ready, 1)
            pool.wait_ge(mhalf_ready, 1)
            for n, v in enumerate((rstd[:, 0:2], hrs[:, 0:8], hrs[:, 0:20], rstd[:, 2:4],
                                   rstd[:, 4:6], hrs[:, 0:8], hrs[:, 0:24], ckss[:, 1:2], rstd[:, 6:8])):
                pool.wait_ge(mean_ready, n + 1)
                p, c = v.shape
                nc.gpsimd.tensor_tensor(v, v, mhalf[0:p, 0:c], ALU.pow).then_inc(rsqrt_ready, 1)
                if n == 0:
                    pool.wait_ge(gla_ops_ready, 1)
                    nc.gpsimd.memset(state, 0.0).then_inc(pool_steps, 1)


_WEIGHTS = ["w_in_e", "gla_gate_up", "w_out_e", "ffn_w_gate", "ffn_w_up", "ffn_w_down", "w_in_o",
            "cmp_w1_k", "cmp_w2_k", "cmp_w1_v", "cmp_w2_v", "w_out_o", "router_w",
            "exp_w_gate", "exp_w_up", "exp_w_down"]


def shape_constants():
    import numpy as np

    c = np.zeros((P, NC), np.float32)
    i = np.arange(P)
    c[:, C_ID:C_ID + P] = np.eye(P)
    chunk = i // 64
    same = chunk[:, None] == chunk[None, :]
    c[:, C_TRI:C_TRI + P] = same & (i[:, None] <= i[None, :])
    c[:, C_SAME:C_SAME + P] = same
    c[:, C_CH:C_CH + 2] = chunk[:, None] == np.arange(2)[None, :]
    for hh in range(4):
        lg = float(np.log(np.float32(1.0) - np.float32(2.0 ** (-5 - hh))))
        diff = i[None, :] - i[:, None]
        c[:, C_RD + hh * P:C_RD + (hh + 1) * P] = np.where(diff >= 0, np.exp(lg * np.maximum(diff, 0)), 0) * HD ** -0.5
        c[:, C_RO + hh * P:C_RO + (hh + 1) * P] = np.exp(lg * (diff + P)) * HD ** -0.5
    diag = np.where(i[None, :] <= i[:, None], 0.0, NEG)
    c[:, C_SWA:C_SWA + P] = np.where(i[None, :] > i[:, None], 0.0, NEG)
    c[:, C_SWA + P:C_SWA + T] = diag
    c[:, C_FULL + P:C_FULL + T] = diag
    end = np.arange(NCMP) * 16 + 31
    for tt in range(TT):
        ok = end[None, :] <= (tt * P + i)[:, None]
        c[:, C_CADD + NCMP * tt:C_CADD + NCMP * (tt + 1)] = np.where(ok, 0.0, NEG)
        c[:, C_CONE + NCMP * tt:C_CONE + NCMP * (tt + 1)] = ok
    f = np.arange(8, dtype=np.float32)
    c[:, C_INV:C_INV + 8] = np.float32(500000.0) ** (-f * np.float32(2.0) / np.float32(16))
    f = np.arange(32, dtype=np.float32)
    c[:, C_INV + 8:C_INV + 40] = np.float32(10000.0) ** (-f * np.float32(2.0) / np.float32(64))
    c[:, C_IOTA:C_IOTA + 8] = np.arange(8)
    return c


def expert_constants():
    import numpy as np

    c = np.zeros((P, ND), np.float32)
    i = np.arange(P)
    c[:, D_SU:D_SU + P] = i[:, None] < i[None, :]
    c[:, D_ONE:D_ONE + P] = 1
    c[:, D_IOTA:D_IOTA + CAP * PARTS] = np.arange(CAP * PARTS)
    q = np.arange(NQ_MORE)
    part = q // N_EXPERTS + 1
    c[:NQ_MORE, D_THR] = c[:NQ_MORE, D_QS] = part * CAP
    c[:NQ_MORE, D_QE] = q % N_EXPERTS
    c[:NQ_MORE, D_LOW:D_LOW + NQ_MORE] = q[:, None] < q[None, :]
    c[:, D_IK:D_IK + MAX_MORE] = np.arange(MAX_MORE)
    return c


def kernel(**inputs):
    import numpy as np
    import concourse.bacc as bacc
    from concourse.bass_utils import run_bass_kernel_spmd

    a = {k: np.ascontiguousarray(v) for k, v in inputs.items()}
    rowv = np.concatenate([a[k].reshape(-1) for k in (
        "gla_gate_bias", "gla_out_norm", "swa_q_norm", "swa_k_norm", "ret_out_norm", "nsa_q_norm", "nsa_kc_norm",
        "nsa_ks_norm", "nsa_kw_norm", "cmp_b2_k", "cmp_b2_v", "swa_sinks", "router_b")])[None, :]
    colv = np.concatenate([a[k].reshape(-1, P).T for k in (
        "ln_mix_e", "ln_ffn_e", "ln_mix_o", "ln_ffn_o", "cmp_b1_k", "cmp_b1_v", "cmp_pos_k", "cmp_pos_v")], axis=1)
    assert rowv.shape[1] == NR and colv.shape[1] == NV
    token = a["positions"].reshape(-1)
    pos = np.zeros((P, 3), token.dtype)
    pos[:, 0], pos[:, 1] = token[:P], token[P:]
    for g in range(2):
        pos[32 * g:32 * g + NCMP, 2] = token[np.arange(NCMP) * 16 + 31]

    nc = bacc.Bacc("TRN2", target_bir_lowering=False, num_devices=1)
    arrays = {}

    def feed(name, arr):
        arr = np.ascontiguousarray(arr)
        arrays[name] = arr
        return nc.dram_tensor(name, arr.shape, mybir.dt.from_np(arr.dtype), kind="ExternalInput").ap()

    x = feed("x_dram", a["x"].reshape(T, D))
    p = feed("pos_dram", pos)
    c = feed("consts_dram", shape_constants())
    ec = feed("expert_consts_dram", expert_constants())
    r = feed("rows_dram", rowv)
    v = feed("cols_dram", colv)
    w = {k: feed(k + "_dram", a[k]) for k in _WEIGHTS}
    w["out"] = nc.dram_tensor("out_dram", (T, D), F32, kind="ExternalOutput").ap()
    build(nc, x, p, c, ec, r, v, w)
    res = run_bass_kernel_spmd(nc, [arrays], core_ids=[0])
    return res.results[0]["out_dram"].reshape(1, T, D)
```

```python
from contextlib import ExitStack

import concourse.bass as bass
from concourse import mybir

F32 = mybir.dt.float32
F32R = mybir.dt.float32r
BF16 = mybir.dt.bfloat16
I32 = mybir.dt.int32
U32 = mybir.dt.uint32
ALU = mybir.AluOpType
ACT = mybir.ActivationFunctionType
AX_X = mybir.AxisListType.X

P = 128
T = 256
TT = T // P
D = 1024
KC = D // P
HD = 64
EPS = 1e-6
SCALE = HD ** -0.5
NEG = -1e30

D_FF = 2816
N_EXPERTS = 8
D_FFE = 3584
TOP_K = 2

GQ, GK, GV, GLOW, GOUT, SQ, SK, SV, L0_IN = 0, 256, 512, 1024, 1040, 1552, 2064, 2192, 2320
RQ, RK, RV, RG, NQ, L1_IN = 0, 256, 512, 1024, 1536, 2840
KS_, KW_, KC_, VC_, VS_, VW_, NG_ = 2048, 2176, 2304, 2432, 2560, 2688, 2816

NCMP = 15
CMP_H = 256
SLAB = 512
RING = 7

C_ID, C_TRI, C_SAME, C_CH, C_RD, C_RO, C_SWA, C_FULL = 0, 128, 256, 384, 386, 898, 1410, 1666
C_CADD, C_CONE, C_INV, C_IOTA, NC = 1922, 1952, 1982, 2022, 2030
R_GB, R_GN, R_SQ, R_SK, R_RN, R_NQ, R_KC, R_KS, R_KW, R_B2K, R_B2V, R_SINK, R_RB, NR = (
    0, 256, 384, 448, 512, 1024, 1088, 1152, 1216, 1280, 1344, 1408, 1416, 1424)
V_LN, V_B1K, V_B1V, V_PK, V_PV, NV = 0, 32, 34, 36, 52, 68

TWO_PI = 6.283185307179586
PI2_A = 6.28125
PI2_B = 0.00193500518798828125
PI2_C = TWO_PI - PI2_A - PI2_B
ROUND = 12582912.0

L0_ORDER = (2, 0, 3, 4, 1)
L1_ORDER = (3, 4, 5, 0, 1, -1, -2, 2)

L0_PROJ = 0
L0_OUT = L0_PROJ + 5
L0_FFN = L0_OUT + 2
FFN_SLABS = -(-D_FF // SLAB)
L1_PROJ = L0_FFN + 3 * FFN_SLABS
L1_OUT = L1_PROJ + len(L1_ORDER)
MOE = L1_OUT + 2
MOE_SLABS = D_FFE // SLAB
MOE_SLOTS = 3 * MOE_SLABS
FFN_TILES = D_FF // P
MOE_TILES = D_FFE // P

CAP = 96
PARTS = -(-T // CAP)
MAX_MORE = TOP_K * T // CAP
NQ_MORE = (PARTS - 1) * N_EXPERTS
D_SU, D_ONE, D_IOTA = 0, P, 2 * P
D_THR = D_IOTA + CAP * PARTS
D_QE, D_QS, D_LOW = D_THR + 1, D_THR + 2, D_THR + 3
D_IK = D_LOW + NQ_MORE
ND = D_IK + MAX_MORE
assert ND <= 1024 and NQ_MORE <= 64
assert MOE_SLOTS % RING == 0

STAGE = RING - 1


def place(n):
    return (n + (n >= L1_PROJ + 2) + (n >= L1_OUT)) % RING


def fills(n):
    return sum(place(m) == place(n) for m in range(n + 1))


assert all(place(n) != STAGE for first, end in ((L0_PROJ, L0_OUT), (L1_PROJ, MOE)) for n in range(first, end))


def gate_slot(j):
    return 3 * j - 1 if j else 0


def up_slot(j):
    return gate_slot(j) + 1


def down_slot(j, slabs):
    return 3 * j + 4 if j < slabs - 1 else 3 * slabs - 1


def ffn_order(slabs):
    order = [None] * (3 * slabs)
    for j in range(slabs):
        order[gate_slot(j)] = ("gate", j)
        order[up_slot(j)] = ("up", j)
        order[down_slot(j, slabs)] = ("down", j)
    return order


def split_quarters():
    def by_chunks(kind, first, slabs):
        return [(first + n, kind, s, i) for n, s in enumerate(slabs) if s >= 0 for i in range(4)]

    ffn = [(L0_FFN + r, kind, j, i) for r, (kind, j) in enumerate(ffn_order(FFN_SLABS))
           for i in range(len(tiles_of(j, FFN_TILES)))]
    parts = [by_chunks("in", L0_PROJ, L0_ORDER), by_chunks("out", L0_OUT, range(2)), ffn,
             by_chunks("in", L1_PROJ, L1_ORDER), by_chunks("out", L1_OUT, range(2))]
    quarters, starts = [], []
    for part in parts:
        starts.append(len(quarters))
        quarters += part
    return quarters, starts


def tiles_of(j, tiles):
    return range(4 * j, min(4 * j + 4, tiles))


def spread(ap, axis, n):
    v = ap.unsqueeze(axis)
    shape = list(v.shape)
    shape[axis] = n
    return v.to_broadcast(shape)


def build(nc, x, pos, consts, expert_consts, rowv, colv, w):
    with ExitStack() as ctx:
        def sb(name, shape, dt=F32):
            return ctx.enter_context(nc.sbuf_tensor(name, shape, dt))

        def sem(name):
            return ctx.enter_context(nc.semaphore(name))

        out = w["out"]
        def here():
            return -(-nc.sbuf_base // 32) * 32

        ring_at = here()
        ring = sb("ring", [P, RING, 4096])
        h = sb("h", [P, TT, D])
        xn = sb("xn", [P, TT, D])
        con = sb("con", [P, NC])
        row = sb("row", [P, NR])
        col = sb("col", [P, NV])
        arena = nc.sbuf_base
        pr = sb("pr", [P, TT, L1_IN])
        xT_at = here()
        xT = sb("xT", [P, KC, T])
        qkT_at = here()
        qkT = sb("qkT", [P, 2048])
        ws_at = here()
        ws = sb("ws", [P, 4096])
        arena_end = nc.sbuf_base
        gT = sb("gT", [16, T])
        gup = sb("gup", [16, 256])
        posi = sb("posi", [P, 3], I32)
        posf = sb("posf", [P, 3])
        trig = sb("trig", [P, 2, 3, 40])
        w2 = sb("w2", [P, 2, 2, HD])
        kcT = sb("kcT", [P, 64])
        cv = sb("cv", [64, 2, HD])
        rw = sb("rw", [P, KC, N_EXPERTS])
        mbf = sb("mbf", [P, 2, T], BF16)
        idb = sb("idb", [P, P], BF16)
        items = sb("items", [1, 3 * MAX_MORE], I32)
        mhalf = sb("mhalf", [P, 24])
        sm = sb("sm", [P, 512])
        ps = [ctx.enter_context(nc.psum_tensor(f"ps{i}", [P, 512], F32)) for i in range(8)]

        ident = con[:, C_ID:C_ID + P]
        tri = con[:, C_TRI:C_TRI + P]
        same = con[:, C_SAME:C_SAME + P]
        mix = xn

        fhi = [nc.alloc_sbuf_tensor_at(f"fhi{i}", [P, 1024], F32R, offset=at + 4 * (i % 2 * L1_IN + i // 2 * 1024))
               for at in [-(-arena // 32) * 32] for i in range(4)]
        pstage = [nc.alloc_sbuf_tensor_at(f"pstage{i}", [P, 1024], F32R, offset=ring_at + 16384 * STAGE + 4096 * i)
                  for i in range(4)]
        flo = [nc.alloc_sbuf_tensor_at(f"flo{i}", [P, 4096], F32R, offset=ring_at + 16384 * i) for i in range(RING)]
        xhi = nc.alloc_sbuf_tensor_at("xhi", [P, KC, T], F32R, offset=xT_at)
        xlo = nc.alloc_sbuf_tensor_at("xlo", [P, KC, T], F32R, offset=qkT_at)
        xlo1 = nc.alloc_sbuf_tensor_at("xlo1", [P, KC, T], F32R, offset=ws_at + 4 * 8 * T)
        hhi = nc.alloc_sbuf_tensor_at("hhi", [P, 8, T], F32R, offset=ws_at)
        hlo = nc.alloc_sbuf_tensor_at("hlo", [P, 8, T], F32R, offset=ws_at + 4 * 8 * T)

        room = [arena]

        def take(name, shape, dt=F32):
            at = -(-room[0] // 32) * 32
            n = 1
            for d in shape[1:]:
                n *= d
            room[0] = at + 4 * n
            assert room[0] <= arena_end
            return nc.alloc_sbuf_tensor_at(name, shape, dt, offset=at)

        whi = take("whi", [P, 4, 1024], F32R)
        wlo = take("wlo", [P, 4, 1024], F32R)
        xehi = take("xehi", [P, KC, CAP], F32R)
        xelo = take("xelo", [P, KC, CAP], F32R)
        ehhi = take("ehhi", [P, 4, CAP], F32R)
        ehlo = take("ehlo", [P, 4, CAP], F32R)
        both = -(-room[0] // 32) * 32
        egate = take("egate", [CAP, SLAB])
        ehrow = take("ehrow", [CAP, SLAB])
        osb = take("osb", [CAP, D])
        pick = take("pick", [P, TT, CAP])
        spreadw = take("spreadw", [P, TT, CAP])
        spreadwT = take("spreadwT", [CAP, T])
        pairs = take("pairs", [P, TT, NQ_MORE])
        chosen = take("chosen", [P, TT, 8])
        rank = take("rank", [P, TT, 8])
        active = take("active", [NQ_MORE, 1])
        slots = take("slots", [NQ_MORE, MAX_MORE])
        xe32 = nc.alloc_sbuf_tensor_at("xe32", [P, KC, CAP], F32, offset=both)
        assert KC * CAP <= 2 * SLAB

        ssq = sm[:, 0:8]
        rstd = sm[:, 8:16]
        hss = sm[:, 16:40]
        hrs = sm[:, 40:64]
        dec = sm[:, 64:72]
        amax = sm[:, 72:80]
        nmax = sm[:, 80:88]
        sinkd = sm[:, 340:356].rearrange("p (t h) -> p t h", t=2)
        esink = sm[:, 356:372].rearrange("p (t h) -> p t h", t=2)
        den = sm[:, 104:120].rearrange("p (t h) -> p t h", t=2)
        rden = sm[:, 120:128]
        wgt = sm[:, 128:136]
        gates = sm[:, 136:184].rearrange("p (t c) -> p t c", t=2)
        logit = sm[:, 184:200].rearrange("p (t e) -> p t e", t=2)
        top = sm[:, 200:216].rearrange("p (t e) -> p t e", t=2)
        topi = sm[:, 216:232].bitcast(U32).rearrange("p (t e) -> p t e", t=2)
        topf = sm[:, 232:248].rearrange("p (t e) -> p t e", t=2)
        dtop = sm[:, 248:250]
        etop = sm[:, 250:252]
        wtop = sm[:, 252:256].rearrange("p (k t) -> p k t", k=2)
        comb = sm[:, 256:272].rearrange("p (t e) -> p t e", t=2)
        comb2 = sm[:, 272:288].rearrange("p (t e) -> p t e", t=2)
        dsum = sm[:, 288:290]
        hmu = sm[:, 296:304]
        cden = sm[:, 304:320].rearrange("p (t h) -> p t h", t=2)
        cmx = sm[:, 320:336].rearrange("p (t h) -> p t h", t=2)
        ckss = sm[0:64, 336:338]

        x_in = [sem(f"x_in{tt}") for tt in range(TT)]
        ident_in = sem("ident_in")
        first_half_in = sem("first_half_in")
        small_in = sem("small_in")
        late_in = sem("late_in")
        slot_full = [sem(f"slot_full{i}") for i in range(RING)]
        sumsq_ready = sem("sumsq_ready")
        xn_ready = sem("xn_ready")
        xnT_done = sem("xnT_done")
        xT_ready = sem("xT_ready")
        proj_out = sem("proj_out")
        dve_steps = sem("dve_steps")
        act_steps = sem("act_steps")
        pool_steps = sem("pool_steps")
        mhalf_ready = sem("mhalf_ready")
        mean_ready = sem("mean_ready")
        rsqrt_ready = sem("rsqrt_ready")
        masks_ready = sem("masks_ready")
        gT_done = sem("gT_done")
        gT_ready = sem("gT_ready")
        z_done = sem("z_done")
        z_ready = sem("z_ready")
        softplus_ready = sem("softplus_ready")
        la_ready = sem("la_ready")
        cum_done = sem("cum_done")
        decay_ready = sem("decay_ready")
        dl_ready = sem("dl_ready")
        ebl_ready = sem("ebl_ready")
        gla_ops_ready = sem("gla_ops_ready")
        gla_T_done = sem("gla_T_done")
        gla_T_ready = sem("gla_T_ready")
        kv_done = sem("kv_done")
        state_ready = sem("state_ready")
        lin_scores_done = sem("lin_scores_done")
        lin_scores_ready = sem("lin_scores_ready")
        lin_out_done = sem("lin_out_done")
        lin_sq_ready = sem("lin_sq_ready")
        silu_ready = sem("silu_ready")
        head_sq_ready = sem("head_sq_ready")
        head_rows_ready = sem("head_rows_ready")
        dup_ready = sem("dup_ready")
        trig_ready = sem("trig_ready")
        angle_ready = sem("angle_ready")
        head_T_done = sem("head_T_done")
        head_T_ready = sem("head_T_ready")
        scores_done = sem("scores_done")
        nmax_ready = sem("nmax_ready")
        esink_ready = sem("esink_ready")
        probs_ready = sem("probs_ready")
        probsT_done = sem("probsT_done")
        probsT_act = sem("probsT_act")
        probsT_dve = sem("probsT_dve")
        pv_done = sem("pv_done")
        pv_used = sem("pv_used")
        mix_ready = sem("mix_ready")
        mixT_done = sem("mixT_done")
        mixT_ready = sem("mixT_ready")
        h_ready = sem("h_ready")
        lin_used = sem("lin_used")
        gain_done = sem("gain_done")
        gated_ready = sem("gated_ready")
        blk_zero = sem("blk_zero")
        ret_rows_ready = sem("ret_rows_ready")
        ret_T_done = sem("ret_T_done")
        ret_T_ready = sem("ret_T_ready")
        kcT_done = sem("kcT_done")
        blk_ready = sem("blk_ready")
        hid_done = sem("hid_done")
        hid_x = sem("hid_x")
        hid_e = sem("hid_e")
        hid_ready = sem("hid_ready")
        cmp_done = sem("cmp_done")
        ckv_ready = sem("ckv_ready")
        ckT_done = sem("ckT_done")
        ckT_ready = sem("ckT_ready")
        cs_done = sem("cs_done")
        cs_ready = sem("cs_ready")
        ce_ready = sem("ce_ready")
        cp_ready = sem("cp_ready")
        cpT_done = sem("cpT_done")
        cpT_ready = sem("cpT_ready")
        cpv_done = sem("cpv_done")
        gates_ready = sem("gates_ready")
        xhi_ready = sem("xhi_ready")
        xlo_ready = sem("xlo_ready")
        upper_ready = sem("upper_ready")
        lower_ready = sem("lower_ready")
        parts_used = sem("parts_used")
        silu_gate = sem("silu_gate")
        hidden_ready = sem("hidden_ready")
        hhi_ready = sem("hhi_ready")
        hlo_ready = sem("hlo_ready")
        y_added = sem("y_added")
        first_tile_done = sem("first_tile_done")
        router_done = sem("router_done")
        dtop_ready = sem("dtop_ready")
        etop_ready = sem("etop_ready")
        expert_consts_in = sem("expert_consts_in")
        chosen_ready = sem("chosen_ready")
        rank_done = sem("rank_done")
        pick_ready = sem("pick_ready")
        gather_done = sem("gather_done")
        whi_ready = sem("whi_ready")
        wlo_ready = sem("wlo_ready")
        quarter_used = sem("quarter_used")
        egate_ready = sem("egate_ready")
        ehrow_ready = sem("ehrow_ready")
        ehT_done = sem("ehT_done")
        ehhi_ready = sem("ehhi_ready")
        ehlo_ready = sem("ehlo_ready")
        xe32_ready = sem("xe32_ready")
        xehi_ready = sem("xehi_ready")
        xelo_ready = sem("xelo_ready")
        spreadw_ready = sem("spreadw_ready")
        spreadwT_done = sem("spreadwT_done")
        spreadwT_ready = sem("spreadwT_ready")
        o_ready = sem("o_ready")
        scatter_done = sem("scatter_done")
        y_used = sem("y_used")
        count_done = sem("count_done")
        active_ready = sem("active_ready")
        place_done = sem("place_done")
        slots_ready = sem("slots_ready")
        list_done = sem("list_done")
        list_ready = sem("list_ready")
        list_pairs_ready = sem("list_pairs_ready")
        moe_done = sem("moe_done")
        stored = sem("stored")

        block = ctx.enter_context(nc.Block())

        SMALL = 16 * 3
        QUARTERS, (IN0_Q, OUT0_Q, FFN_Q, IN1_Q, OUT1_Q) = split_quarters()

        def rows(ap):
            return ap.rearrange("(k p) n -> p k n", p=P)

        def slot3(n, k):
            return ring[:, place(n), :].rearrange("p (k n) -> p k n", k=k)

        def item_of(eng, k):
            def read(n, top_):
                return eng.value_load(items[0:1, bass.ds(k + n * MAX_MORE, 1)], min_val=0, max_val=top_)
            return read(2, 1), read(0, N_EXPERTS - 1), read(1, CAP * (PARTS - 1))

        def any_item(eng):
            return eng.value_load(items[0:1, 2 * MAX_MORE:2 * MAX_MORE + 1], min_val=0, max_val=1)

        @block.sync
        def _(sp):
            def load(n, src):
                k, cols = src.shape[1], src.shape[2]
                dst = ring[:, place(n), 0:k * cols].rearrange("p (k n) -> p k n", k=k)
                sp.dma_start(dst, src).then_inc(slot_full[place(n)], 16)

            def ffn_src(kind, j, wg, wu, wd, tiles):
                lo, hi = SLAB * j, min(SLAB * (j + 1), tiles * P)
                if kind == "down":
                    return rows(wd[lo:hi, :])
                return rows((wg if kind == "gate" else wu)[:, lo:hi])

            def wait_free(n):
                earlier = [m for m in range(n) if place(m) == place(n)]
                if place(n) == STAGE and n < L0_FFN:
                    sp.wait_ge(parts_used, OUT0_Q)
                elif place(n) == STAGE and n >= MOE:
                    sp.wait_ge(parts_used, OUT1_Q)
                elif earlier and earlier[-1] in (L1_PROJ + L1_ORDER.index(-1), L1_PROJ + L1_ORDER.index(-2)):
                    sp.wait_ge(hid_done, -L1_ORDER[earlier[-1] - L1_PROJ])
                elif earlier:
                    sp.wait_ge(parts_used, sum(slot <= earlier[-1] for slot, _, _, _ in QUARTERS))

            sp.dma_start(con[:, C_ID:C_ID + P], consts[:, C_ID:C_ID + P]).then_inc(ident_in, 16)
            sp.dma_start(col[:, :], colv).then_inc(ident_in, 16)
            for tt in range(TT):
                sp.dma_start(h[:, tt, :], x[tt * P:(tt + 1) * P, :]).then_inc(x_in[tt], 16)
            first = rows(w["w_in_e"][0, :, SLAB * L0_ORDER[0]:SLAB * (L0_ORDER[0] + 1)])
            for half, signal in enumerate((first_half_in, slot_full[0])):
                k = slice(half * KC // 2, (half + 1) * KC // 2)
                sp.dma_start(ring[:, 0, :].rearrange("p (k n) -> p k n", k=KC)[:, k, :],
                             first[:, k, :]).then_inc(signal, 16)
            sp.dma_start(con[:, C_ID + P:NC], consts[:, C_ID + P:NC]).then_inc(small_in, 16)
            sp.dma_start(row[:, :], rowv.partition_broadcast(P)).then_inc(small_in, 16)
            sp.dma_start(posi[:, :], pos).then_inc(small_in, 16)
            n = 1
            for s in L0_ORDER[1:]:
                wait_free(n)
                load(n, rows(w["w_in_e"][0, :, SLAB * s:min(SLAB * (s + 1), L0_IN)]))
                n += 1
            for s in range(2):
                wait_free(n)
                load(n, rows(w["w_out_e"][0, :, SLAB * s:SLAB * (s + 1)]))
                n += 1
            for kind, j in ffn_order(FFN_SLABS):
                wait_free(n)
                load(n, ffn_src(kind, j, w["ffn_w_gate"][0], w["ffn_w_up"][0], w["ffn_w_down"][0], FFN_TILES))
                n += 1
            for s in L1_ORDER:
                wait_free(n)
                if s < 0:
                    load(n, rows(w["cmp_w1_k" if s == -1 else "cmp_w1_v"][0]))
                else:
                    load(n, rows(w["w_in_o"][0, :, SLAB * s:min(SLAB * (s + 1), L1_IN)]))
                n += 1
            for s in range(2):
                wait_free(n)
                load(n, rows(w["w_out_o"][0, :, SLAB * s:SLAB * (s + 1)]))
                n += 1

            order = ffn_order(MOE_SLABS)

            def load_expert(e, r):
                kind, j = order[r]
                name = {"gate": "exp_w_gate", "up": "exp_w_up", "down": "exp_w_down"}[kind]
                if kind == "down":
                    src = w[name][0, bass.ds(e, 1), SLAB * j:SLAB * (j + 1), :]
                else:
                    src = w[name][0, bass.ds(e, 1), :, SLAB * j:SLAB * (j + 1)]
                src = src.rearrange("a k n -> (a k) n")
                load(MOE + r, rows(src))

            for r in range(RING):
                wait_free(MOE + r)
                load_expert(0, r)

            def wait_split(i, r):
                sp.wait_ge(wlo_ready, i * 4 * MOE_SLOTS + 4 * (r + 1))

            def rest_of_expert(e):
                for r in range(RING, MOE_SLOTS):
                    wait_split(e, r - RING)
                    load_expert(e, r)

            with sp.Fori(0, N_EXPERTS - 1) as e:
                rest_of_expert(e)
                for r in range(RING):
                    wait_split(e, MOE_SLOTS - RING + r)
                    load_expert(e + 1, r)
            rest_of_expert(N_EXPERTS - 1)
            sp.wait_ge(y_used, TT * N_EXPERTS)
            sp.wait_ge(list_ready, 1)
            with sp.If(any_item(sp) > 0):
                with sp.Fori(0, MAX_MORE) as k:
                    used, e, _ = item_of(sp, k)
                    i = k + N_EXPERTS
                    with sp.If(used > 0):
                        for r in range(MOE_SLOTS):
                            wait_split(i - 1 if r < RING else i, (r - RING) % MOE_SLOTS)
                            load_expert(e, r)
            sp.wait_ge(moe_done, 1)
            sp.dma_start(out.rearrange("(t p) n -> p t n", p=P), h[:, :, :]).then_inc(stored, 16)
            sp.wait_ge(stored, 16)

        UNITS = [(tt, 1024, SV, 0, None) for tt in range(TT)]
        UNITS += [(tt, 1024, VS_, 1, 1) for tt in range(TT)]
        UNITS += [(tt, 1536, VW_, 1, 2) for tt in range(TT)]
        groups_before = [0]
        for u in UNITS:
            groups_before.append(groups_before[-1] + 2 * (u[0] + 1))
        xnf = xn[:, :, :].rearrange("p t c -> p (t c)")
        probs = (xT[:, :, :],
                 ws[:, 0:2048].rearrange("p (h k) -> p h k", h=8))
        probsT = ws[:, 2048:4096].rearrange("p (k h t) -> p k h t", k=2, h=8)
        qT = qkT[:, 0:1024].rearrange("p (j t) -> p j t", j=4)

        def head_of(bank, i, per):
            half = 4 // per
            return 2 * ((bank % half) * per + i) + bank // half

        la = ws[:, 0:512].rearrange("p (t c) -> p t c", t=TT)
        eb = ws[:, 512:1024].rearrange("p (t c) -> p t c", t=TT)
        enb = ws[:, 1024:1536].rearrange("p (t c) -> p t c", t=TT)
        ebl = ws[:, 1536:2048].rearrange("p (t c) -> p t c", t=TT)
        qin = ws[:, 2048:2560].rearrange("p (t c) -> p t c", t=TT)
        kin = ws[:, 2560:3072].rearrange("p (t c) -> p t c", t=TT)
        kst = ws[:, 3072:3584].rearrange("p (t c) -> p t c", t=TT)
        tmp = ws[:, 3584:4096].rearrange("p (t c) -> p t c", t=TT)
        state = ws[:, 0:1536].rearrange("p (c h v) -> p c h v", c=3, h=4)
        linT = {0: [pr[:, i, L0_IN:L0_IN + 512].rearrange("p (j t) -> p j t", j=2) for i in range(2)],
                1: [pr[:, i, RQ:RQ + 512].rearrange("p (j t) -> p j t", j=2) for i in range(2)]}
        glasc = ws[:, 2048:3072].rearrange("p (r t j q) -> p r t j q", r=2, t=TT, j=2)
        retsc = ws[:, 1024:2560].rearrange("p (b h q) -> p b h q", b=3, h=4)
        linsq = {0: ws[:, 3072:4096].rearrange("p (t c) -> p t c", t=TT),
                 1: ws[:, 2560:3584].rearrange("p (t c) -> p t c", t=TT)}
        headsq = xnf[:, 0:1536]
        dup = xnf[:, 1024:2048].rearrange("p (t g d c) -> p t g d c", t=TT, g=4, d=2)
        rtmp = xnf[:, 0:1024]
        blk = ws[:, 0:2048].rearrange("p (v l c) -> p v l c", v=2, l=16)
        hidx = xnf[:, 0:256].rearrange("p (v c) -> p v c", v=2)
        hide = xnf[:, 256:512].rearrange("p (v c) -> p v c", v=2)
        hid = xnf[:, 512:768].rearrange("p (v c) -> p v c", v=2)
        ckdup = xnf[0:64, 768:896]
        cktmp = xnf[0:64, 896:1024]
        csm = ws[:, 3072:3328].rearrange("p (t x) -> p t x", t=TT)
        cpd = ws[:, 3328:3840].rearrange("p (t x) -> p t x", t=TT)
        cpT = ws[0:64, 0:1024].rearrange("p (t j q) -> p t j q", t=TT, j=4)
        x32 = qkT[:, :].rearrange("p (k t) -> p k t", k=KC)
        h32 = ws[:, 2048:4096].rearrange("p (i t) -> p i t", i=8)

        def sg(i):
            return pr[:, i // 2, 2048 + i % 2 * T:2048 + (i % 2 + 1) * T]

        def in_width(slot, slab):
            return min(SLAB, (L0_IN if slot < L0_OUT else L1_IN) - SLAB * slab)

        def quarter(n, lower):
            slot, kind, j, i = QUARTERS[n]
            at = place(slot)
            flat = flo[at][:, :] if lower else ring[:, at, :]
            if kind in ("down", "out"):
                return flat[:, i * D:(i + 1) * D].rearrange("p (k c) -> p k c", k=2)
            if kind == "in":
                c = in_width(slot, j)
                return flat[:, 2 * i * c:2 * (i + 1) * c].rearrange("p (k c) -> p k c", k=2)
            width = P * len(tiles_of(j, FFN_TILES))
            return flat[:, 0:KC * width].rearrange("p (k c) -> p k c", k=KC)[:, :, i * P:(i + 1) * P]

        def upper(n):
            slot, kind, j, _ = QUARTERS[n]
            if kind == "in":
                c = in_width(slot, j)
                return pstage[n % 4][:, 0:2 * c].rearrange("p (k c) -> p k c", k=2)
            return fhi[n % 4][:, :].rearrange("p (k c) -> p k c", k=2 if kind in ("down", "out") else KC)
        econ = con[:, C_RD:C_RD + ND]

        @block.tensor
        def _(pe):
            mm = nc.tensor.matmul

            def slot_wait(n, e=None):
                k = 16 * fills(n)
                pe.wait_ge(slot_full[place(n)], k if e is None else e * (16 * MOE_SLOTS // RING) + k)

            def turn_input(rows_, ready):
                for tt in range(TT):
                    pe.wait_ge(*ready[tt])
                    for b in range(2):
                        for c in range(4):
                            last = nc.tensor.transpose(ps[4 + 2 * tt + b][:, c * P:(c + 1) * P],
                                                       rows_[:, tt, (4 * b + c) * P:(4 * b + c + 1) * P], ident)
                        last.then_inc(xnT_done, 1)

            def project(i, order, n0, x_lo, x_count, copied):
                before = sum(s >= 0 for s in order[:i])
                if before >= 2:
                    pe.wait_ge(proj_out, copied + 2 * before - 2)
                for n in range(n0 + 4 * before, n0 + 4 * before + 4):
                    slot, _, _, q = QUARTERS[n]
                    if before == 0 and q % 2 == 0:
                        pe.wait_ge(xlo_ready, x_count + 2 + q)
                    pe.wait_ge(lower_ready, n + 1)
                    w_hi, w_lo = upper(n), quarter(n, True)
                    for tt in range(TT):
                        bank = ps[(copied + 2 * before + tt) % 4][:, 0:w_hi.shape[2]]
                        for k in range(2):
                            a, b = (v[:, 2 * q + k, tt * P:(tt + 1) * P] for v in (xhi, x_lo))
                            mm(bank, a, w_hi[:, k, :], start=(q == k == 0), stop=False)
                            mm(bank, a, w_lo[:, k, :], start=False, stop=False)
                            last = mm(bank, b, w_hi[:, k, :], start=False, stop=(2 * q + k == KC - 1))
                    last.then_inc(parts_used, 1)

            def project0(i):
                project(i, L0_ORDER, IN0_Q, xlo, 0, 0)

            def project1(i):
                project(i, L1_ORDER, IN1_Q, xlo1, 12, 10)

            def turn_mix(layer, tt):
                pe.wait_ge(gated_ready, TT * layer + tt + 1)
                if layer == 0:
                    pe.wait_ge(pv_used, tt + 1)
                else:
                    pe.wait_ge(mix_ready, tt + 2)
                for b in range(2):
                    for c in range(4):
                        last = nc.tensor.transpose(ps[4 * tt + b][:, c * P:(c + 1) * P],
                                                   mix[:, tt, (4 * b + c) * P:(4 * b + c + 1) * P], ident)
                    last.then_inc(mixT_done, 1)

            def out_projection(layer):
                turn_mix(layer, 1)
                n0 = (OUT0_Q, OUT1_Q)[layer]
                for n in range(n0, n0 + 8):
                    slot, _, s, i = QUARTERS[n]
                    if s == 0 and i % 2 == 0:
                        pe.wait_ge(xlo_ready, (4, 16)[layer] + 3 + i // 2)
                    pe.wait_ge(lower_ready, n + 1)
                    w_hi, w_lo = upper(n), quarter(n, True)
                    for tt in range(TT):
                        bank = ps[2 * s + tt][:, :]
                        for k in range(2):
                            a, b = (v[:, 2 * i + k, tt * P:(tt + 1) * P] for v in (xhi, xlo))
                            mm(bank, a, w_hi[:, k, :], start=(i == k == 0), stop=False)
                            mm(bank, a, w_lo[:, k, :], start=False, stop=False)
                            last = mm(bank, b, w_hi[:, k, :], start=False, stop=(2 * i + k == KC - 1))
                        if (s, i, tt) == (1, 3, 0):
                            last.then_inc(first_tile_done, 1)
                    last.then_inc(parts_used, 1)

            def scores(n):
                tt, k0, _, mask, _ = UNITS[n]
                kT = qkT[:, k0:k0 + 512].rearrange("p (g t) -> p g t", g=2)
                keys = P * (tt + 1)
                per = 512 // keys
                for b in range(8 // per):
                    bank = ps[b][:, :].rearrange("p (h k) -> p h k", h=per)
                    m = mbf[:, mask, T - keys:T]
                    mm(bank, idb[:, :], spread(m, 1, per), start=True, stop=False)
                    for i in range(per):
                        hh = head_of(b, i, per)
                        r = 64 * (hh % 2)
                        last = mm(bank[:, i, :], qT[r:r + 64, hh // 2, tt * P:(tt + 1) * P],
                                  kT[r:r + 64, hh // 4, 0:keys], start=False, stop=(i == per - 1))
                last.then_inc(scores_done, 1)

            def attend(n, another):
                tt, _, v0, _, _ = UNITS[n]
                pe.wait_ge(probs_ready, n + 1)
                if another:
                    scores(n + 1)
                g = groups_before[n]
                for kt in range(tt + 1):
                    for quad in range(2):
                        if g >= 2:
                            pe.wait_ge(probsT_act if g % 2 == 0 else probsT_dve, g // 2)
                        for i in range(4):
                            last = nc.tensor.transpose(ps[4 + g % 2][:, i * P:(i + 1) * P],
                                                       probs[n % 2][:, 4 * quad + i, kt * P:(kt + 1) * P], ident)
                        last.then_inc(probsT_done, 1)
                        g += 1
                if not another:
                    turn_mix(int(n > 1), 0)
                pe.wait_ge(probsT_act, g // 2)
                pe.wait_ge(probsT_dve, g // 2)
                if n:
                    pe.wait_ge(pv_used, n)
                else:
                    pe.wait_ge(lin_used, 2)
                for hh in range(8):
                    for kt in range(tt + 1):
                        c = v0 + HD * (hh // 4)
                        last = mm(ps[6][:, hh * HD:(hh + 1) * HD], probsT[:, kt, hh, :],
                                  pr[:, kt, c:c + HD], start=(kt == 0), stop=(kt == tt))
                last.then_inc(pv_done, 1)

            def feed_forward():
                for n in range(FFN_Q, IN1_Q):
                    slot, kind, j, i = QUARTERS[n]
                    tile = 4 * j + i
                    pe.wait_ge(lower_ready, n + 1)
                    if kind == "down":
                        pe.wait_ge(hlo_ready, tile + 1)
                        cols = slice(i * D, (i + 1) * D)
                        whi_, wlo_ = fhi[n % 4][:, :], flo[place(slot)][:, cols]
                        for tt in range(TT):
                            a, b = (v[:, tile % 8, tt * P:(tt + 1) * P] for v in (hhi, hlo))
                            for half in range(2):
                                c = slice(half * 512, (half + 1) * 512)
                                bank = ps[4 + 2 * tt + half][:, :]
                                mm(bank, a, whi_[:, c], start=(tile == 0), stop=False)
                                mm(bank, a, wlo_[:, c], start=False, stop=False)
                                last = mm(bank, b, whi_[:, c], start=False, stop=(tile == FFN_TILES - 1))
                            if (tile, tt) == (FFN_TILES - 1, 0):
                                last.then_inc(first_tile_done, 1)
                    else:
                        if kind == "up":
                            pe.wait_ge(silu_gate, tile + 1)
                        elif j:
                            pe.wait_ge(hidden_ready, tile - 3)
                        whi_, wlo_ = upper(n), quarter(n, True)
                        c = T * (kind == "up")
                        bank = ps[i][:, c:c + T]
                        for k in range(KC):
                            if n == FFN_Q and k == 4:
                                pe.wait_ge(xlo_ready, 12)
                            mm(bank, whi_[:, k, :], xhi[:, k, :], start=(k == 0), stop=False)
                            mm(bank, whi_[:, k, :], xlo[:, k, :], start=False, stop=False)
                            last = mm(bank, wlo_[:, k, :], xhi[:, k, :], start=False, stop=(k == KC - 1))
                    last.then_inc(parts_used, 1)

            def linear_scores(layer, banks, at, q_tt, k_tt):
                linqT, linkT = linT[layer]
                for hh in range(4):
                    r = 64 * (hh % 2)
                    c = (2 * at + hh // 2) * P
                    last = mm(banks[hh % 2][:, c:c + P], linkT[r:r + 64, hh // 2, k_tt * P:(k_tt + 1) * P],
                              linqT[r:r + 64, hh // 2, q_tt * P:(q_tt + 1) * P], start=True, stop=True)
                last.then_inc(lin_scores_done, 1)

            pe.wait_ge(ident_in, 32)
            turn_input(h, [(x_in[tt], 16) for tt in range(TT)])
            project0(0)
            project0(1)
            pe.wait_ge(proj_out, 2)
            for tt in range(TT):
                last = nc.tensor.transpose(ps[4][0:16, tt * P:(tt + 1) * P], pr[:, tt, GLOW:GLOW + 16], ident)
            last.then_inc(gT_done, 1)
            project0(2)
            pe.wait_ge(gT_ready, 1)
            pe.wait_ge(late_in, 64)
            for tt in range(TT):
                last = mm(ps[5][:, tt * 256:(tt + 1) * 256], gT[:, tt * P:(tt + 1) * P], gup[:, :],
                          start=True, stop=True)
            last.then_inc(z_done, 1)
            project0(3)
            pe.wait_ge(la_ready, 1)
            for tt in range(TT):
                mm(ps[6][:, tt * 256:(tt + 1) * 256], tri, la[:, tt, :], start=True, stop=True)
                mm(ps[7][:, tt * 256:(tt + 1) * 256], same, la[:, tt, :], start=True, stop=True)
                for hp in range(2):
                    c = 4 * hp + 2 * tt
                    last = mm(ps[4][:, c:c + 2], la[:, tt, hp * P:(hp + 1) * P], con[:, C_CH:C_CH + 2],
                              start=True, stop=True)
            last.then_inc(cum_done, 1)
            project0(4)
            pe.wait_ge(gla_ops_ready, 1)
            pe.wait_ge(proj_out, 8)
            for src, bank in ((qin, ps[2]), (kin, ps[3])):
                for hp in range(2):
                    for tt in range(TT):
                        c = (2 * hp + tt) * P
                        last = nc.tensor.transpose(bank[:, c:c + P], src[:, tt, hp * P:(hp + 1) * P], ident)
                last.then_inc(gla_T_done, 1)
            pe.wait_ge(proj_out, 10)
            for c in range(3):
                r = 64 * (c % 2)
                for hp in range(2):
                    last = mm(ps[5 + c][:, hp * 256:(hp + 1) * 256], kst[r:r + 64, c // 2, hp * P:(hp + 1) * P],
                              pr[r:r + 64, c // 2, GV + hp * 256:GV + (hp + 1) * 256], start=True, stop=True)
            last.then_inc(kv_done, 1)
            pe.wait_ge(gla_T_ready, 2)
            for tt in range(TT):
                linear_scores(0, ps[0:2], tt, tt, tt)

            def turn_q(c0, banks):
                for j in range(4):
                    for tt in range(TT):
                        c = (2 * (j % 2) + tt) * P
                        last = nc.tensor.transpose(banks[j // 2][:, c:c + P],
                                                   pr[:, tt, c0 + j * P:c0 + (j + 1) * P], ident)
                    if j % 2:
                        last.then_inc(head_T_done, 1)

            def turn_k(banks):
                for g in range(2 * len(banks)):
                    for tt in range(TT):
                        c = (2 * (g % 2) + tt) * P
                        src = dup[:, tt, g, :, :].rearrange("p d c -> p (d c)")
                        last = nc.tensor.transpose(banks[g // 2][:, c:c + P], src, ident)
                    if g % 2:
                        last.then_inc(head_T_done, 1)

            pe.wait_ge(head_rows_ready, 1)
            turn_q(SQ, ps[2:4])
            pe.wait_ge(dup_ready, 1)
            turn_k(ps[4:5])
            pe.wait_ge(lin_scores_ready, 2)
            pe.wait_ge(head_T_ready, 3)
            pe.wait_ge(masks_ready, 3)
            scores(0)
            pe.wait_ge(state_ready, 1)
            linqT = linT[0][0]
            for tt in range(TT):
                for hh in range(4):
                    for c in range(2 * tt, 2 * tt + 2):
                        t0 = 64 * (c % 2)
                        o = ps[6 + tt][t0:t0 + 64, hh * P:(hh + 1) * P]
                        last = mm(o, glasc[:, hh % 2, tt, hh // 2, t0:t0 + 64],
                                  pr[:, tt, GV + hh * P:GV + (hh + 1) * P], start=True, stop=(c == 0))
                        if c:
                            last = mm(o, linqT[:, hh // 2, c * 64:(c + 1) * 64], state[:, c - 1, hh, :],
                                      start=False, stop=True)
                last.then_inc(lin_out_done, 1)
            attend(0, True)
            attend(1, False)
            out_projection(0)
            turn_input(xn, [(xn_ready, 1), (xn_ready, 2)])
            pe.wait_ge(xlo_ready, 10)
            feed_forward()

            turn_input(h, [(y_added, 1), (y_added, 2)])
            for i in range(4):
                project1(i)
            for i in range(2):
                for tt in range(TT):
                    last = nc.tensor.transpose(ps[6 + i][:, tt * P:(tt + 1) * P],
                                               pr[:, tt, KC_ + i * P:KC_ + (i + 1) * P], ident)
                last.then_inc(kcT_done, 1)
            project1(4)
            pe.wait_ge(head_rows_ready, 2)
            turn_q(NQ, ps[4:6])
            pe.wait_ge(blk_ready, 2)
            for i in range(2):
                slot_wait(L1_PROJ + 5 + i)
                w1 = slot3(L1_PROJ + 5 + i, 16)
                for ht in range(2):
                    for l in range(16):
                        c = (2 * i + ht) * 64
                        last = mm(ps[6][:, c:c + 64], w1[:, l, ht * P:(ht + 1) * P],
                                  blk[:, i, l, :], start=(l == 0), stop=(l == 15))
                last.then_inc(hid_done, 1)
            pe.wait_ge(dup_ready, 2)
            pe.wait_ge(head_T_ready, 5)
            turn_k(ps[4:6])
            project1(7)
            pe.wait_ge(ret_rows_ready, 1)
            pe.wait_ge(head_T_ready, 7)
            for i, bank in ((0, ps[4]), (1, ps[5])):
                for hp in range(2):
                    for tt in range(TT):
                        c = (2 * hp + tt) * P
                        src = pr[:, tt, RQ + 256 * i + hp * P:RQ + 256 * i + (hp + 1) * P]
                        last = nc.tensor.transpose(bank[:, c:c + P], src, ident)
                last.then_inc(ret_T_done, 1)
            pe.wait_ge(hid_ready, 1)
            for i in range(2):
                for ht in range(2):
                    last = mm(ps[7][0:64, i * HD:(i + 1) * HD], hid[:, i, ht * 64:(ht + 1) * 64], w2[:, i, ht, :],
                              start=(ht == 0), stop=(ht == 1))
            last.then_inc(cmp_done, 1)
            pe.wait_ge(ret_T_ready, 2)
            pe.wait_ge(proj_out, 22)
            linear_scores(1, ps[0:2], 0, 0, 0)
            linear_scores(1, ps[0:2], 1, 1, 1)
            linear_scores(1, ps[2:4], 0, 1, 0)
            pe.wait_ge(ckv_ready, 1)
            nc.tensor.transpose(ps[6][:, 0:64], ckdup, ident[0:64, 0:64]).then_inc(ckT_done, 1)
            pe.wait_ge(lin_scores_ready, 2 + 6)
            for tt in range(TT):
                for hh in range(4):
                    blocks = [(0, 0)] if tt == 0 else [(1, 1), (2, 0)]
                    for n, (b, kt) in enumerate(blocks):
                        last = mm(ps[4 + tt][:, hh * P:(hh + 1) * P], retsc[:, b, hh, :],
                                  pr[:, kt, RV + hh * P:RV + (hh + 1) * P], start=(n == 0), stop=(n == tt))
                last.then_inc(lin_out_done, 1)
            pe.wait_ge(ckT_ready, 1)
            for tt in range(TT):
                for hh in range(8):
                    r, g = 64 * (hh % 2), hh // 4
                    c = 64 * tt + (hh % 4 // 2 * 2 + g) * 16
                    last = mm(ps[6 + hh % 2][:, c:c + NCMP], qT[r:r + 64, hh // 2, tt * P:(tt + 1) * P],
                              kcT[r:r + 64, 32 * g:32 * g + NCMP], start=True, stop=True)
            last.then_inc(cs_done, 1)
            scores(2)
            pe.wait_ge(cp_ready, 1)
            for tt in range(TT):
                for j in range(4):
                    last = nc.tensor.transpose(ps[6 + tt][0:64, j * P:(j + 1) * P], cpd[:, tt, j * 64:(j + 1) * 64],
                                               ident)
                last.then_inc(cpT_done, 1)
            pe.wait_ge(cpT_ready, 2)
            for tt in range(TT):
                for hh in range(8):
                    g, j = hh // 4, 2 * (hh % 2) + hh % 4 // 2
                    c = 256 * tt + (hh % 4) * HD
                    last = mm(ps[2 + g][:, c:c + HD], cpT[32 * g:32 * g + 32, tt, j, :],
                              cv[32 * g:32 * g + 32, 1, :], start=True, stop=True)
                last.then_inc(cpv_done, 1)
            pe.wait_ge(mix_ready, 1)
            pe.wait_ge(lin_used, 4)
            for n in range(2, 6):
                attend(n, n < 5)
            out_projection(1)
            turn_input(h, [(h_ready, 7), (h_ready, 8)])
            pe.wait_ge(xT_ready, 16)
            for tt in range(TT):
                for k in range(KC):
                    last = mm(ps[0][:, tt * 8:(tt + 1) * 8], xT[:, k, tt * P:(tt + 1) * P], rw[:, k, :],
                              start=(k == 0), stop=(k == KC - 1))
            last.then_inc(router_done, 1)
            pe.wait_ge(expert_consts_in, 16)
            pe.wait_ge(chosen_ready, 1)
            mm(ps[1][:, 0:8], econ[:, D_SU:D_SU + P], chosen[:, 0, :], start=True, stop=True)
            mm(ps[1][:, 8:16], econ[:, D_SU:D_SU + P], chosen[:, 1, :], start=True, stop=False)
            mm(ps[1][:, 8:16], econ[:, D_ONE:D_ONE + P], chosen[:, 0, :], start=False, stop=True).then_inc(rank_done, 1)

            def gather(i, added):
                pe.wait_ge(pick_ready, i + 1)
                pe.wait_ge(xn_ready, 4)
                if added is not None:
                    pe.wait_ge(y_used, added)
                for c in range(KC):
                    for tt in range(TT):
                        last = mm(ps[4 + c // 4][:, c % 4 * CAP:(c % 4 + 1) * CAP], xn[:, tt, c * P:(c + 1) * P],
                                  pick[:, tt, :], start=(tt == 0), stop=(tt == 1))
                last.then_inc(gather_done, 1)

            def scatter(i):
                pe.wait_ge(o_ready, 2 * i + 2)
                pe.wait_ge(spreadwT_ready, i + 1)
                for tt in range(TT):
                    for half in range(2):
                        last = mm(ps[6 - 2 * tt + half][:, :], spreadwT[:, tt * P:(tt + 1) * P],
                                  osb[:, half * 512:(half + 1) * 512], start=True, stop=True)
                    last.then_inc(scatter_done, 1)

            def expert(i, scatter_before, gather_next, more):
                q0 = i * 4 * MOE_SLOTS

                def product(bank, hi, lo, q, n, start, stop):
                    cols = slice(n * 512, (n + 1) * 512)
                    mm(bank, hi, whi[:, q, cols], start=start, stop=False)
                    mm(bank, lo, whi[:, q, cols], start=False, stop=False)
                    return mm(bank, hi, wlo[:, q, cols], start=False, stop=stop)

                def gate_or_up(r, bank):
                    for q in range(4):
                        pe.wait_ge(wlo_ready, q0 + (4 * r + q + 1))
                        for n in range(2):
                            k = 2 * q + n
                            last = product(bank[0:CAP, :], xehi[:, k, :], xelo[:, k, :], q, n, k == 0, k == KC - 1)
                        last.then_inc(quarter_used, 1)

                def turn_hidden(j):
                    pe.wait_ge(ehrow_ready, i * MOE_SLABS + j + 1)
                    for f in range(4):
                        last = nc.tensor.transpose(ps[7][:, f * CAP:(f + 1) * CAP], ehrow[:, f * P:(f + 1) * P],
                                                   ident[0:CAP, 0:CAP])
                    last.then_inc(ehT_done, 1)

                def down(j):
                    r = down_slot(j, MOE_SLABS)
                    pe.wait_ge(ehlo_ready, i * MOE_SLABS + j + 1)
                    for f in range(4):
                        pe.wait_ge(wlo_ready, q0 + (4 * r + f + 1))
                        for half in range(2):
                            last = product(ps[2 + half][0:CAP, :], ehhi[:, f, :], ehlo[:, f, :], f, half,
                                           (j, f) == (0, 0), (j, f) == (MOE_SLABS - 1, 3))
                        last.then_inc(quarter_used, 1)

                pe.wait_ge(xelo_ready, i + 1)
                for j in range(MOE_SLABS):
                    if j:
                        pe.wait_ge(egate_ready, i * MOE_SLABS + j)
                    gate_or_up(gate_slot(j), ps[0])
                    if j == 1 and scatter_before:
                        pe.wait_ge(y_used, i * 2)
                    if j:
                        turn_hidden(j - 1)
                    gate_or_up(up_slot(j), ps[1])
                    if j == 0 and scatter_before:
                        scatter(i - 1)
                    if j == 0 and more:
                        pe.wait_ge(y_used, i * 2)
                    if j == 3:
                        pe.wait_ge(spreadw_ready, i + 1)
                        for tt in range(TT):
                            last = nc.tensor.transpose(ps[6][0:CAP, tt * P:(tt + 1) * P], spreadw[:, tt, :], ident)
                        last.then_inc(spreadwT_done, 1)
                    if j == 1 and (scatter_before or more):
                        pe.wait_ge(o_ready, i * 2)
                    if j:
                        down(j - 1)
                turn_hidden(MOE_SLABS - 1)
                if gather_next:
                    gather(i + 1, None)
                down(MOE_SLABS - 1)

            gather(0, None)
            expert(0, False, True, False)
            pe.wait_ge(list_pairs_ready, 1)
            for tt in range(TT):
                last = mm(ps[7][0:NQ_MORE, 0:1], pairs[:, tt, :], econ[:, D_ONE:D_ONE + 1], start=(tt == 0), stop=(tt == 1))
            last.then_inc(count_done, 1)
            pe.wait_ge(active_ready, 1)
            mm(ps[7][0:NQ_MORE, 1:2], econ[0:NQ_MORE, D_LOW:D_LOW + NQ_MORE], active[:, :], start=True,
               stop=True).then_inc(place_done, 1)
            pe.wait_ge(slots_ready, 1)
            for n, c in enumerate((D_QE, D_QS, D_ONE)):
                last = mm(ps[7][0:1, 16 + n * MAX_MORE:16 + (n + 1) * MAX_MORE], econ[0:NQ_MORE, c:c + 1], slots[:, :],
                          start=True, stop=True)
            last.then_inc(list_done, 1)
            pe.wait_ge(list_ready, 1)
            with pe.Fori(1, N_EXPERTS - 1) as i:
                expert(i, True, True, False)
            expert(N_EXPERTS - 1, True, False, False)
            scatter(N_EXPERTS - 1)
            with pe.If(any_item(pe) > 0):
                with pe.Fori(0, MAX_MORE) as k:
                    used, _, _ = item_of(pe, k)
                    with pe.If(used > 0):
                        i = k + N_EXPERTS
                        gather(i, i * 2)
                        expert(i, False, False, True)
                        scatter(i)

        @block.scalar
        def _(act):
            A = nc.scalar.activation
            steps = [0]

            def step(ins):
                steps[0] += 1
                ins.then_inc(act_steps, 1)

            def settle():
                act.wait_ge(act_steps, steps[0])

            act.wait_ge(ident_in, 32)
            A(idb[:, :], ident, ACT.Copy).then_inc(masks_ready, 1)
            act.wait_ge(x_in[0], 16)
            act.dma_start(gup[:, :], w["gla_gate_up"][0]).then_inc(late_in, 16)
            act.dma_start(w2[:, 0, :, :], rows(w["cmp_w2_k"][0])).then_inc(late_in, 16)
            act.dma_start(w2[:, 1, :, :], rows(w["cmp_w2_v"][0])).then_inc(late_in, 16)
            act.dma_start(rw[:, :, :], rows(w["router_w"][0])).then_inc(late_in, 16)

            def sums_of_squares(k):
                for tt in range(TT):
                    c = TT * k + tt
                    A(xn[:, tt, :], h[:, tt, :], ACT.Square, accum_out=ssq[:, c:c + 1]).then_inc(sumsq_ready, 1)

            def copy_projection(u, pieces):
                c = 0 if u < 10 else 2 * TT
                done = IN0_Q + 2 * u + 4 if u < 10 else IN1_Q + 2 * (u - 10) + 4
                for tt in range(TT):
                    act.wait_ge(parts_used, done)
                    for n, (src, dst, width) in enumerate(pieces):
                        ins = A(pr[:, tt, dst:dst + width], ps[(u + tt) % 4][:, src:src + width], ACT.Copy,
                                scale=rstd[:, c + tt:c + tt + 1])
                    ins.then_inc(proj_out, 1)

            def copy0(i):
                s = L0_ORDER[i]
                copy_projection(2 * i, [(0, SLAB * s, min(SLAB, L0_IN - SLAB * s))])

            def copy1(i):
                s = L1_ORDER[i]
                pieces = {4: [(0, KC_, 256), (256, KS_, 128), (384, VS_, 128)],
                          5: [(0, KW_, 128), (128, VW_, 152)]}.get(s, [(0, SLAB * s, SLAB)])
                copy_projection(10 + 2 * sum(x >= 0 for x in L1_ORDER[:i]), pieces)

            def head_squares(c0, heads):
                v = headsq[:, 0:TT * heads * HD].rearrange("p (t c) -> p t c", t=TT)
                A(v, pr[:, :, c0:c0 + heads * HD], ACT.Square).then_inc(head_sq_ready, 1)

            def copy_turned(first, banks):
                for i, (b, c) in enumerate(banks):
                    act.wait_ge(head_T_done, first + i + 1)
                    A(qkT[:, c:c + 512], ps[b][:, :], ACT.Copy).then_inc(head_T_ready, 1)

            def exps(n):
                tt = UNITS[n][0]
                keys = P * (tt + 1)
                per = 512 // keys
                act.wait_ge(nmax_ready, n + 1)
                if n >= 2:
                    act.wait_ge(probsT_done, groups_before[n - 1])
                for b in range(8 // per):
                    for i in range(per):
                        hh = head_of(b, i, per)
                        ins = A(probs[n % 2][:, hh, 0:keys], ps[b][:, i * keys:(i + 1) * keys], ACT.Exp,
                                bias=nmax[:, hh:hh + 1], scale=SCALE, accum_out=den[:, tt, hh:hh + 1])
                ins.then_inc(probs_ready, 1)
                if UNITS[n][4] is None:
                    A(esink[:, tt, :], sinkd[:, tt, :], ACT.Exp).then_inc(esink_ready, 1)

            def attend(n, another):
                for g in range(groups_before[n], groups_before[n + 1], 2):
                    kt = (g - groups_before[n]) // 2
                    act.wait_ge(probsT_done, g + 1)
                    if n:
                        act.wait_ge(pv_done, n)
                    A(probsT[:, kt, 0:4, :], ps[4][:, :].rearrange("p (h t) -> p h t", h=4),
                      ACT.Copy).then_inc(probsT_act, 1)
                if another:
                    exps(n + 1)

            def upper_part(n):
                slot = QUARTERS[n][0]
                if n < 2:
                    act.wait_ge(first_half_in, 16)
                else:
                    act.wait_ge(slot_full[place(slot)], 16 * fills(slot))
                if n >= 4:
                    act.wait_ge(parts_used, n - 3)
                A(upper(n), quarter(n, False), ACT.Copy).then_inc(upper_ready, 1)

            def upper_x(source, first, tiles=range(TT), x32=x32):
                for tt in tiles:
                    for b in range(2):
                        act.wait_ge(source, first + 2 * tt + b + 1)
                        part = (slice(None), slice(4 * b, 4 * b + 4), slice(tt * P, (tt + 1) * P))
                        A(xhi[part], x32[part], ACT.Copy).then_inc(xhi_ready, 1)

            def feed_forward():
                for n in range(FFN_Q + 4, IN1_Q + 3):
                    if QUARTERS[n - 4][1] == "gate":
                        _, _, j, i = QUARTERS[n - 4]
                        act.wait_ge(parts_used, n - 3)
                        if j:
                            act.wait_ge(hidden_ready, 4 * j + i - 3)
                        A(sg(i), ps[i][:, 0:T], ACT.Silu).then_inc(silu_gate, 1)
                    if n < IN1_Q:
                        upper_part(n)
                    if n >= FFN_Q + 5 and QUARTERS[n - 5][1] == "up":
                        _, _, j, i = QUARTERS[n - 5]
                        tile = 4 * j + i
                        act.wait_ge(hidden_ready, tile + 1)
                        A(hhi[:, tile % 8, :], h32[:, tile % 8, :], ACT.Copy).then_inc(hhi_ready, 1)

            def first_upper_parts(layer, n0):
                for tt in range(TT):
                    for n in range(n0 + 2 * tt, n0 + 2 * tt + 2):
                        upper_part(n)
                    upper_x(mixT_ready, 4 * layer, [tt])

            def upper_parts(n0, count):
                for n in range(n0, n0 + count):
                    upper_part(n)

            act.wait_ge(x_in[1], 16)
            upper_x(xT_ready, 0)
            upper_parts(IN0_Q, 4)
            sums_of_squares(0)
            act.wait_ge(small_in, SMALL)
            for m, c0 in enumerate((C_SWA, C_FULL)):
                A(mbf[:, m, :], con[:, c0:c0 + T], ACT.Copy).then_inc(masks_ready, 1)
            upper_parts(IN0_Q + 4, 4)
            act.wait_ge(rsqrt_ready, 1)
            copy0(0)
            act.wait_ge(angle_ready, 1)
            A(trig[:, :, :, :], trig[:, :, :, :], ACT.Sin).then_inc(trig_ready, 1)
            upper_parts(IN0_Q + 8, 4)
            copy0(1)
            upper_parts(IN0_Q + 12, 4)
            copy0(2)
            act.wait_ge(z_ready, 1)
            step(A(tmp[:, :, :], eb[:, :, :], ACT.Exp, scale=-1.0))
            settle()
            A(tmp[:, :, :], tmp[:, :, :], ACT.Ln, bias=1.0).then_inc(softplus_ready, 1)
            act.wait_ge(proj_out, 6)
            for tt in range(TT):
                A(pr[:, tt, GOUT:GOUT + 512], pr[:, tt, GOUT:GOUT + 512], ACT.Silu).then_inc(silu_ready, 1)
            upper_parts(IN0_Q + 16, 4)
            copy0(3)
            act.wait_ge(cum_done, 1)
            act.wait_ge(dl_ready, 1)
            cum = ps[6][:, :].rearrange("p (t c) -> p t c", t=TT)
            A(eb[:, :, :], cum, ACT.Exp, scale=1.0 / 16)
            A(enb[:, :, :], cum, ACT.Exp, scale=-1.0 / 16)
            A(dec, ps[4][:, 0:8], ACT.Exp, scale=1.0 / 16).then_inc(decay_ready, 1)
            A(ebl[:, :, :], tmp[:, :, :], ACT.Exp, scale=1.0 / 16).then_inc(ebl_ready, 1)
            act.wait_ge(proj_out, 8)
            head_squares(SQ, 10)
            copy0(4)
            for i, dst in enumerate(linT[0]):
                act.wait_ge(gla_T_done, i + 1)
                A(dst, ps[2 + i][:, :].rearrange("p (j t) -> p j t", j=2), ACT.Copy).then_inc(gla_T_ready, 1)
            act.wait_ge(head_rows_ready, 1)
            for d in range(2):
                ins = A(dup[:, :, 0:2, d, :], pr[:, :, SK:SK + 128].rearrange("p t (g c) -> p t g c", g=2), ACT.Copy)
            ins.then_inc(dup_ready, 1)
            copy_turned(0, [(2, 0), (3, 512), (4, 1024)])
            exps(0)
            for tt in range(TT):
                act.wait_ge(lin_out_done, tt + 1)
                A(linsq[0][:, tt, :], ps[6 + tt][:, :], ACT.Square).then_inc(lin_sq_ready, 1)
            attend(0, True)
            attend(1, False)
            act.wait_ge(gated_ready, 2)
            first_upper_parts(0, OUT0_Q)
            for n in range(OUT0_Q + 4, FFN_Q + 2):
                upper_part(n)
            act.wait_ge(h_ready, 4)
            sums_of_squares(1)
            for n in range(FFN_Q + 2, FFN_Q + 4):
                upper_part(n)
            upper_x(xT_ready, 4)
            feed_forward()

            upper_parts(IN1_Q, 2)
            upper_x(xT_ready, 8, x32=h32)
            upper_parts(IN1_Q + 2, 2)
            sums_of_squares(2)
            upper_parts(IN1_Q + 4, 4)
            act.wait_ge(rsqrt_ready, 5)
            copy1(0)
            upper_parts(IN1_Q + 8, 4)
            copy1(1)
            upper_parts(IN1_Q + 12, 4)
            copy1(2)
            act.wait_ge(proj_out, 16)
            head_squares(NQ, 12)
            A(gates[:, :, :], pr[:, :, NG_:NG_ + 24], ACT.Exp, scale=-1.0).then_inc(gates_ready, 1)
            upper_parts(IN1_Q + 16, 4)
            copy1(3)
            act.wait_ge(head_rows_ready, 2)
            for d in range(2):
                ins = A(dup[:, :, :, d, :], pr[:, :, KS_:KS_ + 256].rearrange("p t (g c) -> p t g c", g=4), ACT.Copy)
            ins.then_inc(dup_ready, 1)
            upper_parts(IN1_Q + 20, 4)
            copy1(4)
            copy_turned(3, [(4, 0), (5, 512)])
            copy_turned(5, [(4, 1024), (5, 1536)])
            act.wait_ge(hid_x, 1)
            A(hide[:, :, :], hide[:, :, :], ACT.Exp, scale=-2 * 0.7978845608028654).then_inc(hid_e, 1)
            copy1(7)
            act.wait_ge(ret_T_done, 2)
            for i, dst in enumerate(linT[1]):
                A(dst, ps[4 + i][:, :].rearrange("p (j t) -> p j t", j=2), ACT.Copy).then_inc(ret_T_ready, 1)
            act.wait_ge(proj_out, 22)
            for tt in range(TT):
                A(pr[:, tt, RG:RG + 512], pr[:, tt, RG:RG + 512], ACT.Silu).then_inc(silu_ready, 1)
            act.wait_ge(ckT_done, 1)
            A(kcT[:, :], ps[6][:, 0:64], ACT.Copy).then_inc(ckT_ready, 1)
            act.wait_ge(lin_scores_ready, 8)
            act.dma_start(econ, expert_consts).then_inc(expert_consts_in, 16)
            act.wait_ge(cs_ready, 1)
            A(csm[:, :, 0:120], csm[:, :, 0:120], ACT.Exp, scale=SCALE).then_inc(ce_ready, 1)
            for tt in range(TT):
                act.wait_ge(cpT_done, tt + 1)
                A(cpT[:, tt, :, :], ps[6 + tt][0:64, :].rearrange("p (j q) -> p j q", j=4),
                  ACT.Copy).then_inc(cpT_ready, 1)
            exps(2)
            for n in range(2, 6):
                attend(n, n < 5)
            act.wait_ge(gated_ready, 4)
            first_upper_parts(1, OUT1_Q)
            for n in range(OUT1_Q + 4, OUT1_Q + 8):
                upper_part(n)
            act.wait_ge(h_ready, 8)
            sums_of_squares(3)
            act.wait_ge(dtop_ready, 1)
            A(etop, dtop, ACT.Exp).then_inc(etop_ready, 1)

            def split_slot(i, r, first):
                n = MOE + r
                act.wait_ge(slot_full[place(n)], i * (16 * MOE_SLOTS // RING) + 16 * fills(n))
                for q in range(4):
                    if not (first and r == 0):
                        act.wait_ge(quarter_used, i * 4 * MOE_SLOTS + (4 * r + q - 3))
                    A(whi[:, q, :], ring[:, place(n), q * 1024:(q + 1) * 1024], ACT.Copy).then_inc(whi_ready, 1)

            def expert(i, output_before, gather_next, first):
                j0 = i * MOE_SLABS

                def hidden(j):
                    act.wait_ge(ehT_done, j0 + (j + 1))
                    A(ehhi[:, :, :], ps[7][:, 0:4 * CAP].rearrange("p (f t) -> p f t", f=4),
                      ACT.Copy).then_inc(ehhi_ready, 1)

                for r, (kind, j) in enumerate(ffn_order(MOE_SLABS)):
                    if not (first and r == 0):
                        split_slot(i, r, first)
                    if r == 0 and output_before:
                        output(i - 1)
                    if kind == "up":
                        if j:
                            hidden(j - 1)
                            act.wait_ge(ehrow_ready, j0 + j)
                        act.wait_ge(quarter_used, i * 4 * MOE_SLOTS + 4 * (gate_slot(j) + 1))
                        A(egate[:, :], ps[0][0:CAP, :], ACT.Silu).then_inc(egate_ready, 1)
                hidden(MOE_SLABS - 1)
                if gather_next:
                    next_tokens(i + 1)

            def next_tokens(i):
                act.wait_ge(xe32_ready, i + 1)
                A(xehi[:, :, :], xe32[:, :, :], ACT.Copy).then_inc(xehi_ready, 1)

            def output(i):
                act.wait_ge(quarter_used, (i + 1) * 4 * MOE_SLOTS)
                for half in range(2):
                    A(osb[:, half * 512:(half + 1) * 512], ps[2 + half][0:CAP, :], ACT.Copy).then_inc(o_ready, 1)

            act.wait_ge(router_done, 1)
            split_slot(0, 0, True)
            next_tokens(0)
            expert(0, False, True, True)
            with act.Fori(1, N_EXPERTS - 1) as i:
                expert(i, True, True, False)
            expert(N_EXPERTS - 1, True, False, False)
            output(N_EXPERTS - 1)
            act.wait_ge(list_ready, 1)
            with act.If(any_item(act) > 0):
                with act.Fori(0, MAX_MORE) as k:
                    used, _, _ = item_of(act, k)
                    with act.If(used > 0):
                        i = k + N_EXPERTS
                        next_tokens(i)
                        expert(i, False, False, False)
                        output(i)

        @block.vector
        def _(dve):
            V = nc.vector
            steps = [0]
            powers = [0]

            def step(ins):
                steps[0] += 1
                ins.then_inc(dve_steps, 1)

            def settle():
                dve.wait_ge(dve_steps, steps[0])

            def link(ins):
                step(ins)
                settle()

            def input_rms(k):
                dve.wait_ge(sumsq_ready, TT * (k + 1))
                rsqrt_mean(rstd[:, TT * k:TT * (k + 1)], ssq[:, TT * k:TT * (k + 1)], D)

            def scale_rows(k):
                for tt in range(TT):
                    c = TT * k + tt
                    V.tensor_scalar(xn[:, tt, :], h[:, tt, :], rstd[:, c:c + 1], None, ALU.mult).then_inc(xn_ready, 1)

            def copy_turned_input(k, dst=xT, parts=((0, 0), (0, 1), (1, 0), (1, 1))):
                for tt, b in parts:
                    dve.wait_ge(xnT_done, 4 * k + 2 * tt + b + 1)
                    g = col[:, V_LN + KC * k + 4 * b:V_LN + KC * k + 4 * b + 4]
                    V.tensor_tensor(dst[:, 4 * b:4 * b + 4, tt * P:(tt + 1) * P],
                                    ps[4 + 2 * tt + b][:, :].rearrange("p (c t) -> p c t", c=4),
                                    spread(g, 2, P), ALU.mult).then_inc(xT_ready, 1)

            def split_turned_input(k, x0, x32, xlo):
                copy_turned_input(k, x32, ((0, 0), (0, 1), (1, 0)))
                lower_x(x0, ((0, 0), (1, 0)), x32, xlo)
                copy_turned_input(k, x32, ((1, 1),))
                lower_x(x0, ((0, 1), (1, 1)), x32, xlo)

            def ask_rsqrt(dst, src, n):
                powers[0] += 1
                V.tensor_scalar(dst, src, 1.0 / n, EPS, ALU.mult, ALU.add).then_inc(mean_ready, 1)

            def rsqrt_mean(dst, src, n):
                ask_rsqrt(dst, src, n)
                dve.wait_ge(rsqrt_ready, powers[0])

            def rotate(x1, x2, cos, sin, t):
                step(V.tensor_tensor(t[0], x1, cos, ALU.mult))
                step(V.tensor_tensor(t[1], x2, sin, ALU.mult))
                step(V.tensor_tensor(t[2], x2, cos, ALU.mult))
                step(V.tensor_tensor(t[3], x1, sin, ALU.mult))
                settle()
                step(V.tensor_tensor(x1, t[0], t[1], ALU.subtract))
                return V.tensor_tensor(x2, t[2], t[3], ALU.add)

            def heads_norm(c0, heads, gains, n):
                dve.wait_ge(head_sq_ready, n + 1)
                v = headsq[:, 0:TT * heads * HD].rearrange("p (t h c) -> p (t h) c", t=TT, c=HD)
                ss = hss[:, 0:TT * heads]
                rs = hrs[:, 0:TT * heads]
                link(V.tensor_reduce(ss, v, AX_X, ALU.add))
                ask_rsqrt(rs, ss, HD)
                xh = pr[:, :, c0:c0 + heads * HD].rearrange("p t (h c) -> p t h c", h=heads)
                at = 0
                for g0, count in gains:
                    for tt in range(TT):
                        g = spread(row[:, g0:g0 + HD], 1, count)
                        step(V.tensor_tensor(xh[:, tt, at:at + count, :], xh[:, tt, at:at + count, :], g, ALU.mult))
                    at += count
                settle()
                sin = spread(trig[:, 0, 0:TT, 0:8], 2, heads)
                cos = spread(trig[:, 1, 0:TT, 0:8], 2, heads)
                w_ = TT * heads * 8
                t = [rtmp[:, i * w_:(i + 1) * w_].rearrange("p (t h c) -> p t h c", t=TT, h=heads) for i in range(4)]
                link(rotate(xh[:, :, :, 0:8], xh[:, :, :, 8:16], cos, sin, t))
                dve.wait_ge(rsqrt_ready, powers[0])
                V.tensor_tensor(xh, xh, spread(rs.rearrange("p (t h) -> p t h", t=TT), 3, HD),
                                ALU.mult).then_inc(head_rows_ready, 1)
                dve.wait_ge(head_rows_ready, n + 1)

            def maxima(n):
                tt, _, _, _, branch = UNITS[n]
                keys = P * (tt + 1)
                per = 512 // keys
                dve.wait_ge(scores_done, n + 1)
                for b in range(8 // per):
                    first = head_of(b, 0, per)
                    heads = amax.rearrange("p (i r) -> p r i", r=2)[:, first % 2, first // 2:first // 2 + per]
                    step(V.tensor_reduce(heads,
                                         ps[b][:, :].rearrange("p (h k) -> p h k", h=per), AX_X, ALU.max))
                settle()
                if branch is None:
                    sink = row[:, R_SINK:R_SINK + 8]
                    link(V.scalar_tensor_tensor(amax, amax, SCALE, sink, ALU.mult, ALU.max))
                    step(V.tensor_tensor(sinkd[:, tt, :], sink, amax, ALU.subtract))
                    V.tensor_scalar(nmax, amax, -1.0, None, ALU.mult).then_inc(nmax_ready, 1)
                else:
                    V.tensor_scalar(nmax, amax, -SCALE, None, ALU.mult).then_inc(nmax_ready, 1)

            def attend(n, another, meanwhile=None):
                tt, _, _, _, branch = UNITS[n]
                if another:
                    maxima(n + 1)
                for g in range(groups_before[n] + 1, groups_before[n + 1], 2):
                    kt = (g - groups_before[n]) // 2
                    dve.wait_ge(probsT_done, g + 1)
                    V.tensor_copy(probsT[:, kt, 4:8, :],
                                  ps[5][:, :].rearrange("p (h t) -> p h t", h=4)).then_inc(probsT_dve, 1)
                dd = den[:, tt, :]
                dve.wait_ge(probs_ready, n + 1)
                if branch is None:
                    dve.wait_ge(esink_ready, n + 1)
                    link(V.tensor_tensor(dd, dd, esink[:, tt, :], ALU.add))
                link(V.reciprocal(rden, dd))
                if meanwhile:
                    meanwhile()
                o = ps[6][:, :].rearrange("p (h c) -> p h c", h=8)
                dst = mix[:, tt, 512:1024].rearrange("p (h c) -> p h c", h=8)
                if branch is None:
                    dve.wait_ge(pv_done, n + 1)
                    V.tensor_tensor(dst, o, spread(rden, 2, HD), ALU.mult).then_inc(pv_used, 1)
                else:
                    gt = gates[:, tt, :].rearrange("p (h b) -> p h b", b=3)[:, :, branch]
                    link(V.tensor_tensor(wgt, rden, gt, ALU.mult))
                    dve.wait_ge(pv_done, n + 1)
                    t = branch_out
                    V.tensor_tensor(t, o, spread(wgt, 2, HD), ALU.mult).then_inc(pv_used, 1)
                    dve.wait_ge(pv_used, n + 1)
                    ins = V.tensor_tensor(dst, dst, t, ALU.add)
                    if branch == 2:
                        ins.then_inc(mix_ready, 1)
                    else:
                        step(ins)
                        settle()

            branch_out = pr[:, 0, 2048:2560].rearrange("p (h c) -> p h c", h=8)

            def lower_part(n):
                dve.wait_ge(upper_ready, n + 1)
                V.tensor_tensor(quarter(n, True), quarter(n, False), upper(n), ALU.subtract).then_inc(lower_ready, 1)

            def lower_x(x0, parts, x32=x32, xlo=xlo):
                for tt, b in parts:
                    dve.wait_ge(xhi_ready, x0 + 2 * tt + b + 1)
                    part = (slice(None), slice(4 * b, 4 * b + 4), slice(tt * P, (tt + 1) * P))
                    V.tensor_tensor(xlo[part], x32[part], xhi[part], ALU.subtract).then_inc(xlo_ready, 1)

            def lower_parts(n0, count):
                for n in range(n0, n0 + count):
                    lower_part(n)

            def copy_mixT(layer, tt):
                for b in range(2):
                    dve.wait_ge(mixT_done, 4 * layer + 2 * tt + b + 1)
                    V.tensor_copy(x32[:, 4 * b:4 * b + 4, tt * P:(tt + 1) * P],
                                  ps[4 * tt + b][:, :].rearrange("p (c t) -> p c t", c=4)).then_inc(mixT_ready, 1)

            def first_mixT(layer, n0, x0):
                copy_mixT(layer, 0)
                lower_part(n0)
                lower_x(x0, ((0, 0), (0, 1)))
                lower_part(n0 + 1)

            def output_projection(layer, n0, x0, follow):
                copy_mixT(layer, 1)
                lower_x(x0, ((1, 0), (1, 1)))
                for n in range(n0 + 2, n0 + 8):
                    lower_part(n)
                for u in range(4):
                    s, tt = u // 2, u % 2
                    if u == 2:
                        for n in range(n0 + 8, n0 + 8 + follow):
                            lower_part(n)
                    if u == 2:
                        dve.wait_ge(first_tile_done, 2 * layer + 1)
                    else:
                        dve.wait_ge(parts_used, n0 + 4 * s + 4)
                    hs = h[:, tt, s * 512:(s + 1) * 512]
                    V.tensor_tensor(hs, hs, ps[u][:, :], ALU.add).then_inc(h_ready, 1)

            def feed_forward():
                for n in range(FFN_Q + 4, IN1_Q + 4):
                    if n < IN1_Q:
                        lower_part(n)
                    if QUARTERS[n - 4][1] == "up":
                        _, _, j, i = QUARTERS[n - 4]
                        tile = 4 * j + i
                        dve.wait_ge(silu_gate, tile + 1)
                        dve.wait_ge(parts_used, n - 3)
                        V.tensor_tensor(h32[:, tile % 8, :], sg(i), ps[i][:, T:2 * T],
                                        ALU.mult).then_inc(hidden_ready, 1)
                    if n >= FFN_Q + 6 and QUARTERS[n - 6][1] == "up":
                        _, _, j, i = QUARTERS[n - 6]
                        tile = 4 * j + i
                        dve.wait_ge(hhi_ready, tile + 1)
                        V.tensor_tensor(hlo[:, tile % 8, :], h32[:, tile % 8, :], hhi[:, tile % 8, :],
                                        ALU.subtract).then_inc(hlo_ready, 1)
                lower_parts(IN1_Q, 2)
                for tt in range(TT):
                    if tt == 0:
                        dve.wait_ge(first_tile_done, 2)
                    else:
                        dve.wait_ge(parts_used, IN1_Q)
                    for half in range(2):
                        hs = h[:, tt, half * 512:(half + 1) * 512]
                        ins = V.tensor_tensor(hs, ps[4 + 2 * tt + half][:, :], hs, ALU.add)
                    ins.then_inc(y_added, 1)

            dve.wait_ge(ident_in, 32)
            split_turned_input(0, 0, x32, xlo)
            lower_parts(IN0_Q, 4)
            input_rms(0)
            dve.wait_ge(small_in, SMALL)
            link(V.tensor_copy(posf[:, :], posi[:, :]))
            ang = ws[:, 0:120].rearrange("p (j f) -> p j f", j=3)
            turns = ws[:, 120:360].rearrange("p (s f) -> p s f", s=2)
            fold = trig[:, :, :, :].rearrange("p s j f -> p s (j f)")
            for j in range(3):
                step(V.tensor_scalar(ang[:, j, :], con[:, C_INV:C_INV + 40], posf[:, j:j + 1], None, ALU.mult))
            settle()
            angf = ws[:, 0:120]
            for s in range(2):
                step(V.tensor_scalar(turns[:, s, :], angf, 1 / TWO_PI, 0.25 * s, ALU.mult, ALU.add))
            settle()
            link(V.tensor_scalar(turns, turns, ROUND, None, ALU.add))
            link(V.tensor_scalar(turns, turns, -ROUND, None, ALU.add))
            for s in range(2):
                step(V.scalar_tensor_tensor(fold[:, s, :], turns[:, s, :], -PI2_A, angf, ALU.mult, ALU.add))
            settle()
            link(V.scalar_tensor_tensor(fold, turns, -PI2_B, fold, ALU.mult, ALU.add))
            link(V.scalar_tensor_tensor(fold, turns, -PI2_C, fold, ALU.mult, ALU.add))
            link(V.tensor_scalar(fold[:, 1, :], fold[:, 1, :], TWO_PI / 4, None, ALU.add))
            V.tensor_scalar(fold, fold, 3.1415925, -3.1415925, ALU.min, ALU.max).then_inc(angle_ready, 1)
            lower_parts(IN0_Q + 4, 8)

            dve.wait_ge(gT_done, 1)
            V.tensor_copy(gT[:, :], ps[4][0:16, 0:T]).then_inc(gT_ready, 1)
            lower_parts(IN0_Q + 12, 4)
            dve.wait_ge(z_done, 1)
            z = ps[5][:, :].rearrange("p (t c) -> p t c", t=TT)
            link(V.tensor_tensor(la, z, spread(row[:, R_GB:R_GB + 256], 1, TT), ALU.add))
            V.scalar_tensor_tensor(eb, la, -1.0, la, ALU.mult, ALU.max).then_inc(z_ready, 1)
            dve.wait_ge(softplus_ready, 1)
            V.scalar_tensor_tensor(la, la, 0.0, tmp, ALU.min, ALU.subtract).then_inc(la_ready, 1)
            lower_parts(IN0_Q + 16, 4)
            dve.wait_ge(cum_done, 1)
            link(V.tensor_copy(ebl, ps[6][:, :].rearrange("p (t c) -> p t c", t=TT)))
            V.tensor_tensor(tmp, ps[7][:, :].rearrange("p (t c) -> p t c", t=TT), ebl,
                            ALU.subtract).then_inc(dl_ready, 1)
            dve.wait_ge(decay_ready, 1)
            step(V.scalar_tensor_tensor(qin, pr[:, :, GQ:GQ + 256], HD ** -0.5, eb, ALU.mult, ALU.mult))
            step(V.tensor_tensor(kin, pr[:, :, GK:GK + 256], enb, ALU.mult))
            dve.wait_ge(ebl_ready, 1)
            V.tensor_tensor(kst, pr[:, :, GK:GK + 256], ebl, ALU.mult).then_inc(gla_ops_ready, 1)
            dve.wait_ge(trig_ready, 1)
            heads_norm(SQ, 10, [(R_SQ, 8), (R_SK, 2)], 0)
            dve.wait_ge(kv_done, 1)
            dve.wait_ge(pool_steps, 1)
            for c in range(3):
                for hp in range(2):
                    for r in range(2):
                        q = slice(64 * r, 64 * r + 64)
                        kv = ps[5 + c][q, hp * 256 + r * P:hp * 256 + (r + 1) * P]
                        s = state[q, c, 2 * hp + r, :]
                        if c == 0:
                            ins = V.tensor_copy(s, kv)
                        else:
                            d = dec[q, 4 * hp + c:4 * hp + c + 1]
                            ins = V.scalar_tensor_tensor(s, state[q, c - 1, 2 * hp + r, :], d, kv,
                                                         ALU.mult, ALU.add)
                        if c < 2 or (hp, r) != (1, 1):
                            step(ins)
                        else:
                            ins.then_inc(state_ready, 1)
                settle()
            dve.wait_ge(lin_scores_done, 2)
            dve.wait_ge(pool_steps, 2)
            for r in range(2):
                V.copy_predicated(glasc[:, r, :, :, :].rearrange("p a b t -> p (a b) t"),
                                  spread(tri.bitcast(I32), 1, 4),
                                  ps[r][:, :].rearrange("p (h t) -> p h t", h=4)).then_inc(lin_scores_ready, 1)

            maxima(0)
            dve.wait_ge(lin_sq_ready, 2)
            link(V.tensor_reduce(hss[:, 0:8], ws[:, 3072:4096].rearrange("p (h c) -> p h c", c=P), AX_X, ALU.add))
            rsqrt_mean(hrs[:, 0:8], hss[:, 0:8], P)
            dve.wait_ge(head_T_done, 3)
            for tt in range(TT):
                V.tensor_tensor(mix[:, tt, 0:512].rearrange("p (h c) -> p h c", h=4),
                                ps[6 + tt][:, :].rearrange("p (h c) -> p h c", h=4),
                                spread(hrs[:, 4 * tt:4 * tt + 4], 2, P), ALU.mult).then_inc(lin_used, 1)
            attend(0, True)
            attend(1, False, lambda: first_mixT(0, OUT0_Q, 4))
            output_projection(0, OUT0_Q, 4, 2)
            dve.wait_ge(h_ready, 4)
            input_rms(1)
            scale_rows(1)
            split_turned_input(1, 8, x32, xlo)
            for n in range(FFN_Q + 2, FFN_Q + 4):
                lower_part(n)
            feed_forward()

            split_turned_input(2, 12, h32, xlo1)
            lower_parts(IN1_Q + 2, 2)
            input_rms(2)
            lower_parts(IN1_Q + 4, 14)
            heads_norm(NQ, 12, [(R_NQ, 8), (R_KS, 2), (R_KW, 2)], 1)
            lower_parts(IN1_Q + 18, 2)
            dve.wait_ge(gates_ready, 1)
            link(V.tensor_scalar(gates, gates, 1.0, None, ALU.add))
            link(V.reciprocal(gates, gates))
            dve.wait_ge(blk_zero, 1)
            for i, v0 in enumerate((V_PK, V_PV)):
                dve.wait_ge(kcT_done, i + 1)
                for r in range(2):
                    for g in range(2):
                        for half in range(2):
                            src = ps[6 + i][64 * g:64 * g + 64, 16 * half:16 * half + 240]\
                                .rearrange("p (n l r) -> p l n r", l=8, r=2)[:, :, :, r]
                            q = slice(64 * r, 64 * r + 64)
                            dst = blk[q, i, 8 * half:8 * half + 8, 32 * g:32 * g + NCMP]
                            pe_ = col[q, v0 + 8 * half:v0 + 8 * half + 8]
                            ins = V.tensor_tensor(dst, src, spread(pe_, 2, NCMP), ALU.add)
                            if (r, g, half) == (1, 1, 1):
                                ins.then_inc(blk_ready, 1)
                            else:
                                step(ins)
            lower_parts(IN1_Q + 20, 4)
            dve.wait_ge(proj_out, 18)
            dve.wait_ge(head_T_done, 7)
            qk = pr[:, :, RQ:RQ + 512].rearrange("p t (h c) -> p t h c", h=8)
            t = [xnf[:, i * 512:(i + 1) * 512].rearrange("p (t h c) -> p t h c", t=TT, h=8) for i in range(4)]
            rotate(qk[:, :, :, 0:32], qk[:, :, :, 32:64], spread(trig[:, 1, 0:TT, 8:40], 2, 8),
                   spread(trig[:, 0, 0:TT, 8:40], 2, 8), t).then_inc(ret_rows_ready, 1)
            dve.wait_ge(hid_done, 2)
            settle()
            for i, b0 in enumerate((V_B1K, V_B1V)):
                step(V.tensor_tensor(hidx[:, i, :].rearrange("p (a c) -> p a c", a=2),
                                     ps[6][:, i * 128:(i + 1) * 128].rearrange("p (a c) -> p a c", a=2),
                                     spread(col[:, b0:b0 + 2], 2, 64), ALU.add))
            settle()
            link(V.tensor_tensor(hid, hidx, hidx, ALU.mult))
            link(V.tensor_scalar(hid, hid, 0.044715, 1.0, ALU.mult, ALU.add))
            V.tensor_tensor(hide, hid, hidx, ALU.mult).then_inc(hid_x, 1)
            dve.wait_ge(hid_e, 1)
            link(V.tensor_scalar(hid, hide, 1.0, None, ALU.add))
            link(V.reciprocal(hid, hid))
            V.tensor_tensor(hid, hid, hidx, ALU.mult).then_inc(hid_ready, 1)
            dve.wait_ge(cmp_done, 1)
            link(V.tensor_tensor(cv[:, :, :], ps[7][0:64, 0:128].rearrange("p (i c) -> p i c", i=2),
                                 row[0:64, R_B2K:R_B2K + 128].rearrange("p (i c) -> p i c", i=2), ALU.add))
            ck = cv[:, 0, :]
            link(V.tensor_tensor(cktmp[:, 0:64], ck, ck, ALU.mult))
            link(V.tensor_reduce(ckss[:, 0:1], cktmp[:, 0:64], AX_X, ALU.add))
            rsqrt_mean(ckss[:, 1:2], ckss[:, 0:1], HD)
            link(V.scalar_tensor_tensor(ck, ck, ckss[:, 1:2], row[0:64, R_KC:R_KC + HD], ALU.mult, ALU.mult))
            t = [cktmp[:, i * 8:(i + 1) * 8] for i in range(4)]
            step(rotate(ck[:, 0:8], ck[:, 8:16], trig[0:64, 1, 2, 0:8], trig[0:64, 0, 2, 0:8], t))
            settle()
            V.tensor_copy(ckdup.rearrange("p (d c) -> p d c", d=2), spread(ck, 1, 2)).then_inc(ckv_ready, 1)
            dve.wait_ge(lin_scores_done, 2 + 3)
            for i, d0 in enumerate((C_RD, C_RD, C_RO)):
                for r in range(2):
                    bank = ps[2 * (i // 2) + r][:, (i % 2) * 256:(i % 2 + 1) * 256]
                    V.tensor_tensor(retsc[:, i, :, :].rearrange("p (j r) q -> p r j q", r=2)[:, r, :, :],
                                    bank.rearrange("p (j q) -> p j q", j=2),
                                    con[:, d0:d0 + 512].rearrange("p (j r q) -> p r j q", j=2, r=2)[:, r, :, :],
                                    ALU.mult).then_inc(lin_scores_ready, 1)
            dve.wait_ge(cs_done, 1)
            for tt in range(TT):
                s4 = csm[:, tt, 0:120].rearrange("p (x n) -> p x n", n=NCMP)
                for r in range(2):
                    src = ps[6 + r][:, tt * 64:(tt + 1) * 64].rearrange("p (x n) -> p x n", n=16)[:, :, 0:NCMP]
                    step(V.tensor_tensor(s4[:, 4 * r:4 * r + 4, :], src,
                                         spread(con[:, C_CADD + NCMP * tt:C_CADD + NCMP * (tt + 1)], 1, 4), ALU.add))
                settle()
                link(V.tensor_reduce(cmx[:, tt, :], s4, AX_X, ALU.max))
                ins = V.tensor_tensor(s4, s4, spread(cmx[:, tt, :], 2, NCMP), ALU.subtract)
                if tt == 0:
                    step(ins)
                else:
                    ins.then_inc(cs_ready, 1)
            link(V.memset(cpd, 0.0))
            dve.wait_ge(ce_ready, 1)
            for tt in range(TT):
                s4 = csm[:, tt, 0:120].rearrange("p (x n) -> p x n", n=NCMP)
                step(V.tensor_reduce(cden[:, tt, :], s4, AX_X, ALU.add))
                dst = cpd[:, tt, :].rearrange("p (x n) -> p x n", n=32)[:, :, 0:NCMP]
                ins = V.tensor_tensor(dst, s4, spread(con[:, C_CONE + NCMP * tt:C_CONE + NCMP * (tt + 1)], 1, 8), ALU.mult)
                if tt == 0:
                    step(ins)
                else:
                    ins.then_inc(cp_ready, 1)
            settle()
            maxima(2)
            link(V.reciprocal(cden, cden))
            for tt in range(TT):
                gt = gates[:, tt, :].rearrange("p (g j r b) -> p g j r b", g=2, j=2, r=2)[:, :, :, :, 0]
                cd = cden[:, tt, :].rearrange("p (r j g) -> p g j r", r=2, j=2)
                link(V.tensor_tensor(wgt.rearrange("p (g j r) -> p g j r", g=2, j=2), cd, gt, ALU.mult))
                dve.wait_ge(cpv_done, 2)
                for g in range(2):
                    ins = V.tensor_tensor(mix[:, tt, 512 + 256 * g:768 + 256 * g].rearrange("p (h c) -> p h c", h=4),
                                          ps[2 + g][:, 256 * tt:256 * (tt + 1)].rearrange("p (h c) -> p h c", h=4),
                                          spread(wgt[:, 4 * g:4 * g + 4], 2, HD), ALU.mult)
                if tt == 0:
                    link(ins)
                else:
                    ins.then_inc(mix_ready, 1)
                    dve.wait_ge(mix_ready, 1)
            for tt in range(TT):
                dve.wait_ge(lin_out_done, 2 + tt + 1)
                step(V.tensor_reduce(hss[:, 4 * tt:4 * tt + 4], ps[4 + tt][:, :].rearrange("p (h c) -> p h c", h=4),
                                     AX_X, ALU.add))
            settle()
            link(V.tensor_scalar(hmu, hss[:, 0:8], 1.0 / P, None, ALU.mult))
            for tt in range(TT):
                m = mix[:, tt, 0:512].rearrange("p (h c) -> p h c", h=4)
                V.tensor_tensor(m, ps[4 + tt][:, :].rearrange("p (h c) -> p h c", h=4),
                                spread(hmu[:, 4 * tt:4 * tt + 4], 2, P), ALU.subtract).then_inc(lin_used, 1)
            for tt in range(TT):
                dve.wait_ge(lin_used, 2 + tt + 1)
                step(V.tensor_tensor(linsq[1][:, tt, :], mix[:, tt, 0:512], mix[:, tt, 0:512], ALU.mult))
            settle()
            link(V.tensor_reduce(hss[:, 0:8], ws[:, 2560:3584].rearrange("p (h c) -> p h c", c=P), AX_X, ALU.add))
            rsqrt_mean(hrs[:, 0:8], hss[:, 0:8], P)
            for tt in range(TT):
                m = mix[:, tt, 0:512].rearrange("p (h c) -> p h c", h=4)
                V.tensor_tensor(m, m, spread(hrs[:, 4 * tt:4 * tt + 4], 2, P), ALU.mult).then_inc(lin_used, 1)
            for n in range(2, 6):
                attend(n, n < 5, (lambda: first_mixT(1, OUT1_Q, 16)) if n == 5 else None)
            output_projection(1, OUT1_Q, 16, 0)
            copy_turned_input(3)
            input_rms(3)
            scale_rows(3)
            dve.wait_ge(router_done, 1)
            for tt in range(TT):
                step(V.scalar_tensor_tensor(logit[:, tt, :], ps[0][:, tt * 8:(tt + 1) * 8], rstd[:, 6 + tt:7 + tt],
                                            row[:, R_RB:R_RB + 8], ALU.mult, ALU.add))
            settle()
            for tt in range(TT):
                step(V.max(top[:, tt, :], logit[:, tt, :]))
            settle()
            for tt in range(TT):
                step(V.max_index(topi[:, tt, :], top[:, tt, :], logit[:, tt, :]))
            settle()
            step(V.tensor_copy(topf, topi))
            V.tensor_tensor(dtop, top[:, :, 1], top[:, :, 0], ALU.subtract).then_inc(dtop_ready, 1)
            dve.wait_ge(etop_ready, 1)
            settle()
            link(V.tensor_scalar(dsum, etop, 1.0, None, ALU.add))
            link(V.reciprocal(wtop[:, 0, :], dsum))
            link(V.tensor_tensor(wtop[:, 1, :], etop, wtop[:, 0, :], ALU.mult))
            for tt in range(TT):
                for k, dst in ((0, chosen), (1, rank)):
                    step(V.tensor_scalar(dst[:, tt, :], con[:, C_IOTA:C_IOTA + 8], topf[:, tt, k:k + 1], None,
                                         ALU.is_equal))
            settle()
            for tt in range(TT):
                for k, (src, dst) in enumerate(((chosen, comb), (rank, comb2))):
                    step(V.tensor_scalar(dst[:, tt, :], src[:, tt, :], wtop[:, k, tt:tt + 1], None, ALU.mult))
            settle()
            V.tensor_tensor(chosen[:, :, :], chosen[:, :, :], rank[:, :, :], ALU.add).then_inc(chosen_ready, 1)
            step(V.tensor_tensor(comb, comb, comb2, ALU.add))
            dve.wait_ge(rank_done, 1)
            dve.wait_ge(chosen_ready, 1)
            settle()
            link(V.scalar_tensor_tensor(rank[:, :, :], ps[1][:, 0:16].rearrange("p (t e) -> p t e", t=TT), 1.0, chosen[:, :, :],
                                        ALU.add, ALU.mult))
            link(V.tensor_scalar(rank[:, :, :], rank[:, :, :], -1.0, None, ALU.add))

            def iota(first):
                return econ[:, D_IOTA:D_IOTA + CAP] if first is None else econ[:, bass.ds(first + D_IOTA, CAP)]

            def make_pick(i, e, first, waits=True):
                if waits:
                    dve.wait_ge(gather_done, i)
                for tt in range(TT):
                    ins = V.tensor_scalar(pick[:, tt, :], iota(first), rank[:, tt, bass.ds(e, 1)], None, ALU.is_equal)
                ins.then_inc(pick_ready, 1)

            def next_tokens(i):
                dve.wait_ge(gather_done, i + 1)
                for b in range(2):
                    g = col[:, V_LN + 3 * KC + 4 * b:V_LN + 3 * KC + 4 * b + 4]
                    ins = V.tensor_tensor(xe32[:, 4 * b:4 * b + 4, :],
                                          ps[4 + b][:, 0:4 * CAP].rearrange("p (c t) -> p c t", c=4),
                                          spread(g, 2, CAP), ALU.mult)
                ins.then_inc(xe32_ready, 1)
                dve.wait_ge(xehi_ready, i + 1)
                V.tensor_tensor(xelo[:, :, :], xe32[:, :, :], xehi[:, :, :].bitcast(F32),
                                ALU.subtract).then_inc(xelo_ready, 1)

            def add_output(i):
                for tt in range(TT):
                    dve.wait_ge(scatter_done, i * 2 + (tt + 1))
                    for half in range(2):
                        hs = h[:, tt, half * 512:(half + 1) * 512]
                        ins = V.tensor_tensor(hs, ps[6 - 2 * tt + half][:, :], hs, ALU.add)
                    ins.then_inc(y_used, 1)

            def lower_quarters(q0, r):
                for q in range(4):
                    dve.wait_ge(whi_ready, q0 + (4 * r + q + 1))
                    V.tensor_tensor(wlo[:, q, :], ring[:, place(MOE + r), q * 1024:(q + 1) * 1024],
                                    whi[:, q, :].bitcast(F32), ALU.subtract).then_inc(wlo_ready, 1)

            def expert(i, e, first, scatter_before, gather_next):
                j0, q0 = i * MOE_SLABS, i * 4 * MOE_SLOTS

                def hidden(j):
                    dve.wait_ge(ehhi_ready, j0 + (j + 1))
                    V.tensor_tensor(ehlo[:, :, :], ps[7][:, 0:4 * CAP].rearrange("p (f t) -> p f t", f=4),
                                    ehhi[:, :, :].bitcast(F32), ALU.subtract).then_inc(ehlo_ready, 1)

                for r, (kind, j) in enumerate(ffn_order(MOE_SLABS)):
                    if not (r == 0 and not scatter_before and gather_next):
                        lower_quarters(q0, r)
                    if kind == "up" and j:
                        hidden(j - 1)
                    if r and ffn_order(MOE_SLABS)[r - 1][0] == "up":
                        j = ffn_order(MOE_SLABS)[r - 1][1]
                        dve.wait_ge(egate_ready, j0 + (j + 1))
                        dve.wait_ge(quarter_used, q0 + 4 * (up_slot(j) + 1))
                        if j:
                            dve.wait_ge(ehT_done, j0 + j)
                        V.tensor_tensor(ehrow[:, :], egate[:, :], ps[1][0:CAP, :], ALU.mult).then_inc(ehrow_ready, 1)
                        if j == 0 and scatter_before:
                            add_output(i - 1)
                        if j == 1:
                            dve.wait_ge(spreadwT_done, i)
                            for tt in range(TT):
                                ins = V.tensor_scalar(spreadw[:, tt, :], iota(first), rank[:, tt, bass.ds(e, 1)],
                                                      comb[:, tt, bass.ds(e, 1)], ALU.is_equal, ALU.mult)
                            ins.then_inc(spreadw_ready, 1)
                        if j == 2 and gather_next:
                            make_pick(i + 1, e + 1, first)
                        if j == 3:
                            dve.wait_ge(spreadwT_done, i + 1)
                            dve.wait_ge(scatter_done, i * 2)
                            V.tensor_copy(spreadwT[:, :], ps[6][0:CAP, 0:T]).then_inc(spreadwT_ready, 1)
                hidden(MOE_SLABS - 1)
                if gather_next:
                    next_tokens(i + 1)

            make_pick(0, 0, None, False)
            lower_quarters(0, 0)
            next_tokens(0)
            expert(0, 0, None, False, True)
            for tt in range(TT):
                ins = V.tensor_copy(pairs[:, tt, :].rearrange("p (c e) -> p c e", e=8),
                                    spread(chosen[:, tt, :], 1, PARTS - 1))
            ins.then_inc(list_pairs_ready, 1)
            dve.wait_ge(count_done, 1)
            V.tensor_scalar(active[:, :], ps[7][0:NQ_MORE, 0:1], econ[0:NQ_MORE, D_THR:D_THR + 1], None,
                            ALU.is_gt).then_inc(active_ready, 1)
            dve.wait_ge(place_done, 1)
            dve.wait_ge(active_ready, 1)
            link(V.tensor_copy(cmx[0:NQ_MORE, 0, 0:1], ps[7][0:NQ_MORE, 1:2]))
            V.tensor_scalar(slots[:, :], econ[0:NQ_MORE, D_IK:D_IK + MAX_MORE], cmx[0:NQ_MORE, 0, 0:1], active[:, :],
                            ALU.is_equal, ALU.mult).then_inc(slots_ready, 1)
            dve.wait_ge(list_done, 1)
            V.tensor_copy(items[:, :], ps[7][0:1, 16:16 + 3 * MAX_MORE]).then_inc(list_ready, 1)
            with dve.Fori(1, N_EXPERTS - 1) as i:
                expert(i, i, None, True, True)
            expert(N_EXPERTS - 1, N_EXPERTS - 1, None, True, False)
            add_output(N_EXPERTS - 1)
            dve.wait_ge(list_ready, 1)
            with dve.If(any_item(dve) > 0):
                with dve.Fori(0, MAX_MORE) as k:
                    used, e, first = item_of(dve, k)
                    with dve.If(used > 0):
                        i = k + N_EXPERTS
                        make_pick(i, e, first)
                        next_tokens(i)
                        expert(i, e, first, False, False)
                        add_output(i)
            V.memset(slots[:, :], 0.0).then_inc(moe_done, 1)

        @block.gpsimd
        def _(pool):
            powers = [0]

            def rsqrts(v):
                powers[0] += 1
                pool.wait_ge(mean_ready, powers[0])
                p, c = v.shape
                nc.gpsimd.tensor_tensor(v, v, mhalf[0:p, 0:c], ALU.pow).then_inc(rsqrt_ready, 1)

            def gate_output(layer, gain, c0, used):
                for tt in range(TT):
                    n = TT * layer + tt + 1
                    m = mix[:, tt, 0:512].rearrange("p (h c) -> p h c", h=4)
                    pool.wait_ge(lin_used, used + tt + 1)
                    nc.gpsimd.tensor_tensor(m, m, gain, ALU.mult).then_inc(gain_done, 1)
                    pool.wait_ge(gain_done, n)
                    pool.wait_ge(silu_ready, n)
                    nc.gpsimd.tensor_tensor(mix[:, tt, 0:512], mix[:, tt, 0:512], pr[:, tt, c0:c0 + 512],
                                            ALU.mult).then_inc(gated_ready, 1)

            nc.gpsimd.memset(mhalf[:, :], -0.5).then_inc(mhalf_ready, 1)
            pool.wait_ge(mhalf_ready, 1)
            rsqrts(rstd[:, 0:2])
            pool.wait_ge(gla_ops_ready, 1)
            nc.gpsimd.memset(state, 0.0).then_inc(pool_steps, 1)
            rsqrts(hrs[:, 0:20])
            pool.wait_ge(gla_T_done, 2)
            nc.gpsimd.memset(glasc, 0.0).then_inc(pool_steps, 1)
            rsqrts(hrs[:, 0:8])
            gate_output(0, spread(row[:, R_GN:R_GN + P], 1, 4), GOUT, 0)
            rsqrts(rstd[:, 2:4])
            rsqrts(rstd[:, 4:6])
            pool.wait_ge(y_added, 2)
            nc.gpsimd.memset(blk, 0.0).then_inc(blk_zero, 1)
            rsqrts(hrs[:, 0:24])
            rsqrts(ckss[:, 1:2])
            rsqrts(hrs[:, 0:8])
            gate_output(1, row[:, R_RN:R_RN + 512].rearrange("p (h c) -> p h c", h=4), RG, 4)
            rsqrts(rstd[:, 6:8])


_WEIGHTS = ["w_in_e", "gla_gate_up", "w_out_e", "ffn_w_gate", "ffn_w_up", "ffn_w_down", "w_in_o",
            "cmp_w1_k", "cmp_w2_k", "cmp_w1_v", "cmp_w2_v", "w_out_o", "router_w",
            "exp_w_gate", "exp_w_up", "exp_w_down"]


def shape_constants():
    import numpy as np

    c = np.zeros((P, NC), np.float32)
    i = np.arange(P)
    c[:, C_ID:C_ID + P] = np.eye(P)
    chunk = i // 64
    same = chunk[:, None] == chunk[None, :]
    c[:, C_TRI:C_TRI + P] = same & (i[:, None] <= i[None, :])
    c[:, C_SAME:C_SAME + P] = same
    c[:, C_CH:C_CH + 2] = chunk[:, None] == np.arange(2)[None, :]
    for hh in range(4):
        lg = float(np.log(np.float32(1.0) - np.float32(2.0 ** (-5 - hh))))
        diff = i[None, :] - i[:, None]
        c[:, C_RD + hh * P:C_RD + (hh + 1) * P] = np.where(diff >= 0, np.exp(lg * np.maximum(diff, 0)), 0) * HD ** -0.5
        c[:, C_RO + hh * P:C_RO + (hh + 1) * P] = np.exp(lg * (diff + P)) * HD ** -0.5
    diag = np.where(i[None, :] <= i[:, None], 0.0, NEG)
    c[:, C_SWA:C_SWA + P] = np.where(i[None, :] > i[:, None], 0.0, NEG)
    c[:, C_SWA + P:C_SWA + T] = diag
    c[:, C_FULL + P:C_FULL + T] = diag
    end = np.arange(NCMP) * 16 + 31
    for tt in range(TT):
        ok = end[None, :] <= (tt * P + i)[:, None]
        c[:, C_CADD + NCMP * tt:C_CADD + NCMP * (tt + 1)] = np.where(ok, 0.0, NEG)
        c[:, C_CONE + NCMP * tt:C_CONE + NCMP * (tt + 1)] = ok
    f = np.arange(8, dtype=np.float32)
    c[:, C_INV:C_INV + 8] = np.float32(500000.0) ** (-f * np.float32(2.0) / np.float32(16))
    f = np.arange(32, dtype=np.float32)
    c[:, C_INV + 8:C_INV + 40] = np.float32(10000.0) ** (-f * np.float32(2.0) / np.float32(64))
    c[:, C_IOTA:C_IOTA + 8] = np.arange(8)
    return c


def expert_constants():
    import numpy as np

    c = np.zeros((P, ND), np.float32)
    i = np.arange(P)
    c[:, D_SU:D_SU + P] = i[:, None] < i[None, :]
    c[:, D_ONE:D_ONE + P] = 1
    c[:, D_IOTA:D_IOTA + CAP * PARTS] = np.arange(CAP * PARTS)
    q = np.arange(NQ_MORE)
    part = q // N_EXPERTS + 1
    c[:NQ_MORE, D_THR] = c[:NQ_MORE, D_QS] = part * CAP
    c[:NQ_MORE, D_QE] = q % N_EXPERTS
    c[:NQ_MORE, D_LOW:D_LOW + NQ_MORE] = q[:, None] < q[None, :]
    c[:, D_IK:D_IK + MAX_MORE] = np.arange(MAX_MORE)
    return c


def kernel(**inputs):
    import numpy as np
    import concourse.bacc as bacc
    from concourse.bass_utils import run_bass_kernel_spmd

    a = {k: np.ascontiguousarray(v) for k, v in inputs.items()}
    rowv = np.concatenate([a[k].reshape(-1) for k in (
        "gla_gate_bias", "gla_out_norm", "swa_q_norm", "swa_k_norm", "ret_out_norm", "nsa_q_norm", "nsa_kc_norm",
        "nsa_ks_norm", "nsa_kw_norm", "cmp_b2_k", "cmp_b2_v", "swa_sinks", "router_b")])[None, :]
    colv = np.concatenate([a[k].reshape(-1, P).T for k in (
        "ln_mix_e", "ln_ffn_e", "ln_mix_o", "ln_ffn_o", "cmp_b1_k", "cmp_b1_v", "cmp_pos_k", "cmp_pos_v")], axis=1)
    assert rowv.shape[1] == NR and colv.shape[1] == NV
    token = a["positions"].reshape(-1)
    pos = np.zeros((P, 3), token.dtype)
    pos[:, 0], pos[:, 1] = token[:P], token[P:]
    for g in range(2):
        pos[32 * g:32 * g + NCMP, 2] = token[np.arange(NCMP) * 16 + 31]

    nc = bacc.Bacc("TRN2", target_bir_lowering=False, num_devices=1)
    arrays = {}

    def feed(name, arr):
        arr = np.ascontiguousarray(arr)
        arrays[name] = arr
        return nc.dram_tensor(name, arr.shape, mybir.dt.from_np(arr.dtype), kind="ExternalInput").ap()

    x = feed("x_dram", a["x"].reshape(T, D))
    p = feed("pos_dram", pos)
    c = feed("consts_dram", shape_constants())
    ec = feed("expert_consts_dram", expert_constants())
    r = feed("rows_dram", rowv)
    v = feed("cols_dram", colv)
    w = {k: feed(k + "_dram", a[k]) for k in _WEIGHTS}
    w["out"] = nc.dram_tensor("out_dram", (T, D), F32, kind="ExternalOutput").ap()
    build(nc, x, p, c, ec, r, v, w)
    res = run_bass_kernel_spmd(nc, [arrays], core_ids=[0])
    return res.results[0]["out_dram"].reshape(1, T, D)
```
